# Optimizing a Trainium2 kernel written in Bass

```python
import jax, jax.numpy as jnp
from jax import lax
import numpy as np

D_MODEL = 1024
BATCH = 1
SEQ = 512
DEPTH = 1

N_META = 16
GLA_HEADS = 4
GLA_DK = 128
GLA_DV = 256
GLA_RANK = 16
GLA_TAU = 16.0
CHUNK = 64
QK_W = GLA_HEADS * GLA_DK
V_W = GLA_HEADS * GLA_DV
CONV_WIDTH = 31
CONV_CH = D_MODEL
N_GROUPS = 8
EXPERTS_PER_GROUP = 8
N_EXPERTS = N_GROUPS * EXPERTS_PER_GROUP
TOP_K = 2
D_EXPERT = 512
MOE_BLOCK = 128
EPS = 1e-6

IN_SPLITS = [QK_W, QK_W, V_W, V_W, GLA_RANK, 2 * CONV_CH, 2 * D_MODEL]
D_IN = int(sum(IN_SPLITS))
IN_OFFSETS = [int(o) for o in np.cumsum(IN_SPLITS)[:-1]]

kernel_name = "gla_conformer_conv_hier_moe_block"

def rmsnorm(x, g):
    xf = x.astype(jnp.float32)
    y = xf * lax.rsqrt(jnp.mean(xf * xf, axis=-1, keepdims=True) + EPS)
    return (y * g.astype(jnp.float32)).astype(x.dtype)

def layernorm(x, g, b):
    xf = x.astype(jnp.float32)
    mu = jnp.mean(xf, axis=-1, keepdims=True)
    xc = xf - mu
    y = xc * lax.rsqrt(jnp.mean(xc * xc, axis=-1, keepdims=True) + EPS)
    return (y * g.astype(jnp.float32) + b.astype(jnp.float32)).astype(x.dtype)

def gla_chunked(q, k, v, log_a):
    B, H, L, DK = q.shape
    DV = v.shape[-1]
    nc = L // CHUNK

    def to_chunks(t):
        return jnp.moveaxis(t.reshape(B, H, nc, CHUNK, t.shape[-1]), 2, 0)

    qc, kc, vc, ac = to_chunks(q), to_chunks(k), to_chunks(v), to_chunks(log_a)
    causal = jnp.tril(jnp.ones((CHUNK, CHUNK), dtype=bool))

    def step(S, inp):
        qi, ki, vi, ai = inp
        b = jnp.cumsum(ai, axis=2)
        diff = b[:, :, :, None, :] - b[:, :, None, :, :]
        decay = jnp.exp(jnp.where(causal[:, :, None], diff, -jnp.inf))
        scores = jnp.einsum('bhtd,bhsd,bhtsd->bhts', qi, ki, decay)
        o = (jnp.einsum('bhts,bhsv->bhtv', scores, vi)
             + jnp.einsum('bhtd,bhdv->bhtv', qi * jnp.exp(b), S))
        b_last = b[:, :, -1:, :]
        k_dec = ki * jnp.exp(b_last - b)
        S = jnp.exp(b_last[:, :, 0, :])[..., None] * S + jnp.einsum('bhsd,bhsv->bhdv', k_dec, vi)
        return S, o

    S0 = jnp.zeros((B, H, DK, DV), jnp.float32)
    _, o = lax.scan(step, S0, (qc, kc, vc, ac))
    return jnp.moveaxis(o, 0, 2).reshape(B, H, L, DV)

def hier_moe(xt, w_rg, b_rg, w_re, b_re, w_gate, w_up, w_down):
    T, D = xt.shape
    xf = xt.astype(jnp.float32)
    g_prob = jax.nn.softmax(xf @ w_rg.astype(jnp.float32) + b_rg.astype(jnp.float32), axis=-1)
    g_w, g_idx = lax.top_k(g_prob, 1)
    e_logits = (xf @ w_re.astype(jnp.float32) + b_re.astype(jnp.float32)).reshape(T, N_GROUPS, EXPERTS_PER_GROUP)
    e_logits = jnp.take_along_axis(e_logits, g_idx[:, :, None], axis=1)[:, 0]
    e_prob = jax.nn.softmax(e_logits, axis=-1)
    top_p, top_i = lax.top_k(e_prob, TOP_K)
    top_p = top_p / jnp.sum(top_p, axis=-1, keepdims=True)
    weights = g_w * top_p
    expert_id = g_idx * EXPERTS_PER_GROUP + top_i

    S = T * TOP_K
    slot_e = expert_id.reshape(S).astype(jnp.int32)
    slot_tok = jnp.repeat(jnp.arange(T, dtype=jnp.int32), TOP_K)
    counts = jax.ops.segment_sum(jnp.ones((S,), jnp.int32), slot_e, num_segments=N_EXPERTS)
    padded = (counts + MOE_BLOCK - 1) // MOE_BLOCK * MOE_BLOCK
    pad_end = jnp.cumsum(padded)
    pad_start = pad_end - padded
    start = jnp.cumsum(counts) - counts
    order = jnp.argsort(slot_e)
    e_sorted = slot_e[order]
    pos = pad_start[e_sorted] + jnp.arange(S, dtype=jnp.int32) - start[e_sorted]
    n_blocks = (S + N_EXPERTS * (MOE_BLOCK - 1) + MOE_BLOCK - 1) // MOE_BLOCK
    P = n_blocks * MOE_BLOCK
    buf_tok = jnp.full((P,), T, dtype=jnp.int32).at[pos].set(slot_tok[order])
    x_pad = jnp.concatenate([xt, jnp.zeros((1, D), xt.dtype)], axis=0)
    xb = x_pad[buf_tok].reshape(n_blocks, MOE_BLOCK, D)
    block_e = jnp.minimum(
        jnp.searchsorted(pad_end, jnp.arange(n_blocks, dtype=jnp.int32) * MOE_BLOCK, side='right'),
        N_EXPERTS - 1)

    def expert_block(args):
        xblk, e = args
        a = xblk @ w_gate[e]
        u = xblk @ w_up[e]
        return (jax.nn.silu(a) * u) @ w_down[e]

    yb = lax.map(expert_block, (xb, block_e)).reshape(P, D)
    y_slot = jnp.zeros((S, D), yb.dtype).at[order].set(yb[pos]).reshape(T, TOP_K, D)
    return jnp.einsum('tk,tkd->td', weights.astype(y_slot.dtype), y_slot)

def setup_inputs(seed: int = 0) -> dict:
    key = jax.random.key(seed)
    ks = jax.random.split(key, 24)
    f32 = jnp.float32
    nrm = lambda k, shape, s: jax.random.normal(k, shape, f32) * s
    Dp = DEPTH
    return {
        "x": nrm(ks[0], (BATCH, SEQ, D_MODEL), 1.0),
        "meta": nrm(ks[1], (N_META, D_MODEL), 1.0),
        "norm1_g": 1.0 + nrm(ks[2], (Dp, D_MODEL), 0.02),
        "w_in": nrm(ks[3], (Dp, D_MODEL, D_IN), D_MODEL ** -0.5),
        "w_decay_up": nrm(ks[4], (Dp, GLA_RANK, QK_W), GLA_RANK ** -0.5),
        "b_decay": nrm(ks[5], (Dp, QK_W), 0.1),
        "gla_norm_g": 1.0 + nrm(ks[6], (Dp, V_W), 0.02),
        "conv_w": nrm(ks[7], (Dp, CONV_WIDTH, CONV_CH), CONV_WIDTH ** -0.5),
        "conv_b": nrm(ks[8], (Dp, CONV_CH), 0.02),
        "conv_ln_g": 1.0 + nrm(ks[9], (Dp, CONV_CH), 0.02),
        "conv_ln_b": nrm(ks[10], (Dp, CONV_CH), 0.02),
        "w_pw2": nrm(ks[11], (Dp, CONV_CH, D_MODEL), CONV_CH ** -0.5),
        "b_gate": nrm(ks[12], (Dp, 2 * D_MODEL), 0.02),
        "w_out": nrm(ks[13], (Dp, D_MODEL, D_MODEL), D_MODEL ** -0.5),
        "norm2_g": 1.0 + nrm(ks[14], (Dp, D_MODEL), 0.02),
        "w_router_group": nrm(ks[15], (Dp, D_MODEL, N_GROUPS), D_MODEL ** -0.5),
        "b_router_group": nrm(ks[16], (Dp, N_GROUPS), 0.01),
        "w_router_expert": nrm(ks[17], (Dp, D_MODEL, N_EXPERTS), D_MODEL ** -0.5),
        "b_router_expert": nrm(ks[18], (Dp, N_EXPERTS), 0.01),
        "w_exp_gate": nrm(ks[19], (Dp, N_EXPERTS, D_MODEL, D_EXPERT), D_MODEL ** -0.5),
        "w_exp_up": nrm(ks[20], (Dp, N_EXPERTS, D_MODEL, D_EXPERT), D_MODEL ** -0.5),
        "w_exp_down": nrm(ks[21], (Dp, N_EXPERTS, D_EXPERT, D_MODEL), D_EXPERT ** -0.5),
        "final_norm_g": 1.0 + nrm(ks[22], (D_MODEL,), 0.02),
    }

def reference(x, meta, norm1_g, w_in, w_decay_up, b_decay, gla_norm_g, conv_w, conv_b,
              conv_ln_g, conv_ln_b, w_pw2, b_gate, w_out, norm2_g, w_router_group,
              b_router_group, w_router_expert, b_router_expert, w_exp_gate, w_exp_up,
              w_exp_down, final_norm_g):
    B = x.shape[0]
    h = jnp.concatenate([jnp.broadcast_to(meta[None].astype(x.dtype), (B, N_META, D_MODEL)), x], axis=1)
    L = h.shape[1]
    pad = (-N_META) % CHUNK

    for i in range(DEPTH):
        hn = rmsnorm(h, norm1_g[i])
        proj = hn @ w_in[i]
        q, k, v, og, dlow, glu, gates = jnp.split(proj, IN_OFFSETS, axis=-1)

        log_a = jax.nn.log_sigmoid((dlow @ w_decay_up[i] + b_decay[i]).astype(jnp.float32)) / GLA_TAU

        def heads(t, d):
            t = t.astype(jnp.float32).reshape(B, L, GLA_HEADS, d).transpose(0, 2, 1, 3)
            return jnp.pad(t, ((0, 0), (0, 0), (pad, 0), (0, 0)))

        o = gla_chunked(heads(q, GLA_DK) * (GLA_DK ** -0.5), heads(k, GLA_DK),
                        heads(v, GLA_DV), heads(log_a, GLA_DK))[:, :, pad:, :]
        o = o * lax.rsqrt(jnp.mean(o * o, axis=-1, keepdims=True) + EPS)
        o = o.transpose(0, 2, 1, 3).reshape(B, L, V_W) * gla_norm_g[i].astype(jnp.float32)
        branch_a = o.astype(h.dtype) * jax.nn.silu(og)

        u_val, u_gate = jnp.split(glu, 2, axis=-1)
        u = u_val * jax.nn.sigmoid(u_gate)
        u = lax.conv_general_dilated(
            u, conv_w[i].reshape(CONV_WIDTH, 1, CONV_CH).astype(u.dtype), window_strides=(1,),
            padding=[(CONV_WIDTH - 1, 0)], dimension_numbers=('NWC', 'WIO', 'NWC'),
            feature_group_count=CONV_CH) + conv_b[i]
        u = jax.nn.silu(layernorm(u, conv_ln_g[i], conv_ln_b[i]))
        branch_b = u @ w_pw2[i]

        g_a, g_b = jnp.split(jax.nn.sigmoid(gates + b_gate[i]), 2, axis=-1)
        h = h + (g_a * branch_a + g_b * branch_b) @ w_out[i]

        hn2 = rmsnorm(h, norm2_g[i]).reshape(B * L, D_MODEL)
        y = hier_moe(hn2, w_router_group[i], b_router_group[i], w_router_expert[i],
                     b_router_expert[i], w_exp_gate[i], w_exp_up[i], w_exp_down[i])
        h = h + y.reshape(B, L, D_MODEL)

    return rmsnorm(h, final_norm_g)[:, N_META:, :]


_drawn_inputs = setup_inputs


def setup_inputs(seed=0):
    import zlib

    import numpy as np

    out = dict(_drawn_inputs(seed))
    spreads = {}
    factors = {'gla_norm_g': 3.537,
     'conv_b': 2.725,
     'conv_ln_g': 3.01,
     'conv_ln_b': 3.46,
     'b_gate': 4.933,
     'norm2_g': 2.843,
     'b_router_group': 3.911,
     'b_router_expert': 3.723,
     'final_norm_g': 2.827}
    for name, (base, spread) in spreads.items():
        noise = np.random.default_rng([zlib.crc32(name.encode()), seed]).standard_normal(out[name].shape)
        drawn = base * np.exp(spread * noise) if base else spread * noise
        out[name] = __import__('jax').numpy.asarray(drawn.astype(out[name].dtype))
    for name, factor in factors.items():
        out[name] = (out[name] * factor).astype(out[name].dtype)
    return out
```

```python
import numpy as np
import concourse.bass as bass
from concourse import mybir
from contextlib import ExitStack

FP = mybir.dt.float32
I32 = mybir.dt.int32
U8 = mybir.dt.uint8

P = 128
D = 1024
KT = D // P
T = 512
META = 16
L = T + META
HALF = L // 2
NT = T // P
H, DK, DV = 4, 128, 256
TAPS = 31
EPS = 1e-6
TAU = 16.0
NG, EPG = 8, 8
NE = NG * EPG
DE = 512
CAP = 64
NX = T * 2 // CAP - 1
NBLK = NE + NX + 1
LEVELS = [64, 32, 16, 8, 4, 2, 1]

Q0, K0, V0, OG0, DL0, GV0, GG0, GA0, GB0 = 0, 512, 1024, 2048, 3072, 3088, 4112, 5136, 6160

R_N1, R_GLA, R_CB, R_LG, R_LB, R_BG, R_BD, R_END = 0, 8, 16, 24, 32, 40, 56, 60


def program(nc, x, meta, norm1_g, w_in, w_decay_up, b_decay, gla_norm_g, conv_w, conv_b, conv_ln_g,
            conv_ln_b, w_pw2, b_gate, w_out, norm2_g, w_rg, b_rg, w_re, b_re, w_eg, w_eu, w_ed,
            final_g, out):
    ALU = mybir.AluOpType
    ACT = mybir.ActivationFunctionType
    AX = mybir.AxisListType
    ctx = ExitStack()
    with ctx:
        sems = {}

        def sem(name):
            if name not in sems:
                sems[name] = ctx.enter_context(nc.semaphore(name))
            return sems[name]

        cst_i = ctx.enter_context(nc.sbuf_tensor("cst_i", [P, 2, P], I32))
        masks = ctx.enter_context(nc.sbuf_tensor("masks", [P, 8, P], U8))
        idx_pair = ctx.enter_context(nc.sbuf_tensor("idx_pair", [P, NBLK // 2], I32))
        idx_over = ctx.enter_context(nc.sbuf_tensor("idx_over", [CAP, 16], I32))
        idx_now = ctx.enter_context(nc.sbuf_tensor("idx_now", [P, 1], I32))
        pos_i = ctx.enter_context(nc.sbuf_tensor("pos_i", [P, 2, NT], I32))
        over_e = ctx.enter_context(nc.sbuf_tensor("over_e", [P, 17], I32))
        ARENA = 52000
        arena = ctx.enter_context(nc.sbuf_tensor("arena", [P, ARENA], FP))
        PS = ctx.enter_context(nc.psum_tensor("PS", [P, 8, 512], FP))
        y_d = nc.dram_tensor("y_rows", (NBLK * CAP, D), FP).ap()
        hn2_d = nc.dram_tensor("hn2_rows", (T, D), FP).ap()

        top = [0]

        def take(n):
            at = top[0]
            top[0] += n
            assert top[0] <= ARENA, top
            return at

        def view(at, n, pattern=None, parts=P, **kw):
            v = arena[0:parts, at:at + n]
            return v.rearrange(pattern, **kw) if pattern else v

        RING = take(3 * 4096)
        HNT = take(KT * L)
        UB = take(8 * 542)
        CV = take(8 * T)
        QF = take(H * T)
        KF = take(H * L)
        BF = take(H * L)
        VB = take(NT * D)
        VM = take(D)
        GTB = take(8 * T)
        EB = take(6 * 512)
        SC = take(2 * 512)
        SB = take(D)
        QE = take(2 * 512)
        KD = take(512)
        OT = take(D)
        OSQ = take(D)
        RST = take(512)
        TH = take(2 * 512)
        PRM = take(320)
        IDN = take(P)
        ONE = take(P)
        MEAN = take(P)
        LTM = take(P)
        SMALL = take(64)
        NHALF = take(1)
        ELAST = take(4 * 4)
        WDL = take(KT * 16)
        TOKID = take(4)
        IOTA = take(NBLK)

        ring = [view(RING + 4096 * s, 4096, "p (k c) -> p k c", k=KT) for s in range(3)]
        hnT = view(HNT, KT * L, "p (k t) -> p k t", k=KT)
        U = view(UB, 8 * 542, "p (k t) -> p k t", k=8)
        cv = view(CV, 8 * T, "p (k t) -> p k t", k=8)
        Qf = view(QF, H * T, "p (h t) -> p h t", h=H)
        Kf = view(KF, H * L, "p (h t) -> p h t", h=H)
        Bf = view(BF, H * L, "p (h t) -> p h t", h=H)
        V = view(VB, NT * D, "p (c v) -> p c v", c=NT)
        Vm = view(VM, D, parts=META)
        GT = view(GTB, 8 * T, "p (k t) -> p k t", k=8)
        E = [view(EB + 512 * i, 512, "p (h t) -> p h t", h=H) for i in range(6)]
        scT = [view(SC + 512 * i, 512, "p (h t) -> p h t", h=H) for i in range(2)]
        S = view(SB, D, "p (h v) -> p h v", h=H)
        qe = [view(QE + 512 * i, 512, "p (h t) -> p h t", h=H) for i in range(2)]
        kd = view(KD, 512, "p (h t) -> p h t", h=H)
        o_t = view(OT, D, "p (b t) -> p b t", b=8)
        o_sq = view(OSQ, D, "p (b t) -> p b t", b=8)
        rst = view(RST, 512)
        th = [view(TH + 512 * i, 512) for i in range(2)]
        prm = view(PRM, 320)
        ident = view(IDN, P)
        ones = view(ONE, P)
        mean_w = view(MEAN, P)
        before = view(LTM, P)
        ss = view(SMALL, 8)
        rs = view(SMALL + 8, 8)
        nhalf = view(NHALF, 1)
        elast = [view(ELAST + 4 * i, 4, "p (h o) -> p h o", o=1) for i in range(4)]
        wdl = view(WDL, KT * 16, "p (k c) -> p k c", k=KT)
        tokid = view(TOKID, 4)
        iota = view(IOTA, NBLK)

        x0 = view(VB, NT * D, "p (i d) -> p i d", i=NT)
        xs = [view(GTB + D * i, D) for i in range(2)]
        xm = view(GTB + 2 * D, D, parts=META)
        prow = view(GTB + 3 * D, 3 * P, "p (a c) -> p a c", a=3)
        junk = view(KF, D)
        glu_t = [view(EB + 528 * i, 528) for i in range(4)]
        wup = view(OT, 512, parts=16)
        dlow = view(OSQ, L, parts=16)

        def cw(t, c):
            return prm[:, 8 * t + c:8 * t + c + 1]

        PB = TAPS * 8

        def par(row, c):
            return prm[:, PB + row + c:PB + row + c + 1]

        xr = view(QF, NT * D, "p (i d) -> p i d", i=NT)
        hn2 = view(VB, NT * D, "p (i d) -> p i d", i=NT)
        hn2T = [view(BF + D * i, D, "p (k t) -> p k t", k=KT) for i in range(2)]
        g2b = view(EB, D)
        wr = view(EB + D, KT * 72, "p (k c) -> p k c", k=KT)
        brb = view(EB + D + 576, 72)
        junk2 = view(OT, D)
        fgb = view(SB, D)
        lg = view(EB + D + 648, NT * 72, "p (i c) -> p i c", i=NT)
        rt = [GTB]

        def arr(n, pattern=None, **kw):
            at = rt[0]
            rt[0] += n
            assert rt[0] <= GTB + 8 * T
            return view(at, n, pattern, **kw)

        oh = arr(32, "p (i g) -> p i g", i=NT)
        tb = arr(32, "p (i g) -> p i g", i=NT)
        eg = arr(32, "p (i g) -> p i g", i=NT)
        prod = arr(256, "p (i g e) -> p i g e", i=NT, g=NG)
        sel = arr(32, "p (i g) -> p i g", i=NT)
        sel2 = arr(32, "p (i g) -> p i g", i=NT)
        o12 = [arr(32, "p (i g) -> p i g", i=NT) for _ in range(2)]
        m4 = [arr(4) for _ in range(8)]
        gid = arr(4)
        wgt = [arr(4) for _ in range(2)]
        e_id = arr(8, "p (k i) -> p k i", k=2)
        rank = arr(8, "p (k i) -> p k i", k=2)
        rnd = arr(8, "p (k i) -> p k i", k=2)
        row = arr(8, "p (k i) -> p k i", k=2)
        stt_ = arr(8, "p (k i) -> p k i", k=2)
        isj = arr(8, "p (k i) -> p k i", k=2)
        blk = arr(8, "p (k i) -> p k i", k=2)
        A = [arr(256, "p (i e) -> p i e", i=NT) for _ in range(2)]
        Asum = arr(256, "p (i e) -> p i e", i=NT)
        Ccnt = arr(320, "p (i e) -> p i e", i=NT + 1)
        nx = arr(64)
        end = arr(64)
        start = arr(64)
        OR = [arr(256, "p (i r) -> p i r", i=NT) for _ in range(2)]
        AB = [arr(4 * NBLK, "p (i b) -> p i b", i=NT) for _ in range(2)]
        desc8 = arr(8)
        becmp = view(HNT, 16 * 64, "p (b e) -> p b e", b=16)
        be_f = arr(16)
        ones64 = arr(64)

        WB = [HNT, RING]
        wgu = [view(b, 8192, "p (k a f) -> p k a f", k=KT, a=2) for b in WB]
        wdn = [view(b + 8192, 4096, "p (j d) -> p j d", j=4) for b in WB]
        xg = view(VB, D)
        xT = view(VB + D, D, "p (k t) -> p k t", k=KT)
        gth = [view(VB + 2048 + 256 * i, 256) for i in range(2)]
        hS = [view(VB + 2560 + 256 * i, 256) for i in range(2)]
        hT = [view(VB + 3072 + 256 * i, 256, "p (b g s) -> p b g s", b=2, g=2) for i in range(2)]
        ysb = [view(VB + 3584 + 512 * i, 512) for i in range(2)]
        yt = [view(HNT + D * i, D) for i in range(8)]
        fin = [view(RING + D * i, D) for i in range(NT)]

        win_c = w_in.rearrange("(k p) c -> p k c", p=P)
        chunks = []
        for j in range(4):
            chunks.append([(win_c[:, :, GV0 + 256 * j:GV0 + 256 * j + 256], 0, 256),
                           (win_c[:, :, GG0 + 256 * j:GG0 + 256 * j + 256], 256, 512)])
        for c0 in (K0, Q0, V0, V0 + 512, GA0, GA0 + 512, OG0, OG0 + 512, GB0, GB0 + 512):
            chunks.append([(win_c[:, :, c0:c0 + 512], 0, 512)])
        for w in (w_pw2, w_out):
            wv = w.rearrange("(k p) c -> p k c", p=P)
            for j in range(2):
                chunks.append([(wv[:, :, 512 * j:512 * j + 512], 0, 512)])
        C_K, C_Q, C_V, C_GATES, C_PW, C_OUT = 4, 5, 6, 8, 14, 16
        loaded = [0, 0, 0]
        chunk_at = []
        for n, parts in enumerate(chunks):
            loaded[n % 3] += 16 * len(parts)
            chunk_at.append(loaded[n % 3])

        chunk_end = [("pair_done", 4 * n + 4) for n in range(5)] + [("single_done", n) for n in (4, 9, 14)]
        chunk_end += [("single_done", 14 + 4 * n + 4) for n in range(10)]

        def used(eng, n):
            eng.wait_ge(sem(chunk_end[n][0]), chunk_end[n][1])

        tasks = [("kdm", 0), ("Sm", 0)]
        for c in range(NT):
            body = [("lv", c, i) for i in range(7)] + [("diag", c)]
            if c:
                body.insert(2, ("ss", c - 1))
            if c < NT - 1:
                body.append(("kd", c))
            body.append(("o", c))
            if c < NT - 1:
                body.append(("S", c))
            tasks += body
        tasks.append(("ss", NT - 1))
        e_tasks = [t for t in tasks if t[0] in ("kdm", "lv", "kd")]
        s_tasks = [t for t in tasks if t[0] in ("kdm", "lv", "diag", "kd", "ss")]
        a_tasks = [t for t in tasks if t[0] in ("Sm", "o", "S")]
        NSLOT = 24
        slots = [[] for _ in range(NSLOT)]
        left = list(tasks)
        for b in range(3, NSLOT):
            n = 2 if b < 9 else -(-len(left) // (NSLOT - b))
            for _ in range(min(n, len(left))):
                slots[b].append(left.pop(0))
        assert not left
        GA_BLOCKS, OG_BLOCKS = range(0, 8), range(8, 16)

        freed = []
        counts = {"sgl_act": 0, "sgl_dve": 0}

        def use(by):
            counts[by] += 1
            freed.append((by, counts[by]))
        for _ in range(4 + 10 + 8):
            use("sgl_act")
        for _ in range(8):
            use("sgl_dve")
        for _ in range(8):
            use("sgl_act")
        for _ in range(8 + 8):
            use("sgl_dve")

        def linker(eng, name):
            count = [0]
            s = sem(name)

            def link(ins):
                count[0] += 1
                ins.then_inc(s, 1)
                eng.wait_ge(s, count[0])
            return link

        block = ctx.enter_context(nc.Block())

        @block.sync
        def _(sp):
            for i in range(NT):
                sp.dma_start(x0[:, i, :], x[P * i:P * i + P, :]).then_inc(sem(f"x_loaded{i}"), 16)
            sp.dma_start(xm, meta).then_inc(sem("meta_loaded"), 16)

            def chunk(n):
                for src, a, b in chunks[n]:
                    sp.dma_start(ring[n % 3][:, :, a:b], src).then_inc(sem(f"chunk_loaded{n % 3}"), 16)
            chunk(0)
            chunk(1)
            chunk(2)
            for n in range(3, len(chunks)):
                used(sp, n - 3)
                chunk(n)
                if n == C_PW + 1:
                    sp.wait_ge(sem("attention_done"), 1)
                    sp.wait_ge(sem("e_mul"), len(e_tasks))
                    sp.dma_start(xr, x.rearrange("(i p) d -> p i d", p=P)).then_inc(sem("xr_loaded"), 16)
                    sp.dma_start(g2b, norm2_g.partition_broadcast(P)).then_inc(sem("g2_loaded"), 16)
                    sp.dma_start(fgb, final_g.partition_broadcast(P)).then_inc(sem("fg_loaded"), 16)
                    sp.dma_start(wr[:, :, 0:8], w_rg.rearrange("(k p) c -> p k c", p=P)).then_inc(sem("wr_loaded"), 16)
                    sp.dma_start(wr[:, :, 8:72], w_re.rearrange("(k p) c -> p k c", p=P)).then_inc(sem("wr_loaded"), 16)
                    sp.dma_start(brb[:, 0:8], b_rg.partition_broadcast(P)).then_inc(sem("wr_loaded"), 16)
                    sp.dma_start(brb[:, 8:72], b_re.partition_broadcast(P)).then_inc(sem("wr_loaded"), 16)

            def expert(buf, e, s):
                ws = bass.ds(e, 1)
                sp.dma_start(wgu[buf][:, :, 0, :], w_eg[ws].rearrange("o (p k) f -> p (o k) f", k=KT)).then_inc(sem("gu_loaded" + s), 16)
                sp.dma_start(wgu[buf][:, :, 1, :], w_eu[ws].rearrange("o (p k) f -> p (o k) f", k=KT)).then_inc(sem("gu_loaded" + s), 16)

            def expert_down(buf, e, s):
                sp.dma_start(wdn[buf], w_ed[bass.ds(e, 1)].rearrange("o (j p) d -> p (o j) d", p=P)).then_inc(sem("dn_loaded" + s), 16)
            sp.wait_ge(sem("pw_used"), 1)
            expert(0, 0, "0")
            expert_down(0, 0, "0")
            used(sp, len(chunks) - 1)
            expert(1, 1, "1")
            expert_down(1, 1, "1")
            with sp.Fori(1, NE // 2) as i:
                for b in range(2):
                    sp.wait_ge(sem(f"gu_used{b}"), i)
                    expert(b, 2 * i + b, str(b))
                    sp.wait_ge(sem(f"dn_used{b}"), i)
                    expert_down(b, 2 * i + b, str(b))
            sp.wait_ge(sem("tables_ready"), 1)
            flag = sp.value_load(over_e[0:1, 16:17], min_val=0, max_val=NX)
            with sp.If(flag > 0):
                sp.wait_ge(sem("gu_used0"), NE // 2)
                sp.wait_ge(sem("dn_used0"), NE // 2)
                with sp.Fori(0, NX) as i:
                    sp.wait_ge(sem("over_free"), i + 1)
                    e = sp.value_load(over_e[0:1, bass.ds(i, 1)], min_val=0, max_val=NE - 1)
                    expert(0, e, "_over")
                    expert_down(0, e, "_over")
            with sp.Else():
                sp.nop()
            for i in range(NT):
                sp.wait_ge(sem("fin_ready"), i + 1)
                sp.dma_start(out[P * i:P * i + P, :], fin[i]).then_inc(sem("out_stored"), 16)
            sp.wait_ge(sem("out_stored"), 16 * NT)

        @block.tensor
        def _(pe):
            pe.wait_ge(sem("const_ready"), 5)
            pe.wait_ge(sem("prow_loaded"), 16 * 9)
            for a, (r0, n) in enumerate(((0, P), (P, 120), (PB, R_END))):
                t = pe.transpose(PS[:, 7, r0:r0 + n], prow[0:n, a, :], ident[0:n, 0:n])
            t.then_inc(sem("prm_turned"), 1)
            for i in range(NT):
                if i == NT - 1:
                    pe.wait_ge(sem("prm_ready"), 1)
                pe.wait_ge(sem("xs_ready"), i + 1)
                for k in range(KT):
                    t = pe.transpose(PS[:, 2 * i + k // 4, P * (k % 4):P * (k % 4) + P], xs[i % 2][:, P * k:P * k + P], ident)
                t.then_inc(sem("xT_done"), 1)
            pe.wait_ge(sem("xs_ready"), NT + 1)
            pe.wait_ge(sem("xT_taken"), 1)
            for k in range(KT):
                t = pe.transpose(PS[:, 0, META * k:META * k + META], xs[0][0:META, P * k:P * k + P], ident[0:META, 0:META])
            t.then_inc(sem("xT_done"), 1)
            pe.wait_ge(sem("xT_taken"), NT + 1)
            pair = [0]

            def next_pair():
                u = pair[0]
                pair[0] += 1
                if u >= 4:
                    pe.wait_ge(sem("pair_free"), u - 3)
                return 2 * (u % 4)

            def proj528(w, cols, rows=P):
                b = next_pair()
                for k in range(KT):
                    for hf in range(2):
                        t = pe.matmul(PS[0:rows, b + hf, 0:HALF], w[:, k, cols], hnT[:, k, HALF * hf:HALF * hf + HALF],
                                      start=(k == 0), stop=(k == KT - 1))
                t.then_inc(sem("pair_done"), 1)
                return t

            def chunk_ready(n):
                pe.wait_ge(sem(f"chunk_loaded{n % 3}"), chunk_at[n])
                return ring[n % 3]

            for n in range(4):
                w = chunk_ready(n)
                for c in range(2):
                    proj528(w, slice(P * c, P * c + P))
                    proj528(w, slice(256 + P * c, 256 + P * c + P))
            w = chunk_ready(C_K)
            for h in range(H):
                proj528(w, slice(P * h, P * h + P))
            pe.wait_ge(sem("wdl_loaded"), 16)
            proj528(wdl, slice(0, 16), rows=16)
            pe.wait_ge(sem("dlow_ready"), 1)
            pe.wait_ge(sem("wup_loaded"), 16)
            for h in range(H):
                b = next_pair()
                for hf in range(2):
                    t = pe.matmul(PS[:, b + hf, 0:HALF], wup[:, P * h:P * h + P], dlow[:, HALF * hf:HALF * hf + HALF],
                                  start=True, stop=True)
                t.then_inc(sem("pair_done"), 1)
            pe.wait_ge(sem("pair_free"), pair[0])

            single = [0]

            def next_single():
                u = single[0]
                single[0] += 1
                if u >= 4:
                    s, n = freed[u - 4]
                    pe.wait_ge(sem(s), n)
                return u % 4

            def proj512(w, c, moving):
                b = next_single()
                for k in range(KT):
                    t = pe.matmul(PS[:, b, :], w[:, k, P * c:P * c + P], moving[:, k, 0:T], start=(k == 0), stop=(k == KT - 1))
                t.then_inc(sem("single_done"), 1)
                return t

            w = chunk_ready(C_Q)
            for h in range(H):
                proj512(w, h, hnT)
            pe.wait_ge(sem("conv_done"), 8)
            for k in range(8):
                t = pe.matmul(PS[:, 6, :], mean_w, cv[:, k, :], start=(k == 0), stop=(k == 7))
            t.then_inc(sem("ln_mean"), 1)
            for j in range(2):
                w = chunk_ready(C_V + j)
                for i in range(NT + 1):
                    rows = P if i < NT else META
                    b = next_single()
                    for k in range(KT):
                        t = pe.matmul(PS[0:rows, b, :], hnT[:, k, P * i:P * i + rows], w[:, k, :], start=(k == 0), stop=(k == KT - 1))
                    t.then_inc(sem("single_done"), 1)
                if j == 0:
                    for k in range(8):
                        pe.wait_ge(sem("ln_sq"), k + 1)
                        t = pe.matmul(PS[:, 7, :], mean_w, th[k % 2], start=(k == 0), stop=(k == 7))
                        t.then_inc(sem("ln_sq_used"), 1)

            n_e, n_s, n_a = [0], [0], [0]

            def attend(t):
                kind, c = t[0], t[1]
                if kind in ("kdm", "lv", "diag", "kd", "ss"):
                    s = n_s[0]
                    n_s[0] += 1
                    bank = 4 + s % 2
                    if s >= 2:
                        pe.wait_ge(sem("score_taken"), s - 1)
                if kind in ("kdm", "lv", "kd"):
                    ei = n_e[0]
                    n_e[0] += 1
                    pe.wait_ge(sem("e_mul"), ei + 1)
                    ev = E[ei % 6]
                if kind == "kdm":
                    for h in range(H):
                        m = pe.transpose(PS[0:META, bank, P * h:P * h + P], ev[:, h, 0:META], ident)
                elif kind == "kd":
                    for h in range(H):
                        m = pe.transpose(PS[:, bank, P * h:P * h + P], ev[:, h, :], ident)
                elif kind == "lv":
                    for h in range(H):
                        m = pe.matmul(PS[:, bank, P * h:P * h + P], ev[:, h, :], ev[:, h, :], start=True, stop=True)
                elif kind == "diag":
                    for h in range(H):
                        m = pe.matmul(PS[:, bank, P * h:P * h + P], Kf[:, h, P * c:P * c + P], Qf[:, h, P * c:P * c + P],
                                      start=True, stop=True)
                elif kind == "ss":
                    pe.wait_ge(sem("o_sq"), c + 1)
                    sq = o_sq.rearrange("p (h b) t -> p h b t", h=H)
                    for vb in range(2):
                        m = pe.matmul(PS[:, bank, :].rearrange("p (h t) -> p h t", h=H), ones, sq[:, :, vb, :], start=(vb == 0), stop=(vb == 1))
                if kind in ("kdm", "lv", "diag", "kd", "ss"):
                    m.then_inc(sem("score_done"), 1)
                    return
                a = n_a[0]
                n_a[0] += 1
                if a >= 1:
                    pe.wait_ge(sem("acc_taken"), a)
                pe.wait_ge(sem("score_taken"), n_s[0])
                if kind == "o":
                    pe.wait_ge(sem("qe_ready"), c + 1)
                    for h in range(H):
                        for vb in range(2):
                            j = 2 * h + vb
                            o = PS[:, 6 + j // 4, P * (j % 4):P * (j % 4) + P]
                            pe.matmul(o, S[:, h, P * vb:P * vb + P], qe[c % 2][:, h, :], start=True, stop=False)
                            m = pe.matmul(o, V[:, c, P * j:P * j + P], scT[c % 2][:, h, :], start=False, stop=True)
                else:
                    rows = META if kind == "Sm" else P
                    vs = Vm if kind == "Sm" else V[:, c, :]
                    for h in range(H):
                        m = pe.matmul(PS[:, 6 + h // 2, DV * (h % 2):DV * (h % 2) + DV], kd[0:rows, h, :], vs[0:rows, DV * h:DV * h + DV],
                                      start=True, stop=True)
                m.then_inc(sem("acc_done"), 1)

            for b in range(NSLOT):
                n = C_GATES + b // 4
                if b % 4 == 0:
                    w = chunk_ready(n)
                proj512(w, b % 4, hnT)
                if b == 3:
                    pe.wait_ge(sem("ln_read"), 2)
                    pe.wait_ge(sem("sgl_act"), 14)
                for t_ in slots[b]:
                    attend(t_)
            pe.wait_ge(sem("u_final"), 8)
            for b in range(8):
                if b % 4 == 0:
                    w = chunk_ready(C_PW + b // 4)
                proj512(w, b % 4, cv)
            pe.wait_ge(sem("mix_ready"), 8)
            for j in range(2):
                w = chunk_ready(C_OUT + j)
                for i in range(NT):
                    b = next_single()
                    for k in range(KT):
                        t = pe.matmul(PS[:, b, :], GT[:, k, P * i:P * i + P], w[:, k, :], start=(k == 0), stop=(k == KT - 1))
                    t.then_inc(sem("single_done"), 1)
            pe.wait_ge(sem("wr_loaded"), 64)
            for i in range(NT):
                pe.wait_ge(sem("hn2_ready"), i + 1)
                if i >= 1:
                    pe.wait_ge(sem("hn2T_ready"), i)
                for k in range(KT):
                    t = pe.transpose(PS[:, 4 + k // 4, P * (k % 4):P * (k % 4) + P], hn2[:, i, P * k:P * k + P], ident)
                t.then_inc(sem("hn2T_done"), 1)
                pe.wait_ge(sem("hn2T_ready"), i + 1)
                if i >= 2:
                    pe.wait_ge(sem("logits_taken"), i - 1)
                for k in range(KT):
                    t = pe.matmul(PS[:, 6 + i % 2, 0:72], hn2T[i % 2][:, k, :], wr[:, k, :], start=(k == 0), stop=(k == KT - 1))
                t.then_inc(sem("logits_done"), 1)
            pe.wait_ge(sem("choice_ready"), 1)
            for i in range(NT + 1):
                for j in range(min(i + 1, NT)):
                    t = pe.matmul(PS[:, 0, NE * i:NE * i + NE], before if j == i else ones, Asum[:, j, :],
                                  start=(j == 0), stop=(j == min(i, NT - 1)))
            t.then_inc(sem("ranks_done"), 1)
            pe.wait_ge(sem("onehot_ready"), 1)
            for g in range(2):
                for n in range(2 * NT):
                    t = pe.matmul(PS[CAP * g:CAP * g + CAP, 1, 0:NBLK // 2], OR[n // NT][:, n % NT, :],
                                  AB[n // NT][:, n % NT, g::2], start=(n == 0), stop=(n == 2 * NT - 1))
            for n in range(2 * NT):
                t = pe.matmul(PS[0:CAP, 2, 0:16], OR[n // NT][:, n % NT, :], AB[n // NT][:, n % NT, NE:NBLK],
                              start=(n == 0), stop=(n == 2 * NT - 1))
            t.then_inc(sem("idx_done"), 1)

            def turn_rows():
                xv = xg.rearrange("r (p k) -> r k p", k=KT)
                for k in range(KT):
                    t = pe.transpose(PS[:, k // 4, P * (k % 4):P * (k % 4) + P], xv[:, k, :], ident)
                return t

            def gate_up(buf, col0, bank):
                for k in range(KT):
                    for g in range(2):
                        t = pe.matmul(PS[CAP * g:CAP * g + CAP, bank, :].rearrange("p (a f) -> p a f", a=2),
                                      xT[:, k, col0:col0 + CAP], wgu[buf][:, k, :, 256 * g:256 * g + 256],
                                      start=(k == 0), stop=(k == KT - 1))
                return t

            def turn_h(buf, bank):
                for b in range(2):
                    t = pe.transpose(PS[:, bank, P * b:P * b + P], hS[buf][:, P * b:P * b + P], ident)
                return t

            def down(buf, bank):
                for j in range(4):
                    for g in range(2):
                        t = pe.matmul(PS[CAP * g:CAP * g + CAP, bank, :], hT[buf][:, j % 2, j // 2, :],
                                      wdn[buf][:, j, 512 * g:512 * g + 512], start=(j == 0), stop=(j == 3))
                return t

            def pair_of_experts(i, first):
                pe.wait_ge(sem("rows_gathered"), 16 * (i + 1))
                if not first:
                    pe.wait_ge(sem("xT_ready"), i)
                turn_rows().then_inc(sem("rows_turned"), 1)
                pe.wait_ge(sem("xT_ready"), i + 1)
                for e in range(2):
                    pe.wait_ge(sem(f"gu_loaded{e}"), 32 * (i + 1))
                    if not first:
                        pe.wait_ge(sem(f"h_ready{e}"), i)
                    gate_up(e, CAP * e, 2 + e).then_inc(sem(f"gu_used{e}"), 1)
                    pe.wait_ge(sem(f"h_ready{e}"), i + 1)
                    if not first:
                        pe.wait_ge(sem(f"hT_ready{e}"), i)
                    turn_h(e, 4 + e).then_inc(sem(f"h_turned{e}"), 1)
                    pe.wait_ge(sem(f"hT_ready{e}"), i + 1)
                    pe.wait_ge(sem(f"dn_loaded{e}"), 16 * (i + 1))
                    if not first:
                        pe.wait_ge(sem(f"y_taken{e}"), i)
                    down(e, 6 + e).then_inc(sem(f"dn_used{e}"), 1)
            pair_of_experts(0, True)
            with pe.Fori(1, NE // 2) as i:
                pair_of_experts(i, False)

            pe.wait_ge(sem("tables_ready"), 1)
            flag = pe.value_load(over_e[0:1, 16:17], min_val=0, max_val=NX)
            with pe.If(flag > 0):
                with pe.Fori(0, NX) as i:
                    pe.wait_ge(sem("rows_gathered_over"), 16 * (i + 1))
                    turn_rows().then_inc(sem("rows_turned_over"), 1)
                    pe.wait_ge(sem("xT_ready_over"), i + 1)
                    pe.wait_ge(sem("gu_loaded_over"), 32 * (i + 1))
                    gate_up(0, 0, 2).then_inc(sem("gu_used_over"), 1)
                    pe.wait_ge(sem("h_ready_over"), i + 1)
                    turn_h(0, 4).then_inc(sem("h_turned_over"), 1)
                    pe.wait_ge(sem("hT_ready_over"), i + 1)
                    pe.wait_ge(sem("dn_loaded_over"), 16 * (i + 1))
                    down(0, 6).then_inc(sem("dn_used_over"), 1)
            with pe.Else():
                pe.nop()

        @block.scalar
        def _(act):
            link = linker(act, "act_order")
            cwr = conv_w.rearrange("t (c p) -> (t c) p", p=P)
            for dst, src in ((prow[:, 0, :], cwr[0:P]), (prow[0:120, 1, :], cwr[P:248]),
                             (prow[R_N1:R_N1 + 8, 2, :], norm1_g), (prow[R_GLA:R_GLA + 8, 2, :], gla_norm_g),
                             (prow[R_CB:R_CB + 8, 2, :], conv_b), (prow[R_LG:R_LG + 8, 2, :], conv_ln_g),
                             (prow[R_LB:R_LB + 8, 2, :], conv_ln_b), (prow[R_BG:R_BG + 16, 2, :], b_gate),
                             (prow[R_BD:R_BD + 4, 2, :], b_decay)):
                act.dma_start(dst, src).then_inc(sem("prow_loaded"), 16)
            act.dma_start(wdl, win_c[:, :, DL0:DL0 + 16]).then_inc(sem("wdl_loaded"), 16)
            act.dma_start(wup, w_decay_up).then_inc(sem("wup_loaded"), 16)
            for i in range(NT + 1):
                src = x0[:, i, :] if i < NT else xm
                n = P if i < NT else META
                act.wait_ge(sem(f"x_loaded{i}" if i < NT else "meta_loaded"), 16)
                link(act.activation(junk[0:n, :], src, ACT.Square, accum_out=ss[0:n, i:i + 1]))
                act.nop().then_inc(sem("ss_ready"), 1)
            for i in range(NT + 1):
                src = x0[:, i, :] if i < NT else xm
                n = P if i < NT else META
                act.wait_ge(sem("rs_ready"), i + 1)
                if i >= 2:
                    act.wait_ge(sem("xT_done"), i - 1)
                act.activation(xs[i % 2][0:n, :], src, ACT.Copy, scale=rs[0:n, i:i + 1]).then_inc(sem("xs_ready"), 1)
            act.wait_ge(sem("prm_ready"), 1)
            u = 0

            def pair_view(u, rows=P):
                b = 2 * (u % 4)
                return PS[0:rows, b:b + 2, 0:HALF]

            def split(t):
                return t.rearrange("p (a t) -> p a t", a=2)
            for c in range(8):
                if c >= 2:
                    act.wait_ge(sem("u_ready"), c - 1)
                act.wait_ge(sem("pair_done"), u + 1)
                act.activation(split(glu_t[c % 2]), pair_view(u), ACT.Copy).then_inc(sem("pair_free"), 1)
                u += 1
                act.wait_ge(sem("pair_done"), u + 1)
                act.activation(split(glu_t[2 + c % 2]), pair_view(u), ACT.Tanh, scale=0.5).then_inc(sem("pair_free"), 1)
                u += 1
            for h in range(H):
                act.wait_ge(sem("pair_done"), u + 1)
                act.activation(split(Kf[:, h, :]), pair_view(u), ACT.Copy).then_inc(sem("pair_free"), 1)
                u += 1
            act.wait_ge(sem("pair_done"), u + 1)
            act.wait_ge(sem("u_ready"), 8)
            link(act.activation(split(dlow), pair_view(u, 16), ACT.Copy))
            act.nop().then_inc(sem("dlow_ready"), 1)
            act.nop().then_inc(sem("pair_free"), 1)
            u += 1
            for h in range(H):
                act.wait_ge(sem("pair_done"), u + 1)
                if h >= 2:
                    act.wait_ge(sem("decay_taken"), h - 1)
                act.activation(split(glu_t[h % 2]), pair_view(u), ACT.Identity, bias=par(R_BD, h))
                link(act.activation(split(glu_t[2 + h % 2]), pair_view(u), ACT.Abs, bias=par(R_BD, h)))
                act.nop().then_inc(sem("pair_free"), 1)
                u += 1
                link(act.activation(glu_t[2 + h % 2], glu_t[2 + h % 2], ACT.Exp, scale=-1.0))
                act.activation(glu_t[2 + h % 2], glu_t[2 + h % 2], ACT.Ln, bias=1.0).then_inc(sem("decay_logs"), 1)
            s = 0
            for h in range(H):
                act.wait_ge(sem("single_done"), s + 1)
                act.activation(Qf[:, h, :], PS[:, s % 4, :], ACT.Copy, scale=float(DK) ** -0.5).then_inc(sem("sgl_act"), 1)
                s += 1

            def values(j):
                nonlocal s
                for i in range(NT + 1):
                    act.wait_ge(sem("single_done"), s + 1)
                    n = P if i < NT else META
                    dst = V[:, i, 512 * j:512 * j + 512] if i < NT else Vm[:, 512 * j:512 * j + 512]
                    act.activation(dst, PS[0:n, s % 4, :], ACT.Copy).then_inc(sem("sgl_act"), 1)
                    s += 1
            for k in range(8):
                act.wait_ge(sem("ln_centred"), k + 1)
                if k >= 2:
                    act.wait_ge(sem("ln_sq_used"), k - 1)
                act.activation(th[k % 2], cv[:, k, :], ACT.Square).then_inc(sem("ln_sq"), 1)
                if k == 1:
                    values(0)
            for k in range(8):
                act.wait_ge(sem("ln_scaled"), k + 1)
                if k >= 2:
                    act.wait_ge(sem("u_final"), k - 1)
                act.activation(th[k % 2], cv[:, k, :], ACT.Tanh, scale=par(R_LG, k), bias=par(R_LB, k)).then_inc(sem("ln_tanh"), 1)
                if k == 1:
                    values(1)
            n_e = 0
            for b in range(NSLOT):
                for t in slots[b]:
                    if t[0] in ("kdm", "lv", "kd"):
                        act.wait_ge(sem("e_sub"), n_e + 1)
                        ev = E[n_e % 6]
                        if t[0] == "kdm":
                            ev = ev[:, :, 0:META]
                        act.activation(ev, ev, ACT.Exp, scale=1.0 / TAU).then_inc(sem("e_exp"), 1)
                        n_e += 1
                    if t[0] == "lv" and t[2] == 0:
                        c = t[1]
                        if c == 0:
                            act.wait_ge(sem("over_zeroed"), 16 * ((NBLK - NE) * CAP // P))
                        if c >= 2:
                            act.wait_ge(sem("acc_done"), a_tasks.index(("o", c - 2)) + 1)
                        act.activation(elast[c], Bf[:, :, P * c + P - 1:P * c + P], ACT.Exp, scale=1.0 / TAU)
                        act.activation(qe[c % 2], Bf[:, :, P * c:P * c + P], ACT.Exp, scale=1.0 / TAU).then_inc(sem("qe_exp"), 1)
                act.wait_ge(sem("single_done"), s + 1)
                bank = PS[:, s % 4, :]
                s += 1
                if b in GA_BLOCKS:
                    act.activation(GT[:, b, :], bank, ACT.Tanh, scale=0.5, bias=par(R_BG, b)).then_inc(sem("sgl_act"), 1)
                elif b in OG_BLOCKS:
                    k = b - 8
                    if k >= 2:
                        act.wait_ge(sem("sgl_dve"), k - 1)
                    else:
                        act.wait_ge(sem("u_final"), 8)
                    act.activation(th[k % 2], bank, ACT.Tanh, scale=0.5).then_inc(sem("og_tanh"), 1)
                else:
                    if b == 16:
                        act.wait_ge(sem("conv_done"), 8)
                    act.activation(U[:, b - 16, 0:T], bank, ACT.Tanh, scale=0.5, bias=par(R_BG, 8 + b - 16)).then_inc(sem("sgl_act"), 1)
            for i in range(NT):
                act.wait_ge(sem("h_ready"), i + 1)
                if i == 0:
                    act.wait_ge(sem("attention_done"), 1)
                link(act.activation(junk2, xr[:, i, :], ACT.Square, accum_out=ss[:, i:i + 1]))
                act.nop().then_inc(sem("ss2_ready"), 1)
                act.wait_ge(sem("rs2_ready"), i + 1)
                act.activation(hn2[:, i, :], xr[:, i, :], ACT.Copy, scale=rs[:, i:i + 1]).then_inc(sem("hn2_scaled"), 1)
            act.wait_ge(sem("group_diff"), 1)
            act.activation(eg, eg, ACT.Exp).then_inc(sem("group_exp"), 1)
            act.wait_ge(sem("choice_diff"), 1)
            act.activation(m4[3], m4[3], ACT.Exp).then_inc(sem("choice_exp"), 1)

            def expert(i, e, buf, s, first, store):
                act.wait_ge(sem("gu_used" + s), i + 1)
                if not first:
                    act.wait_ge(sem("h_ready" + s), i)
                act.activation(gth[buf], PS[:, 2 + buf, 0:256], ACT.Tanh, scale=0.5).then_inc(sem("g_tanh" + s), 1)
                act.wait_ge(sem("dn_used" + s), i + 1)
                if not first:
                    act.wait_ge(sem("y_stored" + s), 32 * i)
                act.activation(ysb[buf], PS[:, 6 + buf, :], ACT.Copy).then_inc(sem("y_taken" + s), 1)
                act.wait_ge(sem("y_taken" + s), i + 1)
                for g in range(2):
                    act.dma_start(y_d[bass.ds(store * CAP, CAP), 512 * g:512 * g + 512],
                                  ysb[buf][CAP * g:CAP * g + CAP, :]).then_inc(sem("y_stored" + s), 16)
            act.wait_ge(sem("rows_gathered"), 16)
            for e in range(2):
                expert(0, e, e, str(e), True, e)
            with act.Fori(1, NE // 2) as i:
                for e in range(2):
                    expert(i, e, e, str(e), False, 2 * i + e)
            act.wait_ge(sem("tables_ready"), 1)
            flag = act.value_load(over_e[0:1, 16:17], min_val=0, max_val=NX)
            with act.If(flag > 0):
                act.wait_ge(sem("y_stored0"), 16 * NE)
                act.nop().then_inc(sem("over_free"), 1)
                with act.Fori(0, NX) as i:
                    act.wait_ge(sem("gu_used_over"), i + 1)
                    act.activation(gth[0], PS[:, 2, 0:256], ACT.Tanh, scale=0.5).then_inc(sem("g_tanh_over"), 1)
                    act.wait_ge(sem("dn_used_over"), i + 1)
                    act.activation(ysb[0], PS[:, 6, :], ACT.Copy).then_inc(sem("y_taken_over"), 1)
                    act.wait_ge(sem("y_taken_over"), i + 1)
                    for g in range(2):
                        act.dma_start(y_d[bass.ds((i + NE) * CAP, CAP), 512 * g:512 * g + 512],
                                      ysb[0][CAP * g:CAP * g + CAP, :]).then_inc(sem("y_stored_over"), 16)
                    act.wait_ge(sem("y_stored_over"), 32 * (i + 1))
                    act.nop().then_inc(sem("over_free"), 1)
            with act.Else():
                act.nop()
            act.wait_ge(sem("y_stored0"), 16 * NE)
            act.wait_ge(sem("y_stored1"), 16 * NE)
            act.wait_ge(sem("over_zeroed"), 16 * ((NBLK - NE) * CAP // P))
            act.nop().then_inc(sem("y_all"), 1)
            for i in range(NT):
                act.wait_ge(sem("h_final"), i + 1)
                link(act.activation(fin[i], xr[:, i, :], ACT.Square, accum_out=ss[:, i:i + 1]))
                act.nop().then_inc(sem("ss3_ready"), 1)
                act.wait_ge(sem("rs3_ready"), i + 1)
                act.activation(fin[i], xr[:, i, :], ACT.Copy, scale=rs[:, i:i + 1]).then_inc(sem("fin_scaled"), 1)

        @block.gpsimd
        def _(pool):
            link = linker(pool, "pool_order")
            link(pool.memset(ident, 0.0))
            pool.affine_select(out=ident, in_=ident, compare_op=ALU.not_equal, fill=1.0, base=0,
                               pattern=[[-1, P]], channel_multiplier=1).then_inc(sem("const_ready"), 1)
            pool.memset(ones, 1.0).then_inc(sem("const_ready"), 1)
            pool.memset(mean_w, 1.0 / D).then_inc(sem("const_ready"), 1)
            link(pool.memset(before, 1.0))
            pool.affine_select(out=before, in_=before, compare_op=ALU.is_gt, fill=0.0, base=0,
                               pattern=[[1, P]], channel_multiplier=-1).then_inc(sem("const_ready"), 1)
            pool.iota(cst_i[:, 0, :], pattern=[[1, P]], base=0, channel_multiplier=0).then_inc(sem("iota_ready"), 1)
            pool.iota(cst_i[:, 1, :], pattern=[[0, P]], base=0, channel_multiplier=1).then_inc(sem("iota_ready"), 1)
            pool.iota(iota, pattern=[[1, NBLK]], base=0, channel_multiplier=0, allow_small_or_imprecise_dtypes=True)
            pool.iota(tokid, pattern=[[P, NT]], base=0, channel_multiplier=1, allow_small_or_imprecise_dtypes=True)
            pool.memset(U[:, :, 0:14], 0.0)
            pool.memset(nhalf, -0.5)
            pool.memset(view(QE, D), 0.0)
            pool.memset(scT[0], 0.0)
            pool.memset(scT[1], 0.0).then_inc(sem("const_ready"), 1)

            pool.wait_ge(sem("const_ready"), 5)
            for j in range((NBLK - NE) * CAP // P):
                pool.dma_start(y_d[NE * CAP + P * j:NE * CAP + P * j + P, :], view(QE, D)).then_inc(sem("over_zeroed"), 16)

            def rsqrt(v, wait, n, done, rows=P):
                pool.wait_ge(sem(wait), n)
                pool.tensor_tensor(v, v, nhalf[0:rows, :].to_broadcast([rows, v.shape[-1]]), ALU.pow).then_inc(sem(done), 1)
            for i in range(NT + 1):
                n = P if i < NT else META
                rsqrt(rs[0:n, i:i + 1], "ms_ready", i + 1, "rs_ready", n)
            for c in range(8):
                v, g = glu_t[c % 2], glu_t[2 + c % 2]
                pool.wait_ge(sem("pair_free"), 2 * c + 2)
                link(pool.tensor_tensor(g, g, v, ALU.mult))
                pool.tensor_tensor(U[:, c, 30:542], g[:, 0:T], v[:, 0:T], ALU.add)
                pool.tensor_tensor(U[:, c, 14:30], g[:, T:L], v[:, T:L], ALU.add).then_inc(sem("u_ready"), 1)
            rsqrt(rst, "ln_read", 2, "ln_rstd")
            n_e = 0
            for b in range(NSLOT):
                for t in slots[b]:
                    c = t[1]
                    if t[0] in ("kdm", "lv", "kd"):
                        ev = E[n_e % 6]
                        pool.wait_ge(sem("e_exp"), n_e + 1)
                        if t[0] == "kdm":
                            m = pool.tensor_tensor(ev[:, :, 0:META], ev[:, :, 0:META], Kf[:, :, T:L], ALU.mult)
                        elif t[0] == "kd":
                            m = pool.tensor_tensor(ev, ev, Kf[:, :, P * c:P * c + P], ALU.mult)
                        else:
                            w = LEVELS[t[2]]
                            e4 = ev.rearrange("p h (g a w) -> p h g a w", a=2, w=w)
                            k4 = Kf[:, :, P * c:P * c + P].rearrange("p h (g a w) -> p h g a w", a=2, w=w)
                            q4 = Qf[:, :, P * c:P * c + P].rearrange("p h (g a w) -> p h g a w", a=2, w=w)
                            pool.tensor_tensor(e4[:, :, :, 0, :], e4[:, :, :, 0, :], k4[:, :, :, 0, :], ALU.mult)
                            m = pool.tensor_tensor(e4[:, :, :, 1, :], e4[:, :, :, 1, :], q4[:, :, :, 1, :], ALU.mult)
                        m.then_inc(sem("e_mul"), 1)
                        n_e += 1
                    if t[0] == "lv" and t[2] == 0:
                        pool.wait_ge(sem("qe_exp"), c + 1)
                        pool.tensor_tensor(qe[c % 2], qe[c % 2], Qf[:, :, P * c:P * c + P], ALU.mult).then_inc(sem("qe_ready"), 1)
                    if t[0] == "o":
                        pool.wait_ge(sem("acc_taken"), a_tasks.index(t) + 1)
                        if c >= 1:
                            pool.wait_ge(sem("score_done"), s_tasks.index(("ss", c - 1)) + 1)
                        pool.tensor_tensor(o_sq, o_t, o_t, ALU.mult).then_inc(sem("o_sq"), 1)
                    if t[0] == "ss":
                        rsqrt(rst, "score_taken", s_tasks.index(t) + 1, "o_rstd")
                if b in GA_BLOCKS:
                    pool.wait_ge(sem("sgl_act"), 14 + b + 1)
                    pool.tensor_scalar(GT[:, b, :], GT[:, b, :], 1.0, None, ALU.add).then_inc(sem("ga_ready"), 1)
            pool.wait_ge(sem("g2_loaded"), 16)
            for i in range(NT):
                rsqrt(rs[:, i:i + 1], "ms2_ready", i + 1, "rs2_ready")
                pool.wait_ge(sem("hn2_scaled"), i + 1)
                pool.tensor_tensor(hn2[:, i, :], hn2[:, i, :], g2b, ALU.mult).then_inc(sem("hn2_ready"), 1)
                pool.wait_ge(sem("hn2_ready"), i + 1)
                pool.dma_start(hn2_d[P * i:P * i + P, :], hn2[:, i, :]).then_inc(sem("hn2_stored"), 16)

            def gather(nth, first):
                if not first:
                    pool.wait_ge(sem("rows_turned"), nth - 1)
                pool.tensor_copy(idx_now[:, :], idx_pair[:, bass.ds(nth - 1, 1)]).then_inc(sem("idx_now"), 1)
                pool.wait_ge(sem("tables_ready"), 1)
                pool.wait_ge(sem("idx_now"), nth)
                pool.indirect_dma_start(xg, None, hn2_d, bass.IndirectOffsetOnAxis(ap=idx_now[:, 0:1], axis=0)).then_inc(sem("rows_gathered"), 16)
            pool.wait_ge(sem("hn2_stored"), 16 * NT)
            pool.wait_ge(sem("hn2T_done"), NT)
            pool.wait_ge(sem("tables_ready"), 1)
            gather(1, True)
            with pool.Fori(2, NE // 2 + 1) as nth:
                gather(nth, False)
            flag = pool.value_load(over_e[0:1, 16:17], min_val=0, max_val=NX)
            with pool.If(flag > 0):
                pool.wait_ge(sem("rows_turned"), NE // 2)
                pool.wait_ge(sem("gu_used1"), NE // 2)
                with pool.Fori(0, NX) as i:
                    nth = i + 1
                    pool.wait_ge(sem("over_free"), nth)
                    pool.tensor_copy(idx_now[0:CAP, :], idx_over[:, bass.ds(i, 1)]).then_inc(sem("idx_now_over"), 1)
                    pool.wait_ge(sem("tables_ready"), 1)
                    pool.wait_ge(sem("idx_now_over"), nth)
                    pool.indirect_dma_start(xg[0:CAP, :], None, hn2_d, bass.IndirectOffsetOnAxis(ap=idx_now[0:CAP, 0:1], axis=0)).then_inc(sem("rows_gathered_over"), 16)
            with pool.Else():
                pool.nop()
            pool.wait_ge(sem("y_all"), 1)
            pool.wait_ge(sem("gu_used0"), NE // 2)
            for i in range(NT):
                for k in range(2):
                    pool.indirect_dma_start(yt[2 * i + k], None, y_d, bass.IndirectOffsetOnAxis(ap=pos_i[:, k, i:i + 1], axis=0)).then_inc(sem(f"y_back{2 * i + k}"), 16)
            for i in range(NT):
                rsqrt(rs[:, i:i + 1], "ms3_ready", i + 1, "rs3_ready")

        @block.vector
        def _(dve):
            link = linker(dve, "dve_order")
            dve.wait_ge(sem("iota_ready"), 2)
            xi, xf = cst_i[:, 0, :], view(SB, P)
            link(dve.tensor_tensor(xi, cst_i[:, 0, :], cst_i[:, 1, :], ALU.bitwise_xor))
            link(dve.tensor_copy(xf, xi))
            dve.wait_ge(sem("const_ready"), 5)
            big = view(SB + P, P)
            link(dve.tensor_tensor(big, before, ident, ALU.add))
            link(dve.tensor_scalar(big, big, -1000.0, 1000.0, ALU.mult, ALU.add))
            link(dve.tensor_tensor(xf, xf, big, ALU.add))
            for n, w in enumerate(LEVELS + [0.5]):
                link(dve.tensor_scalar(masks[:, n, :], xf, float(2 * w), None, ALU.is_lt))
            for i in range(NT + 1):
                n = P if i < NT else META
                dve.wait_ge(sem("ss_ready"), i + 1)
                dve.tensor_scalar(rs[0:n, i:i + 1], ss[0:n, i:i + 1], 1.0 / D, EPS, ALU.mult, ALU.add).then_inc(sem("ms_ready"), 1)
            dve.wait_ge(sem("prm_turned"), 1)
            link(dve.tensor_copy(prm[:, 0:PB + R_END], PS[:, 7, 0:PB + R_END]))
            link(dve.tensor_scalar(prm[:, 0:PB], prm[:, 0:PB], 0.5, None, ALU.mult))
            link(dve.tensor_scalar(prm[:, PB + R_GLA:PB + R_GLA + 8], prm[:, PB + R_GLA:PB + R_GLA + 8], 0.25, None, ALU.mult))
            link(dve.tensor_scalar(prm[:, PB + R_LG:PB + R_BG + 16], prm[:, PB + R_LG:PB + R_BG + 16], 0.5, None, ALU.mult))
            dve.nop().then_inc(sem("prm_ready"), 1)
            for i in range(NT + 1):
                dve.wait_ge(sem("xT_done"), i + 1)
                if i < NT:
                    for hf in range(2):
                        g = prm[:, PB + 4 * hf:PB + 4 * hf + 4].rearrange("p (k o) -> p k o", o=1)
                        m = dve.tensor_tensor(hnT[:, 4 * hf:4 * hf + 4, P * i:P * i + P],
                                              PS[:, 2 * i + hf, :].rearrange("p (k t) -> p k t", k=4),
                                              g.to_broadcast([P, 4, P]), ALU.mult)
                else:
                    g = prm[:, PB:PB + 8].rearrange("p (k o) -> p k o", o=1)
                    m = dve.tensor_tensor(hnT[:, :, T:L], PS[:, 0, 0:KT * META].rearrange("p (k t) -> p k t", k=KT),
                                          g.to_broadcast([P, KT, META]), ALU.mult)
                m.then_inc(sem("xT_taken"), 1)
            for c in range(8):
                dve.wait_ge(sem("u_ready"), c + 1)
                link(dve.tensor_scalar(cv[:, c, :], U[:, c, 0:T], cw(0, c), par(R_CB, c), ALU.mult, ALU.add))
                for t in range(1, TAPS):
                    m = dve.scalar_tensor_tensor(out=cv[:, c, :], in0=U[:, c, t:t + T], scalar=cw(t, c), in1=cv[:, c, :],
                                                 op0=ALU.mult, op1=ALU.add)
                    if t < TAPS - 1:
                        link(m)
                m.then_inc(sem("conv_done"), 1)
            for h in range(H):
                dve.wait_ge(sem("decay_logs"), h + 1)
                dve.scalar_tensor_tensor(out=Bf[:, h, :], in0=glu_t[h % 2], scalar=0.0, in1=glu_t[2 + h % 2],
                                         op0=ALU.min, op1=ALU.subtract).then_inc(sem("decay_taken"), 1)
                dve.wait_ge(sem("decay_taken"), h + 1)
                for c in range(NT + 1):
                    a, n = P * c, P if c < NT else META
                    m = dve.tensor_tensor_scan(Bf[:, h, a:a + n], ones[:, 0:n], Bf[:, h, a:a + n], 0.0, ALU.mult, ALU.add)
            link(m)
            dve.wait_ge(sem("ln_mean"), 1)
            for k in range(8):
                m = dve.tensor_tensor(cv[:, k, :], cv[:, k, :], PS[:, 6, :], ALU.subtract)
                m.then_inc(sem("ln_centred"), 1)
            dve.nop().then_inc(sem("ln_read"), 1)
            dve.wait_ge(sem("ln_sq_used"), 8)
            dve.tensor_scalar(rst, PS[:, 7, :], EPS, None, ALU.add).then_inc(sem("ln_read"), 1)
            dve.wait_ge(sem("ln_rstd"), 1)
            for k in range(8):
                dve.tensor_tensor(cv[:, k, :], cv[:, k, :], rst, ALU.mult).then_inc(sem("ln_scaled"), 1)
            for k in range(8):
                dve.wait_ge(sem("ln_tanh"), k + 1)
                link(dve.tensor_scalar(cv[:, k, :], cv[:, k, :], par(R_LG, k), par(R_LB, k), ALU.mult, ALU.add))
                dve.scalar_tensor_tensor(out=cv[:, k, :], in0=th[k % 2], scalar=1.0, in1=cv[:, k, :],
                                         op0=ALU.add, op1=ALU.mult).then_inc(sem("u_final"), 1)

            n_e, n_s, n_a = [0], [0], [0]

            def differences(t):
                c = t[1]
                ei = n_e[0]
                n_e[0] += 1
                if ei >= 6:
                    dve.wait_ge(sem("score_done"), s_tasks.index(e_tasks[ei - 6]) + 1)
                ev = E[ei % 6]
                if t[0] in ("kdm", "kd"):
                    a, n = (T, META) if t[0] == "kdm" else (P * c, P)
                    m = dve.tensor_tensor(ev[:, :, 0:n], Bf[:, :, a + n - 1:a + n].to_broadcast([P, H, n]), Bf[:, :, a:a + n], ALU.subtract)
                else:
                    w = LEVELS[t[2]]
                    e4 = ev.rearrange("p h (g a w) -> p h g a w", a=2, w=w)
                    b4 = Bf[:, :, P * c:P * c + P].rearrange("p h (g a w) -> p h g a w", a=2, w=w)
                    ref = b4[:, :, :, 0, w - 1:w].to_broadcast([P, H, 64 // w, w])
                    dve.tensor_tensor(e4[:, :, :, 0, :], ref, b4[:, :, :, 0, :], ALU.subtract)
                    m = dve.tensor_tensor(e4[:, :, :, 1, :], b4[:, :, :, 1, :], ref, ALU.subtract)
                m.then_inc(sem("e_sub"), 1)

            def take(t):
                kind, c = t[0], t[1]
                if kind in ("kdm", "lv", "diag", "kd", "ss"):
                    s = n_s[0]
                    n_s[0] += 1
                    bank = PS[:, 4 + s % 2, :].rearrange("p (h t) -> p h t", h=H)
                    dve.wait_ge(sem("score_done"), s + 1)
                    if kind in ("lv", "diag"):
                        lv = t[2] if kind == "lv" else 7
                        mk = masks[:, lv, :].rearrange("p (o t) -> p o t", o=1).broadcast_to([P, H, P])
                        if lv == 0 and c >= 2:
                            dve.wait_ge(sem("acc_done"), a_tasks.index(("o", c - 2)) + 1)
                        dve.copy_predicated(scT[c % 2], mk, bank).then_inc(sem("score_taken"), 1)
                        dve.wait_ge(sem("score_taken"), s + 1)
                    elif kind == "ss":
                        dve.tensor_scalar(rst, PS[:, 4 + s % 2, :], 1.0 / DV, EPS, ALU.mult, ALU.add).then_inc(sem("score_taken"), 1)
                        dve.wait_ge(sem("o_rstd"), c + 1)
                        o4 = o_t.rearrange("p (h b) t -> p h b t", h=H)
                        r4 = rst.rearrange("p (h o t) -> p h o t", h=H, o=1).broadcast_to([P, H, 2, P])
                        link(dve.tensor_tensor(o4, o4, r4, ALU.mult))
                        g = prm[:, PB + R_GLA:PB + R_GLA + 8].rearrange("p (k o) -> p k o", o=1).to_broadcast([P, 8, P])
                        link(dve.tensor_tensor(o_t, o_t, g, ALU.mult))
                        gt = GT[:, :, P * c:P * c + P]
                        dve.wait_ge(sem("ga_ready"), 8)
                        m = dve.tensor_tensor(gt, gt, o_t, ALU.mult)
                        link(m)
                        if c == NT - 1:
                            dve.nop().then_inc(sem("attention_done"), 1)
                    else:
                        rows = META if kind == "kdm" else P
                        if kind == "kd" and c >= 0:
                            dve.wait_ge(sem("acc_done"), a_tasks.index(("S", c - 1) if c else ("Sm", 0)) + 1)
                        dve.tensor_copy(kd[0:rows], bank[0:rows]).then_inc(sem("score_taken"), 1)
                    return
                a = n_a[0]
                n_a[0] += 1
                dve.wait_ge(sem("acc_done"), a + 1)
                pair = PS[:, 6:8, :]
                if kind == "o":
                    m = dve.tensor_copy(o_t.rearrange("p (a b) t -> p a (b t)", a=2), pair)
                elif kind == "Sm":
                    m = dve.tensor_copy(S.rearrange("p (a h) v -> p a (h v)", a=2), pair)
                else:
                    for h in range(H):
                        m = dve.scalar_tensor_tensor(out=S[:, h, :], in0=S[:, h, :], scalar=elast[c][:, h, :],
                                                     in1=PS[:, 6 + h // 2, DV * (h % 2):DV * (h % 2) + DV], op0=ALU.mult, op1=ALU.add)
                m.then_inc(sem("acc_taken"), 1)
                dve.wait_ge(sem("acc_taken"), a + 1)

            s = 14
            og = 0
            for b in range(NSLOT + 1):
                if b < NSLOT:
                    for t in slots[b]:
                        if t[0] in ("kdm", "lv", "kd"):
                            differences(t)
                if b >= 1:
                    for t in slots[b - 1]:
                        take(t)
                    if b - 1 in OG_BLOCKS:
                        k = b - 1 - 8
                        bank = PS[:, (14 + b - 1) % 4, :]
                        dve.wait_ge(sem("og_tanh"), k + 1)
                        dve.wait_ge(sem("ga_ready"), 8)
                        link(dve.scalar_tensor_tensor(out=th[k % 2], in0=th[k % 2], scalar=1.0, in1=bank, op0=ALU.add, op1=ALU.mult))
                        link(dve.tensor_tensor(GT[:, k, :], GT[:, k, :], th[k % 2], ALU.mult))
                        dve.nop().then_inc(sem("sgl_dve"), 1)
            u = 38
            for k in range(8):
                dve.wait_ge(sem("single_done"), u + 1)
                bank = PS[:, u % 4, :]
                u += 1
                dve.wait_ge(sem("sgl_act"), 14 + 8 + k + 1)
                link(dve.scalar_tensor_tensor(out=th[k % 2], in0=U[:, k, 0:T], scalar=1.0, in1=bank, op0=ALU.add, op1=ALU.mult))
                dve.nop().then_inc(sem("sgl_dve"), 1)
                link(dve.scalar_tensor_tensor(out=GT[:, k, :], in0=th[k % 2], scalar=0.5, in1=GT[:, k, :], op0=ALU.mult, op1=ALU.add))
                dve.nop().then_inc(sem("mix_ready"), 1)
            dve.nop().then_inc(sem("pw_used"), 1)
            dve.wait_ge(sem("xr_loaded"), 16)
            for j in range(2):
                for i in range(NT):
                    dve.wait_ge(sem("single_done"), u + 1)
                    hv = xr[:, i, 512 * j:512 * j + 512]
                    m = dve.tensor_tensor(hv, hv, PS[:, u % 4, :], ALU.add)
                    u += 1
                    m.then_inc(sem("sgl_dve"), 1)
                    if j == 1:
                        dve.wait_ge(sem("sgl_dve"), 16 + 4 + i + 1)
                        dve.nop().then_inc(sem("h_ready"), 1)
            dve.wait_ge(sem("wr_loaded"), 64)

            def rms(i, a, b):
                dve.wait_ge(sem(a), i + 1)
                dve.tensor_scalar(rs[:, i:i + 1], ss[:, i:i + 1], 1.0 / D, EPS, ALU.mult, ALU.add).then_inc(sem(b), 1)
            for i in range(NT):
                rms(i, "ss2_ready", "ms2_ready")
                dve.wait_ge(sem("hn2T_done"), i + 1)
                if i >= 2:
                    dve.wait_ge(sem("logits_done"), i - 1)
                dve.tensor_copy(hn2T[i % 2].rearrange("p (a k) t -> p a (k t)", a=2), PS[:, 4:6, :]).then_inc(sem("hn2T_ready"), 1)
                dve.wait_ge(sem("logits_done"), i + 1)
                dve.tensor_tensor(lg[:, i, :], PS[:, 6 + i % 2, 0:72], brb, ALU.add).then_inc(sem("logits_taken"), 1)
            dve.wait_ge(sem("logits_taken"), NT)
            used(dve, len(chunks) - 1)

            def tt(o, a, b, op):
                link(dve.tensor_tensor(o, a, b, op))

            def red(o, a, op=ALU.add):
                link(dve.tensor_reduce(o, a, AX.X, op))

            def b3(v, n):
                return v.rearrange("p (i o) -> p i o", o=1).to_broadcast([P, NT, n])

            def over_i(v, n):
                return v.rearrange("p (o n) -> p o n", o=1).broadcast_to([P, NT, n])
            io8 = over_i(iota[:, 0:8], 8)
            link(dve.tensor_scalar(desc8, iota[:, 0:8], -1.0, 8.0, ALU.mult, ALU.add))
            link(dve.memset(ones64, 1.0))

            def first_max(one, vals, mx):
                red(mx, vals, ALU.max)
                tt(one, vals, b3(mx, 8), ALU.is_equal)
                tt(tb, one, over_i(desc8, 8), ALU.mult)
                red(m4[7], tb, ALU.max)
                tt(one, tb, b3(m4[7], 8), ALU.is_equal)
            lgg = lg[:, :, 0:8]
            first_max(oh, lgg, m4[0])
            dve.tensor_tensor(eg, lgg, b3(m4[0], 8), ALU.subtract).then_inc(sem("group_diff"), 1)
            lge = lg[:, :, 8:72].rearrange("p i (g e) -> p i g e", g=NG)
            tt(prod, lge, oh.rearrange("p i (g o) -> p i g o", o=1).to_broadcast([P, NT, NG, EPG]), ALU.mult)
            red(sel, prod.rearrange("p i g e -> p i e g"))
            first_max(o12[0], sel, m4[1])
            link(dve.scalar_tensor_tensor(out=sel2, in0=o12[0], scalar=-3e38, in1=sel, op0=ALU.mult, op1=ALU.add))
            first_max(o12[1], sel2, m4[2])
            dve.tensor_tensor(m4[3], m4[2], m4[1], ALU.subtract).then_inc(sem("choice_diff"), 1)
            tt(tb, oh, io8, ALU.mult)
            red(gid, tb)
            for k in range(2):
                tt(tb, o12[k], io8, ALU.mult)
                red(e_id[:, k, :], tb)
                link(dve.scalar_tensor_tensor(out=e_id[:, k, :], in0=gid, scalar=float(EPG), in1=e_id[:, k, :], op0=ALU.mult, op1=ALU.add))
                tt(A[k], over_i(iota[:, 0:NE], NE), b3(e_id[:, k, :], NE), ALU.is_equal)
            tt(Asum, A[0], A[1], ALU.add)
            dve.nop().then_inc(sem("choice_ready"), 1)
            dve.wait_ge(sem("group_exp"), 1)
            red(m4[4], eg)
            dve.wait_ge(sem("choice_exp"), 1)
            link(dve.tensor_scalar(m4[5], m4[3], 1.0, None, ALU.add))
            tt(m4[4], m4[4], m4[5], ALU.mult)
            link(dve.reciprocal(wgt[0], m4[4]))
            tt(wgt[1], wgt[0], m4[3], ALU.mult)
            dve.wait_ge(sem("ranks_done"), 1)
            link(dve.tensor_copy(Ccnt, PS[:, 0, 0:320].rearrange("p (i e) -> p i e", i=NT + 1)))
            link(dve.memset(nx, 0.0))
            for m in range(1, T // CAP):
                link(dve.scalar_tensor_tensor(out=nx, in0=Ccnt[:, NT, :], scalar=float(CAP * m), in1=nx, op0=ALU.is_gt, op1=ALU.add))
            link(dve.tensor_tensor_scan(end, ones64, nx, 0.0, ALU.mult, ALU.add))
            tt(start, end, nx, ALU.subtract)
            big3 = prod.rearrange("p i g e -> p i (g e)")
            for k in range(2):
                tt(big3, A[k], Ccnt[:, 0:NT, :], ALU.mult)
                red(rank[:, k, :], big3)
                tt(big3, A[k], over_i(start, NE), ALU.mult)
                red(stt_[:, k, :], big3)
            link(dve.memset(rnd, 0.0))
            for m in range(1, T // CAP):
                link(dve.scalar_tensor_tensor(out=rnd, in0=rank, scalar=float(CAP * m), in1=rnd, op0=ALU.is_ge, op1=ALU.add))
            link(dve.scalar_tensor_tensor(out=row, in0=rnd, scalar=-float(CAP), in1=rank, op0=ALU.mult, op1=ALU.add))
            link(dve.tensor_scalar(isj, rnd, 1.0, None, ALU.is_ge))
            tt(blk, stt_, rnd, ALU.add)
            link(dve.tensor_scalar(blk, blk, float(NE - 1), None, ALU.add))
            tt(blk, blk, e_id, ALU.subtract)
            tt(blk, blk, isj, ALU.mult)
            tt(blk, blk, e_id, ALU.add)
            link(dve.scalar_tensor_tensor(out=stt_, in0=blk, scalar=float(CAP), in1=row, op0=ALU.mult, op1=ALU.add))
            link(dve.tensor_copy(pos_i[:, :, :], stt_))
            for k in range(2):
                tt(OR[k], over_i(iota[:, 0:CAP], CAP), b3(row[:, k, :], CAP), ALU.is_equal)
                tt(AB[k], over_i(iota, NBLK), b3(blk[:, k, :], NBLK), ALU.is_equal)
                tt(AB[k], AB[k], b3(tokid, NBLK), ALU.mult)
            dve.nop().then_inc(sem("onehot_ready"), 1)
            e3 = end.rearrange("p (o e) -> p o e", o=1).broadcast_to([P, 16, NE])
            i3 = iota[:, 0:16].rearrange("p (b o) -> p b o", o=1).to_broadcast([P, 16, NE])
            bc = view(SC, 1024, "p (b e) -> p b e", b=16)
            tt(bc, e3, i3, ALU.is_le)
            red(be_f, bc)
            link(dve.tensor_scalar(be_f, be_f, float(NE - 1), None, ALU.min))
            link(dve.tensor_copy(over_e[:, 0:16], be_f))
            link(dve.tensor_copy(over_e[:, 16:17], end[:, NE - 1:NE]))
            dve.wait_ge(sem("idx_done"), 1)
            link(dve.tensor_copy(idx_pair[:, :], PS[:, 1, 0:NBLK // 2]))
            link(dve.tensor_copy(idx_over[:, :], PS[0:CAP, 2, 0:16]))
            dve.nop().then_inc(sem("tables_ready"), 1)

            def half_swiglu(i, buf, s, first):
                dve.wait_ge(sem("g_tanh" + s), i + 1)
                if not first:
                    dve.wait_ge(sem("h_turned" + s), i)
                ps = PS[:, 2 + buf, :]
                dve.scalar_tensor_tensor(out=gth[buf], in0=gth[buf], scalar=1.0, in1=ps[:, 0:256], op0=ALU.add,
                                         op1=ALU.mult).then_inc(sem("silu" + s), 1)
                dve.wait_ge(sem("silu" + s), i + 1)
                dve.scalar_tensor_tensor(out=hS[buf], in0=gth[buf], scalar=0.5, in1=ps[:, 256:512], op0=ALU.mult,
                                         op1=ALU.mult).then_inc(sem("h_ready" + s), 1)
                dve.wait_ge(sem("h_turned" + s), i + 1)
                if not first:
                    dve.wait_ge(sem("dn_used" + s), i)
                dve.tensor_copy(hT[buf].rearrange("p b g s -> p (b g s)"), PS[:, 4 + buf, 0:256]).then_inc(sem("hT_ready" + s), 1)

            def pair(i, first):
                dve.wait_ge(sem("rows_turned"), i + 1)
                if not first:
                    dve.wait_ge(sem("gu_used1"), i)
                dve.tensor_copy(xT.rearrange("p (a k) t -> p a (k t)", a=2), PS[:, 0:2, :]).then_inc(sem("xT_ready"), 1)
                for e in range(2):
                    half_swiglu(i, e, str(e), first)
            pair(0, True)
            with dve.Fori(1, NE // 2) as i:
                pair(i, False)
            flag = dve.value_load(over_e[0:1, 16:17], min_val=0, max_val=NX)
            with dve.If(flag > 0):
                dve.wait_ge(sem("gu_used1"), NE // 2)
                with dve.Fori(0, NX) as i:
                    dve.wait_ge(sem("rows_turned_over"), i + 1)
                    dve.tensor_copy(xT[:, :, 0:CAP].rearrange("p (a k) t -> p a k t", a=2),
                                    PS[:, 0:2, :].rearrange("p a (k t) -> p a k t", k=4)[:, :, :, 0:CAP]).then_inc(sem("xT_ready_over"), 1)
                    half_swiglu(i, 0, "_over", True)
            with dve.Else():
                dve.nop()
            for i in range(NT):
                for k in range(2):
                    dve.wait_ge(sem(f"y_back{2 * i + k}"), 16)
                    link(dve.scalar_tensor_tensor(out=xr[:, i, :], in0=yt[2 * i + k], scalar=wgt[k][:, i:i + 1], in1=xr[:, i, :],
                                                  op0=ALU.mult, op1=ALU.add))
                dve.nop().then_inc(sem("h_final"), 1)
            dve.wait_ge(sem("fg_loaded"), 16)
            for i in range(NT):
                rms(i, "ss3_ready", "ms3_ready")
                dve.wait_ge(sem("fin_scaled"), i + 1)
                dve.tensor_tensor(fin[i], fin[i], fgb, ALU.mult).then_inc(sem("fin_ready"), 1)


def kernel(**inputs):
    import concourse.bacc as bacc
    from concourse.bass_utils import run_bass_kernel_spmd

    a = {k: np.ascontiguousarray(v) for k, v in inputs.items()}
    row = lambda v: v.reshape(-1)
    rows = lambda v: v.reshape(-1, P)
    data = {
        "x": a["x"].reshape(T, D), "meta": a["meta"], "norm1_g": rows(a["norm1_g"]), "w_in": a["w_in"][0],
        "w_decay_up": a["w_decay_up"][0], "b_decay": rows(a["b_decay"]), "gla_norm_g": rows(a["gla_norm_g"]),
        "conv_w": a["conv_w"][0], "conv_b": rows(a["conv_b"]), "conv_ln_g": rows(a["conv_ln_g"]),
        "conv_ln_b": rows(a["conv_ln_b"]), "w_pw2": a["w_pw2"][0], "b_gate": rows(a["b_gate"]),
        "w_out": a["w_out"][0], "norm2_g": row(a["norm2_g"]), "w_rg": a["w_router_group"][0],
        "b_rg": row(a["b_router_group"]), "w_re": a["w_router_expert"][0], "b_re": row(a["b_router_expert"]),
        "w_eg": a["w_exp_gate"][0], "w_eu": a["w_exp_up"][0], "w_ed": a["w_exp_down"][0],
        "final_g": row(a["final_norm_g"]),
    }
    nc = bacc.Bacc("TRN2", target_bir_lowering=False, num_devices=1)
    aps = {n: nc.dram_tensor(n, v.shape, mybir.dt.from_np(v.dtype), kind="ExternalInput").ap() for n, v in data.items()}
    o = nc.dram_tensor("out", (T, D), FP, kind="ExternalOutput").ap()
    program(nc, out=o, **aps)
    r = run_bass_kernel_spmd(nc, [data], core_ids=[0])
    return r.results[0]["out"].reshape(1, T, D)
```

```python
import numpy as np
import concourse.bass as bass
from concourse import mybir
from contextlib import ExitStack

FP = mybir.dt.float32
I32 = mybir.dt.int32
U8 = mybir.dt.uint8

P = 128
D = 1024
KT = D // P
T = 512
META = 16
L = T + META
HALF = L // 2
NT = T // P
H, DK, DV = 4, 128, 256
TAPS = 31
EPS = 1e-6
TAU = 16.0
NG, EPG = 8, 8
NE = NG * EPG
DE = 512
CAP = 64
NX = T * 2 // CAP - 1
NBLK = NE + NX + 1
LEVELS = [64, 32, 16, 8, 4, 2, 1]

Q0, K0, V0, OG0, DL0, GV0, GG0, GA0, GB0 = 0, 512, 1024, 2048, 3072, 3088, 4112, 5136, 6160

R_N1, R_GLA, R_CB, R_LG, R_LB, R_BG, R_BD, R_END = 0, 8, 16, 24, 32, 40, 56, 60


def program(nc, x, meta, norm1_g, w_in, w_decay_up, b_decay, gla_norm_g, conv_w, conv_b, conv_ln_g,
            conv_ln_b, w_pw2, b_gate, w_out, norm2_g, w_rg, b_rg, w_re, b_re, w_eg, w_eu, w_ed,
            final_g, out):
    ALU = mybir.AluOpType
    ACT = mybir.ActivationFunctionType
    AX = mybir.AxisListType
    ctx = ExitStack()
    with ctx:
        sems = {}

        def sem(name):
            if name not in sems:
                sems[name] = ctx.enter_context(nc.semaphore(name))
            return sems[name]

        cst_i = ctx.enter_context(nc.sbuf_tensor("cst_i", [P, 2, P], I32))
        masks = ctx.enter_context(nc.sbuf_tensor("masks", [P, 8, P], U8))
        idx_pair = ctx.enter_context(nc.sbuf_tensor("idx_pair", [P, NBLK // 2], I32))
        idx_over = ctx.enter_context(nc.sbuf_tensor("idx_over", [CAP, 16], I32))
        idx_now = ctx.enter_context(nc.sbuf_tensor("idx_now", [P, 1], I32))
        pos_i = ctx.enter_context(nc.sbuf_tensor("pos_i", [P, 2, NT], I32))
        over_e = ctx.enter_context(nc.sbuf_tensor("over_e", [P, 17], I32))
        ARENA = 52000
        arena = ctx.enter_context(nc.sbuf_tensor("arena", [P, ARENA], FP))
        PS = ctx.enter_context(nc.psum_tensor("PS", [P, 8, 512], FP))
        y_d = nc.dram_tensor("y_rows", (NBLK * CAP, D), FP).ap()
        hn2_d = nc.dram_tensor("hn2_rows", (T, D), FP).ap()

        top = [0]

        def take(n):
            at = top[0]
            top[0] += n
            assert top[0] <= ARENA, top
            return at

        def view(at, n, pattern=None, parts=P, **kw):
            v = arena[0:parts, at:at + n]
            return v.rearrange(pattern, **kw) if pattern else v

        RING = take(3 * 4096)
        HNT = take(KT * L)
        UB = take(8 * 542)
        CV = take(8 * T)
        QF = take(H * T)
        KF = take(H * L)
        BF = take(H * L)
        VB = take(NT * D)
        VM = take(D)
        EB = take(6 * 512)
        SC = take(2 * 512)
        SB = take(D)
        QE = take(2 * 512)
        KD = take(512)
        OT = take(D)
        OSQ = take(D)
        RST = take(512)
        TH = take(2 * 512)
        GTB = take(8 * T)
        PRM = take(320)
        IDN = take(P)
        ONE = take(P)
        MEAN = take(P)
        LTM = take(P)
        SMALL = take(64)
        NHALF = take(1)
        ELAST = take(4 * 4)
        WDL = take(KT * 16)
        TOKID = take(4)
        IOTA = take(NBLK)

        ring = [view(RING + 4096 * s, 4096, "p (k c) -> p k c", k=KT) for s in range(3)]
        hnT = view(HNT, KT * L, "p (k t) -> p k t", k=KT)
        U = view(UB, 8 * 542, "p (k t) -> p k t", k=8)
        cv = view(CV, 8 * T, "p (k t) -> p k t", k=8)
        Qf = view(QF, H * T, "p (h t) -> p h t", h=H)
        Kf = view(KF, H * L, "p (h t) -> p h t", h=H)
        Bf = view(BF, H * L, "p (h t) -> p h t", h=H)
        V = view(VB, NT * D, "p (c v) -> p c v", c=NT)
        Vm = view(VM, D, parts=META)
        GT = view(GTB, 8 * T, "p (k t) -> p k t", k=8)
        E = [view(EB + 512 * i, 512, "p (h t) -> p h t", h=H) for i in range(6)]
        scT = [view(SC + 512 * i, 512, "p (h t) -> p h t", h=H) for i in range(2)]
        S = view(SB, D, "p (h v) -> p h v", h=H)
        qe = [view(QE + 512 * i, 512, "p (h t) -> p h t", h=H) for i in range(2)]
        kd = view(KD, 512, "p (h t) -> p h t", h=H)
        o_t = view(OT, D, "p (b t) -> p b t", b=8)
        o_sq = view(OSQ, D, "p (b t) -> p b t", b=8)
        conv_sum = view(OT + 512, 512)
        sq_sum = view(KD, 512)
        diag4 = view(RST, 512, "p (h t) -> p h t", h=H)
        th = [view(TH + 512 * i, 512) for i in range(2)]
        prm = view(PRM, 320)
        ident = view(IDN, P)
        ones = view(ONE, P)
        mean_w = view(MEAN, P)
        before = view(LTM, P)
        ss = view(SMALL, 8)
        rs = view(SMALL + 8, 8)
        nhalf = view(NHALF, 1)
        elast = [view(ELAST + 4 * i, 4, "p (h o) -> p h o", o=1) for i in range(4)]
        wdl = view(WDL, KT * 16, "p (k c) -> p k c", k=KT)
        tokid = view(TOKID, 4)
        iota = view(IOTA, NBLK)

        x0 = view(VB, NT * D, "p (i d) -> p i d", i=NT)
        xs = [view(GTB + D * i, D) for i in range(2)]
        xm = view(GTB + 2 * D, D, parts=META)
        prow = view(GTB + 3 * D, 3 * P, "p (a c) -> p a c", a=3)
        junk = view(KF, D)
        glu_t = [view(EB + 528 * i, 528) for i in range(4)]
        wup = view(OT, 512, parts=16)
        dlow = view(OSQ, L, parts=16)

        def cw(t, c):
            return prm[:, 8 * t + c:8 * t + c + 1]

        PB = TAPS * 8

        def par(row, c):
            return prm[:, PB + row + c:PB + row + c + 1]

        xr = view(QF, NT * D, "p (i d) -> p i d", i=NT)
        MID = BF + 8192
        hn2T = [view(MID + D * i, D, "p (k t) -> p k t", k=KT) for i in range(2)]
        assert MID + 2 * D <= SC
        hn2 = [view(SC + D * i, D) for i in range(2)]
        g2b = view(SC + 2 * D, D)
        wr = view(SC + 3 * D, KT * 72, "p (k c) -> p k c", k=KT)
        brb = view(SC + 3 * D + 576, 72)
        lg = view(SC + 3 * D + 648, NT * 72, "p (i c) -> p i c", i=NT)
        rt = [SC + 3 * D + 936]

        def arr(n, pattern=None, **kw):
            at = rt[0]
            rt[0] += n
            assert rt[0] <= GTB
            return view(at, n, pattern, **kw)

        squares = view(TH, D)

        oh = arr(32, "p (i g) -> p i g", i=NT)
        tb = arr(32, "p (i g) -> p i g", i=NT)
        eg = arr(32, "p (i g) -> p i g", i=NT)
        prod = arr(256, "p (i g e) -> p i g e", i=NT, g=NG)
        sel = arr(32, "p (i g) -> p i g", i=NT)
        sel2 = arr(32, "p (i g) -> p i g", i=NT)
        o12 = [arr(32, "p (i g) -> p i g", i=NT) for _ in range(2)]
        m4 = [arr(4) for _ in range(8)]
        gid = arr(4)
        wgt = [arr(4) for _ in range(2)]
        e_id = arr(8, "p (k i) -> p k i", k=2)
        rank = arr(8, "p (k i) -> p k i", k=2)
        rnd = arr(8, "p (k i) -> p k i", k=2)
        row = arr(8, "p (k i) -> p k i", k=2)
        stt_ = arr(8, "p (k i) -> p k i", k=2)
        isj = arr(8, "p (k i) -> p k i", k=2)
        blk = arr(8, "p (k i) -> p k i", k=2)
        A = [arr(256, "p (i e) -> p i e", i=NT) for _ in range(2)]
        Asum = arr(256, "p (i e) -> p i e", i=NT)
        Ccnt = arr(320, "p (i e) -> p i e", i=NT + 1)
        nx = arr(64)
        end = arr(64)
        start = arr(64)
        OR = [view(MID + 256 * k, 256, "p (i r) -> p i r", i=NT) for k in range(2)]
        AB = [view(MID + 512 + 4 * NBLK * k, 4 * NBLK, "p (i b) -> p i b", i=NT) for k in range(2)]
        ends = view(MID, 16 * NE, "p (b e) -> p b e", b=16)
        desc8 = arr(8)
        be_f = arr(16)
        ones64 = arr(64)
        assert rt[0] <= TH

        wgu = [view(b, 8192, "p (a k f) -> p a k f", k=KT, a=2) for b in (HNT, RING, BF)]
        wdn = [view(b, 4096, "p (j d) -> p j d", j=4) for b in (HNT + 8192, RING + 8192, GTB)]
        xg = hn2[0]
        xT = view(SC + D, D, "p (k t) -> p k t", k=KT)
        gth = [view(MID + 256 * i, 256) for i in range(2)]
        hS = [view(MID + 512 + 256 * i, 256) for i in range(2)]
        hT = [view(MID + 1024 + 256 * i, 256, "p (b g s) -> p b g s", b=2, g=2) for i in range(2)]
        ysb = [view(SC + 2 * D + 512 * i, 512) for i in range(2)]
        fgb = view(RING + 4096, D)
        yt = [view(HNT + D * i, D) for i in range(8)]
        fin = [view(RING + D * i, D) for i in range(NT)]

        win_c = w_in.rearrange("(k p) c -> p k c", p=P)
        chunks = []
        for j in range(4):
            chunks.append([(win_c[:, :, GV0 + 256 * j:GV0 + 256 * j + 256], 0, 256),
                           (win_c[:, :, GG0 + 256 * j:GG0 + 256 * j + 256], 256, 512)])
        for c0 in (K0, Q0, V0, V0 + 512, GA0, GA0 + 512, OG0, OG0 + 512, GB0, GB0 + 512):
            chunks.append([(win_c[:, :, c0:c0 + 512], 0, 512)])
        for w in (w_pw2, w_out):
            wv = w.rearrange("(k p) c -> p k c", p=P)
            for j in range(2):
                chunks.append([(wv[:, :, 512 * j:512 * j + 512], 0, 512)])
        C_K, C_Q, C_V, C_GATES, C_PW, C_OUT = 4, 5, 6, 8, 14, 16
        loaded = [0, 0, 0]
        chunk_at = []
        for n, parts in enumerate(chunks):
            loaded[n % 3] += 16 * len(parts)
            chunk_at.append(loaded[n % 3])

        chunk_end = [("pair_done", 4 * n + 4) for n in range(5)] + [("single_done", n) for n in (4, 9, 14)]
        chunk_end += [("single_done", 14 + 4 * n + 4) for n in range(10)]

        def conv_done(c):
            return 2 * TAPS * (c // 2 + 1) - 1 + c % 2

        def used(eng, n):
            eng.wait_ge(sem(chunk_end[n][0]), chunk_end[n][1])

        NLOOP = (NE // 2 - 2) // 3
        LAST0 = (NE - 1) // 3 + 1

        def turn(n0, j):
            return n0 % 3, 2 * j + n0 // 3 + 1

        tasks = [("kdm", 0), ("Sm", 0)]
        for c in range(NT):
            body = [("lv", c, i) for i in range(7)] + [("diag", c)]
            if c:
                body.insert(2, ("ss", c - 1))
                body.insert(5, ("bc", c - 1))
            if c < NT - 1:
                body.append(("kd", c))
            body.append(("o", c))
            if c < NT - 1:
                body.append(("S", c))
            tasks += body
        tasks += [("ss", NT - 1), ("bc", NT - 1)]
        e_tasks = [t for t in tasks if t[0] in ("kdm", "lv", "kd")]
        s_tasks = [t for t in tasks if t[0] in ("kdm", "lv", "diag", "kd", "ss", "bc")]
        a_tasks = [t for t in tasks if t[0] in ("Sm", "o", "S")]
        NSLOT = 24
        slots = [[] for _ in range(NSLOT)]
        left = list(tasks)
        for b in range(3, NSLOT):
            n = 2 if b < 9 else -(-len(left) // (NSLOT - b))
            for _ in range(min(n, len(left))):
                slots[b].append(left.pop(0))
        assert not left
        GA_BLOCKS, OG_BLOCKS = range(0, 8), range(8, 16)

        freed = []
        counts = {"sgl_act": 0, "sgl_dve": 0}

        def use(by):
            counts[by] += 1
            freed.append((by, counts[by]))
        for _ in range(4 + 10 + 8):
            use("sgl_act")
        for _ in range(8):
            use("sgl_dve")
        for _ in range(8):
            use("sgl_act")
        for _ in range(8 + 8):
            use("sgl_dve")

        def linker(eng, name):
            count = [0]
            s = sem(name)

            def link(ins):
                count[0] += 1
                ins.then_inc(s, 1)
                eng.wait_ge(s, count[0])
            return link

        block = ctx.enter_context(nc.Block())

        @block.sync
        def _(sp):
            for i in range(NT):
                sp.dma_start(x0[:, i, :], x[P * i:P * i + P, :]).then_inc(sem(f"x_loaded{i}"), 16)
            sp.dma_start(xm, meta).then_inc(sem("meta_loaded"), 16)
            cwr = conv_w.rearrange("t (c p) -> (t c) p", p=P)
            for dst, src in ((prow[:, 0, :], cwr[0:P]), (prow[0:120, 1, :], cwr[P:248]),
                             (prow[R_N1:R_N1 + 8, 2, :], norm1_g), (prow[R_GLA:R_GLA + 8, 2, :], gla_norm_g),
                             (prow[R_CB:R_CB + 8, 2, :], conv_b), (prow[R_LG:R_LG + 8, 2, :], conv_ln_g),
                             (prow[R_LB:R_LB + 8, 2, :], conv_ln_b), (prow[R_BG:R_BG + 16, 2, :], b_gate),
                             (prow[R_BD:R_BD + 4, 2, :], b_decay)):
                sp.dma_start(dst, src).then_inc(sem("prow_loaded"), 16)

            def chunk(n):
                for src, a, b in chunks[n]:
                    sp.dma_start(ring[n % 3][:, :, a:b], src).then_inc(sem(f"chunk_loaded{n % 3}"), 16)
            chunk(0)
            chunk(1)
            chunk(2)
            sp.dma_start(wdl, win_c[:, :, DL0:DL0 + 16]).then_inc(sem("wdl_loaded"), 16)
            sp.dma_start(wup, w_decay_up).then_inc(sem("wup_loaded"), 16)

            def gate_up_load(buf, e, s):
                for a, w in ((0, w_eg), (1, w_eu)):
                    sp.dma_start(wgu[buf][:, a, :, :], w[bass.ds(e, 1)].rearrange("o (p k) f -> p (o k) f", k=KT)).then_inc(sem("gu_loaded" + s), 16)

            def down_load(buf, e, s):
                sp.dma_start(wdn[buf], w_ed[bass.ds(e, 1)].rearrange("o (j p) d -> p (o j) d", p=P)).then_inc(sem("dn_loaded" + s), 16)
            for n in range(3, len(chunks)):
                used(sp, n - 3)
                chunk(n)
                if n == C_PW + 1:
                    sp.wait_ge(sem("attention_done"), 1)
                    sp.dma_start(xr, x.rearrange("(i p) d -> p i d", p=P)).then_inc(sem("xr_loaded"), 16)
                    sp.dma_start(g2b, norm2_g.partition_broadcast(P)).then_inc(sem("g2_loaded"), 16)
                    sp.dma_start(wr[:, :, 0:8], w_rg.rearrange("(k p) c -> p k c", p=P)).then_inc(sem("wr_loaded"), 16)
                    sp.dma_start(wr[:, :, 8:72], w_re.rearrange("(k p) c -> p k c", p=P)).then_inc(sem("wr_loaded"), 16)
                    sp.dma_start(brb[:, 0:8], b_rg.partition_broadcast(P)).then_inc(sem("wr_loaded"), 16)
                    sp.dma_start(brb[:, 8:72], b_re.partition_broadcast(P)).then_inc(sem("wr_loaded"), 16)
                    gate_up_load(2, 2, "2")

            used(sp, C_PW + 1)
            sp.wait_ge(sem("pw_used"), 1)
            gate_up_load(0, 0, "0")
            down_load(0, 0, "0")
            used(sp, len(chunks) - 1)
            gate_up_load(1, 1, "1")
            down_load(1, 1, "1")
            down_load(2, 2, "2")

            def expert(n0, j):
                b, _ = turn(n0, j)
                n = n0 + 6 * j
                sp.wait_ge(sem(f"gu_used{b}"), turn(n0 - 3, j)[1])
                gate_up_load(b, n, str(b))
                sp.wait_ge(sem(f"dn_used{b}"), turn(n0 - 3, j)[1])
                down_load(b, n, str(b))
            expert(3, 0)
            with sp.Fori(0, NLOOP) as j:
                for r in range(6):
                    expert(4 + r, j)
            sp.wait_ge(sem("tables_ready"), 1)
            flag = sp.value_load(over_e[0:1, 16:17], min_val=0, max_val=NX)
            with sp.If(flag > 0):
                sp.wait_ge(sem("gu_used0"), LAST0)
                sp.wait_ge(sem("dn_used0"), LAST0)
                with sp.Fori(0, NX) as i:
                    sp.wait_ge(sem("over_free"), i + 1)
                    e = sp.value_load(over_e[0:1, bass.ds(i, 1)], min_val=0, max_val=NE - 1)
                    gate_up_load(0, e, "_over")
                    down_load(0, e, "_over")
            with sp.Else():
                sp.nop()
            sp.wait_ge(sem("gu_used1"), (NE - 2) // 3 + 1)
            sp.dma_start(fgb, final_g.partition_broadcast(P)).then_inc(sem("fg_loaded"), 16)
            for i in range(NT):
                sp.wait_ge(sem("fin_ready"), i + 1)
                sp.dma_start(out[P * i:P * i + P, :], fin[i]).then_inc(sem("out_stored"), 16)
            sp.wait_ge(sem("out_stored"), 16 * NT)

        @block.tensor
        def _(pe):
            pe.wait_ge(sem("const_ready"), 5)
            pe.wait_ge(sem("prow_loaded"), 16 * 9)
            for a, (r0, n) in enumerate(((0, P), (P, 120), (PB, R_END))):
                t = pe.transpose(PS[:, 7, r0:r0 + n], prow[0:n, a, :], ident[0:n, 0:n])
            t.then_inc(sem("prm_turned"), 1)
            for i in range(NT):
                if i == NT - 1:
                    pe.wait_ge(sem("prm_ready"), 1)
                pe.wait_ge(sem("xs_ready"), i + 1)
                for k in range(KT):
                    t = pe.transpose(PS[:, 2 * i + k // 4, P * (k % 4):P * (k % 4) + P], xs[i % 2][:, P * k:P * k + P], ident)
                t.then_inc(sem("xT_done"), 1)
            pe.wait_ge(sem("xs_ready"), NT + 1)
            pe.wait_ge(sem("xT_taken"), 1)
            for k in range(KT):
                t = pe.transpose(PS[:, 0, META * k:META * k + META], xs[0][0:META, P * k:P * k + P], ident[0:META, 0:META])
            t.then_inc(sem("xT_done"), 1)
            pe.wait_ge(sem("xT_taken"), NT + 1)
            pair = [0]

            def next_pair():
                u = pair[0]
                pair[0] += 1
                if u >= 4:
                    pe.wait_ge(sem("pair_free"), u - 3)
                return 2 * (u % 4)

            def proj528(w, cols, rows=P):
                b = next_pair()
                for k in range(KT):
                    for hf in range(2):
                        t = pe.matmul(PS[0:rows, b + hf, 0:HALF], w[:, k, cols], hnT[:, k, HALF * hf:HALF * hf + HALF],
                                      start=(k == 0), stop=(k == KT - 1))
                t.then_inc(sem("pair_done"), 1)
                return t

            def chunk_ready(n):
                pe.wait_ge(sem(f"chunk_loaded{n % 3}"), chunk_at[n])
                return ring[n % 3]

            for n in range(4):
                w = chunk_ready(n)
                for c in range(2):
                    proj528(w, slice(P * c, P * c + P))
                    proj528(w, slice(256 + P * c, 256 + P * c + P))
            w = chunk_ready(C_K)
            for h in range(H):
                proj528(w, slice(P * h, P * h + P))
            pe.wait_ge(sem("wdl_loaded"), 16)
            proj528(wdl, slice(0, 16), rows=16)
            pe.wait_ge(sem("dlow_ready"), 1)
            pe.wait_ge(sem("wup_loaded"), 16)
            for h in range(H):
                b = next_pair()
                for hf in range(2):
                    t = pe.matmul(PS[:, b + hf, 0:HALF], wup[:, P * h:P * h + P], dlow[:, HALF * hf:HALF * hf + HALF],
                                  start=True, stop=True)
                t.then_inc(sem("pair_done"), 1)
            pe.wait_ge(sem("pair_free"), pair[0])

            single = [0]

            def next_single():
                u = single[0]
                single[0] += 1
                if u >= 4:
                    s, n = freed[u - 4]
                    pe.wait_ge(sem(s), n)
                return u % 4

            def proj512(w, c, moving):
                b = next_single()
                for k in range(KT):
                    t = pe.matmul(PS[:, b, :], w[:, k, P * c:P * c + P], moving[:, k, 0:T], start=(k == 0), stop=(k == KT - 1))
                t.then_inc(sem("single_done"), 1)
                return t

            w = chunk_ready(C_Q)
            for h in range(H):
                proj512(w, h, hnT)
            for j in range(2):
                w = chunk_ready(C_V + j)
                for i in range(NT + 1):
                    rows = P if i < NT else META
                    b = next_single()
                    for k in range(KT):
                        t = pe.matmul(PS[0:rows, b, :], hnT[:, k, P * i:P * i + rows], w[:, k, :], start=(k == 0), stop=(k == KT - 1))
                    t.then_inc(sem("single_done"), 1)
                if j == 0:
                    pe.wait_ge(sem("conv_summed"), 8)
                    pe.matmul(PS[:, 6, :], mean_w, conv_sum, start=True, stop=True).then_inc(sem("ln_mean"), 1)
            pe.wait_ge(sem("ln_sq_used"), 8)
            for i in range(NT):
                t = pe.matmul(PS[:, 7, i:i + 1], sq_sum[:, P * i:P * i + P], mean_w[:, 0:1], start=True, stop=True)
            t.then_inc(sem("ln_var"), 1)

            n_e, n_s, n_a = [0], [0], [0]

            def attend(t):
                kind, c = t[0], t[1]
                if kind in ("kdm", "lv", "diag", "kd", "ss", "bc"):
                    s = n_s[0]
                    n_s[0] += 1
                    bank = 4 + s % 2
                    if s >= 2:
                        pe.wait_ge(sem("score_taken"), s - 1)
                if kind in ("kdm", "lv", "kd"):
                    ei = n_e[0]
                    n_e[0] += 1
                    pe.wait_ge(sem("e_mul"), ei + 1)
                    ev = E[ei % 6]
                if kind == "kdm":
                    for h in range(H):
                        m = pe.transpose(PS[0:META, bank, P * h:P * h + P], ev[:, h, 0:META], ident)
                elif kind == "kd":
                    for h in range(H):
                        m = pe.transpose(PS[:, bank, P * h:P * h + P], ev[:, h, :], ident)
                elif kind == "lv":
                    for h in range(H):
                        m = pe.matmul(PS[:, bank, P * h:P * h + P], ev[:, h, :], ev[:, h, :], start=True, stop=True)
                elif kind == "diag":
                    for h in range(H):
                        m = pe.matmul(PS[:, bank, P * h:P * h + P], Kf[:, h, P * c:P * c + P], Qf[:, h, P * c:P * c + P],
                                      start=True, stop=True)
                elif kind == "ss":
                    pe.wait_ge(sem("o_sq"), c + 1)
                    for j in range(8):
                        m = pe.matmul(PS[:, bank, j // 2:j // 2 + 1], o_sq[:, j, :], ones[:, 0:1], start=(j % 2 == 0), stop=(j % 2 == 1))
                elif kind == "bc":
                    pe.wait_ge(sem("o_diag"), c + 1)
                    m = pe.matmul(PS[:, bank, :], ones, view(RST, 512), start=True, stop=True)
                if kind in ("kdm", "lv", "diag", "kd", "ss", "bc"):
                    m.then_inc(sem("score_done"), 1)
                    return
                a = n_a[0]
                n_a[0] += 1
                if a >= 1:
                    pe.wait_ge(sem("acc_taken"), a)
                pe.wait_ge(sem("score_taken"), n_s[0])
                if kind == "o":
                    pe.wait_ge(sem("qe_ready"), c + 1)
                    for h in range(H):
                        for vb in range(2):
                            j = 2 * h + vb
                            o = PS[:, 6 + j // 4, P * (j % 4):P * (j % 4) + P]
                            pe.matmul(o, S[:, h, P * vb:P * vb + P], qe[c % 2][:, h, :], start=True, stop=False)
                            m = pe.matmul(o, V[:, c, P * j:P * j + P], scT[c % 2][:, h, :], start=False, stop=True)
                else:
                    rows = META if kind == "Sm" else P
                    vs = Vm if kind == "Sm" else V[:, c, :]
                    for h in range(H):
                        m = pe.matmul(PS[:, 6 + h // 2, DV * (h % 2):DV * (h % 2) + DV], kd[0:rows, h, :], vs[0:rows, DV * h:DV * h + DV],
                                      start=True, stop=True)
                m.then_inc(sem("acc_done"), 1)

            for b in range(NSLOT):
                n = C_GATES + b // 4
                if b % 4 == 0:
                    w = chunk_ready(n)
                if b == 2:
                    pe.wait_ge(sem("ln_diag"), 1)
                    pe.matmul(PS[:, 7, :], ones, view(RST, 512), start=True, stop=True).then_inc(sem("ln_spread"), 1)
                proj512(w, b % 4, hnT)
                if b == 3:
                    pe.wait_ge(sem("ln_scaled"), 8)
                    pe.wait_ge(sem("sgl_act"), 14)
                for t_ in slots[b]:
                    attend(t_)
            pe.wait_ge(sem("u_final"), 8)
            for b in range(8):
                if b % 4 == 0:
                    w = chunk_ready(C_PW + b // 4)
                proj512(w, b % 4, cv)
            pe.wait_ge(sem("mix_ready"), 8)
            def out_half(i, j):
                w = chunk_ready(C_OUT + j)
                b = next_single()
                for k in range(KT):
                    t = pe.matmul(PS[:, b, :], GT[:, k, P * i:P * i + P], w[:, k, :], start=(k == 0), stop=(k == KT - 1))
                t.then_inc(sem("single_done"), 1)

            def turn_hn2(i):
                pe.wait_ge(sem("hn2_ready"), i + 1)
                if i >= 1:
                    pe.wait_ge(sem("hn2T_ready"), i)
                for k in range(KT):
                    t = pe.transpose(PS[:, 4 + k // 4, P * (k % 4):P * (k % 4) + P], hn2[i % 2][:, P * k:P * k + P], ident)
                t.then_inc(sem("hn2T_done"), 1)

            def logits(i):
                pe.wait_ge(sem("wr_loaded"), 64)
                pe.wait_ge(sem("hn2T_ready"), i + 1)
                if i >= 2:
                    pe.wait_ge(sem("logits_taken"), i - 1)
                for k in range(KT):
                    t = pe.matmul(PS[:, 6 + i % 2, 0:72], hn2T[i % 2][:, k, :], wr[:, k, :], start=(k == 0), stop=(k == KT - 1))
                t.then_inc(sem("logits_done"), 1)
            for i in range(NT):
                out_half(i, 0)
                if i >= 2:
                    logits(i - 2)
                out_half(i, 1)
                if i >= 1:
                    turn_hn2(i - 1)
            logits(NT - 2)
            turn_hn2(NT - 1)
            logits(NT - 1)
            pe.wait_ge(sem("choice_ready"), 1)
            for i in range(NT + 1):
                for j in range(min(i + 1, NT)):
                    t = pe.matmul(PS[:, 0, NE * i:NE * i + NE], before if j == i else ones, Asum[:, j, :],
                                  start=(j == 0), stop=(j == min(i, NT - 1)))
            t.then_inc(sem("ranks_done"), 1)
            pe.wait_ge(sem("onehot_ready"), 1)
            for g in range(2):
                for n in range(2 * NT):
                    t = pe.matmul(PS[CAP * g:CAP * g + CAP, 1, 0:NBLK // 2], OR[n // NT][:, n % NT, :],
                                  AB[n // NT][:, n % NT, g::2], start=(n == 0), stop=(n == 2 * NT - 1))
            for n in range(2 * NT):
                t = pe.matmul(PS[0:CAP, 2, 0:16], OR[n // NT][:, n % NT, :], AB[n // NT][:, n % NT, NE:NBLK],
                              start=(n == 0), stop=(n == 2 * NT - 1))
            t.then_inc(sem("idx_done"), 1)

            def turn_rows():
                xv = xg.rearrange("r (p k) -> r k p", k=KT)
                for k in range(KT):
                    t = pe.transpose(PS[:, k // 4, P * (k % 4):P * (k % 4) + P], xv[:, k, :], ident)
                return t

            def gate_up(buf, col0, bank):
                for k in range(KT):
                    for g in range(2):
                        t = pe.matmul(PS[CAP * g:CAP * g + CAP, bank, :].rearrange("p (a f) -> p a f", a=2),
                                      xT[:, k, col0:col0 + CAP], wgu[buf][:, :, k, 256 * g:256 * g + 256],
                                      start=(k == 0), stop=(k == KT - 1))
                return t

            def turn_h(e, bank):
                for b in range(2):
                    t = pe.transpose(PS[:, bank, P * b:P * b + P], hS[e][:, P * b:P * b + P], ident)
                return t

            def down(e, buf, bank):
                for j in range(4):
                    for g in range(2):
                        t = pe.matmul(PS[CAP * g:CAP * g + CAP, bank, :], hT[e][:, j % 2, j // 2, :],
                                      wdn[buf][:, j, 512 * g:512 * g + 512], start=(j == 0), stop=(j == 3))
                return t

            def pair_of_experts(i0, j):
                first = i0 == 0
                i = i0 + 3 * j
                pe.wait_ge(sem("rows_gathered"), 16 * (i + 1))
                if not first:
                    pe.wait_ge(sem("xT_ready"), i)
                turn_rows().then_inc(sem("rows_turned"), 1)
                pe.wait_ge(sem("xT_ready"), i + 1)
                for e in range(2):
                    b, nth = turn(2 * i0 + e, j)
                    pe.wait_ge(sem(f"gu_loaded{b}"), 32 * nth)
                    if not first:
                        pe.wait_ge(sem(f"h_ready{e}"), i)
                    gate_up(b, CAP * e, 2 + e).then_inc(sem(f"gu_used{b}"), 1)
                    pe.wait_ge(sem(f"h_ready{e}"), i + 1)
                    if not first:
                        pe.wait_ge(sem(f"hT_ready{e}"), i)
                    turn_h(e, 4 + e).then_inc(sem(f"h_turned{e}"), 1)
                    pe.wait_ge(sem(f"hT_ready{e}"), i + 1)
                    pe.wait_ge(sem(f"dn_loaded{b}"), 16 * nth)
                    if not first:
                        pe.wait_ge(sem(f"y_taken{e}"), i)
                    down(e, b, 6 + e).then_inc(sem(f"dn_used{b}"), 1)
            pair_of_experts(0, 0)
            pair_of_experts(1, 0)
            with pe.Fori(0, NLOOP) as j:
                for r in range(3):
                    pair_of_experts(2 + r, j)

            pe.wait_ge(sem("tables_ready"), 1)
            flag = pe.value_load(over_e[0:1, 16:17], min_val=0, max_val=NX)
            with pe.If(flag > 0):
                with pe.Fori(0, NX) as i:
                    pe.wait_ge(sem("rows_gathered_over"), 16 * (i + 1))
                    turn_rows().then_inc(sem("rows_turned_over"), 1)
                    pe.wait_ge(sem("xT_ready_over"), i + 1)
                    pe.wait_ge(sem("gu_loaded_over"), 32 * (i + 1))
                    gate_up(0, 0, 2).then_inc(sem("gu_used_over"), 1)
                    pe.wait_ge(sem("h_ready_over"), i + 1)
                    turn_h(0, 4).then_inc(sem("h_turned_over"), 1)
                    pe.wait_ge(sem("hT_ready_over"), i + 1)
                    pe.wait_ge(sem("dn_loaded_over"), 16 * (i + 1))
                    down(0, 0, 6).then_inc(sem("dn_used_over"), 1)
            with pe.Else():
                pe.nop()

        @block.scalar
        def _(act):
            link = linker(act, "act_order")
            def rows_of_x(i):
                return (x0[:, i, :], P) if i < NT else (xm, META)
            for i in range(NT + 2):
                if i <= NT:
                    src, n = rows_of_x(i)
                    act.wait_ge(sem(f"x_loaded{i}" if i < NT else "meta_loaded"), 16)
                    link(act.activation(junk[0:n, :], src, ACT.Square, accum_out=ss[0:n, i:i + 1]))
                    act.nop().then_inc(sem("ss_ready"), 1)
                if i == 0:
                    continue
                i -= 1
                src, n = rows_of_x(i)
                act.wait_ge(sem("rs_ready"), i + 1)
                if i >= 2:
                    act.wait_ge(sem("xT_done"), i - 1)
                act.activation(xs[i % 2][0:n, :], src, ACT.Copy, scale=rs[0:n, i:i + 1]).then_inc(sem("xs_ready"), 1)
            act.wait_ge(sem("prm_ready"), 1)
            u = 0

            def pair_view(u, rows=P):
                b = 2 * (u % 4)
                return PS[0:rows, b:b + 2, 0:HALF]

            def split(t):
                return t.rearrange("p (a t) -> p a t", a=2)
            for c in range(8):
                if c >= 2:
                    act.wait_ge(sem("u_ready"), c - 1)
                act.wait_ge(sem("pair_done"), u + 1)
                act.activation(split(glu_t[c % 2]), pair_view(u), ACT.Copy).then_inc(sem("pair_free"), 1)
                u += 1
                act.wait_ge(sem("pair_done"), u + 1)
                act.activation(split(glu_t[2 + c % 2]), pair_view(u), ACT.Tanh, scale=0.5).then_inc(sem("pair_free"), 1)
                u += 1
            for h in range(H):
                act.wait_ge(sem("pair_done"), u + 1)
                act.activation(split(Kf[:, h, :]), pair_view(u), ACT.Copy).then_inc(sem("pair_free"), 1)
                u += 1
            act.wait_ge(sem("pair_done"), u + 1)
            act.wait_ge(sem("u_ready"), 8)
            link(act.activation(split(dlow), pair_view(u, 16), ACT.Copy))
            act.nop().then_inc(sem("dlow_ready"), 1)
            act.nop().then_inc(sem("pair_free"), 1)
            u += 1
            for h in range(H):
                act.wait_ge(sem("pair_done"), u + 1)
                if h >= 2:
                    act.wait_ge(sem("decay_taken"), h - 1)
                act.activation(split(glu_t[h % 2]), pair_view(u), ACT.Relu, scale=-1.0, bias=par(R_BD, h))
                link(act.activation(split(glu_t[2 + h % 2]), pair_view(u), ACT.Abs, scale=-1.0, bias=par(R_BD, h)))
                act.nop().then_inc(sem("pair_free"), 1)
                u += 1
                link(act.activation(glu_t[2 + h % 2], glu_t[2 + h % 2], ACT.Exp, scale=-1.0))
                act.activation(glu_t[2 + h % 2], glu_t[2 + h % 2], ACT.Ln, bias=1.0).then_inc(sem("decay_logs"), 1)
            s = 0
            for h in range(H):
                act.wait_ge(sem("single_done"), s + 1)
                act.activation(Qf[:, h, :], PS[:, s % 4, :], ACT.Copy, scale=float(DK) ** -0.5).then_inc(sem("sgl_act"), 1)
                s += 1

            def values(j):
                nonlocal s
                for i in range(NT + 1):
                    act.wait_ge(sem("single_done"), s + 1)
                    n = P if i < NT else META
                    dst = V[:, i, 512 * j:512 * j + 512] if i < NT else Vm[:, 512 * j:512 * j + 512]
                    act.activation(dst, PS[0:n, s % 4, :], ACT.Copy).then_inc(sem("sgl_act"), 1)
                    s += 1
            values(0)
            for k in range(8):
                act.wait_ge(sem("ln_centred"), k + 1)
                if k >= 2:
                    act.wait_ge(sem("ln_sq_used"), k - 1)
                act.activation(th[k % 2], cv[:, k, :], ACT.Square).then_inc(sem("ln_sq"), 1)
            values(1)
            n_e = 0
            for b in range(NSLOT):
                if b == 2:
                    for k in range(8):
                        act.wait_ge(sem("ln_scaled"), k + 1)
                        if k >= 2:
                            act.wait_ge(sem("u_final"), k - 1)
                        act.activation(th[k % 2], cv[:, k, :], ACT.Tanh, scale=par(R_LG, k), bias=par(R_LB, k)).then_inc(sem("ln_tanh"), 1)
                for t in slots[b]:
                    if t[0] in ("kdm", "lv", "kd"):
                        act.wait_ge(sem("e_sub"), n_e + 1)
                        ev = E[n_e % 6]
                        if t[0] == "kdm":
                            ev = ev[:, :, 0:META]
                        act.activation(ev, ev, ACT.Exp, scale=-1.0 / TAU).then_inc(sem("e_exp"), 1)
                        n_e += 1
                    if t[0] == "lv" and t[2] == 0:
                        c = t[1]
                        if c == 0:
                            act.wait_ge(sem("over_zeroed"), 16 * ((NBLK - NE) * CAP // P))
                        if c >= 2:
                            act.wait_ge(sem("acc_done"), a_tasks.index(("o", c - 2)) + 1)
                        act.activation(elast[c], Bf[:, :, P * c + P - 1:P * c + P], ACT.Exp, scale=-1.0 / TAU)
                        act.activation(qe[c % 2], Bf[:, :, P * c:P * c + P], ACT.Exp, scale=-1.0 / TAU).then_inc(sem("qe_exp"), 1)
                act.wait_ge(sem("single_done"), s + 1)
                bank = PS[:, s % 4, :]
                s += 1
                if b in GA_BLOCKS:
                    act.activation(GT[:, b, :], bank, ACT.Tanh, scale=0.5, bias=par(R_BG, b)).then_inc(sem("sgl_act"), 1)
                elif b in OG_BLOCKS:
                    k = b - 8
                    if k >= 2:
                        act.wait_ge(sem("sgl_dve"), k - 1)
                    else:
                        act.wait_ge(sem("u_final"), 8)
                    act.activation(th[k % 2], bank, ACT.Tanh, scale=0.5).then_inc(sem("og_tanh"), 1)
                else:
                    if b == 16:
                        act.wait_ge(sem("conv_taps"), conv_done(7))
                    act.activation(U[:, b - 16, 0:T], bank, ACT.Tanh, scale=0.5, bias=par(R_BG, 8 + b - 16)).then_inc(sem("sgl_act"), 1)
            for i in range(NT):
                act.wait_ge(sem("h_ready"), i + 1)
                link(act.activation(squares, xr[:, i, :], ACT.Square, accum_out=ss[:, i:i + 1]))
                act.nop().then_inc(sem("ss2_ready"), 1)
            act.wait_ge(sem("group_diff"), 1)
            act.activation(eg, eg, ACT.Exp).then_inc(sem("group_exp"), 1)
            act.wait_ge(sem("choice_diff"), 1)
            act.activation(m4[3], m4[3], ACT.Exp).then_inc(sem("choice_exp"), 1)

            def expert(i0, e, j):
                i = i0 + 3 * j
                b, nth = turn(2 * i0 + e, j)
                act.wait_ge(sem(f"gu_used{b}"), nth)
                if i0:
                    act.wait_ge(sem(f"h_ready{e}"), i)
                act.activation(gth[e], PS[:, 2 + e, 0:256], ACT.Tanh, scale=0.5).then_inc(sem(f"g_tanh{e}"), 1)
                act.wait_ge(sem(f"dn_used{b}"), nth)
                if i0:
                    act.wait_ge(sem(f"y_stored{e}"), 32 * i)
                act.activation(ysb[e], PS[:, 6 + e, :], ACT.Copy).then_inc(sem(f"y_taken{e}"), 1)
                act.wait_ge(sem(f"y_taken{e}"), i + 1)
                for g in range(2):
                    act.dma_start(y_d[bass.ds((2 * i + e) * CAP, CAP), 512 * g:512 * g + 512],
                                  ysb[e][CAP * g:CAP * g + CAP, :]).then_inc(sem(f"y_stored{e}"), 16)
            act.wait_ge(sem("rows_gathered"), 16)
            for i0 in range(2):
                for e in range(2):
                    expert(i0, e, 0)
            with act.Fori(0, NLOOP) as j:
                for r in range(3):
                    for e in range(2):
                        expert(2 + r, e, j)
            act.wait_ge(sem("tables_ready"), 1)
            flag = act.value_load(over_e[0:1, 16:17], min_val=0, max_val=NX)
            with act.If(flag > 0):
                act.wait_ge(sem("y_stored0"), 16 * NE)
                act.nop().then_inc(sem("over_free"), 1)
                with act.Fori(0, NX) as i:
                    act.wait_ge(sem("gu_used_over"), i + 1)
                    act.activation(gth[0], PS[:, 2, 0:256], ACT.Tanh, scale=0.5).then_inc(sem("g_tanh_over"), 1)
                    act.wait_ge(sem("dn_used_over"), i + 1)
                    act.activation(ysb[0], PS[:, 6, :], ACT.Copy).then_inc(sem("y_taken_over"), 1)
                    act.wait_ge(sem("y_taken_over"), i + 1)
                    for g in range(2):
                        act.dma_start(y_d[bass.ds((i + NE) * CAP, CAP), 512 * g:512 * g + 512],
                                      ysb[0][CAP * g:CAP * g + CAP, :]).then_inc(sem("y_stored_over"), 16)
                    act.wait_ge(sem("y_stored_over"), 32 * (i + 1))
                    act.nop().then_inc(sem("over_free"), 1)
            with act.Else():
                act.nop()
            act.wait_ge(sem("y_stored0"), 16 * NE)
            act.wait_ge(sem("y_stored1"), 16 * NE)
            act.wait_ge(sem("over_zeroed"), 16 * ((NBLK - NE) * CAP // P))
            act.nop().then_inc(sem("y_all"), 1)
            for i in range(NT):
                act.wait_ge(sem("h_final"), i + 1)
                link(act.activation(fin[i], xr[:, i, :], ACT.Square, accum_out=ss[:, i:i + 1]))
                act.nop().then_inc(sem("ss3_ready"), 1)
                act.wait_ge(sem("rs3_ready"), i + 1)
                act.activation(fin[i], xr[:, i, :], ACT.Copy, scale=rs[:, i:i + 1]).then_inc(sem("fin_scaled"), 1)

        @block.gpsimd
        def _(pool):
            link = linker(pool, "pool_order")
            link(pool.memset(ident, 0.0))
            pool.affine_select(out=ident, in_=ident, compare_op=ALU.not_equal, fill=1.0, base=0,
                               pattern=[[-1, P]], channel_multiplier=1).then_inc(sem("const_ready"), 1)
            pool.memset(ones, 1.0).then_inc(sem("const_ready"), 1)
            pool.memset(mean_w, 1.0 / D).then_inc(sem("const_ready"), 1)
            link(pool.memset(before, 1.0))
            pool.affine_select(out=before, in_=before, compare_op=ALU.is_gt, fill=0.0, base=0,
                               pattern=[[1, P]], channel_multiplier=-1).then_inc(sem("const_ready"), 1)
            pool.iota(cst_i[:, 0, :], pattern=[[1, P]], base=0, channel_multiplier=0).then_inc(sem("iota_ready"), 1)
            pool.iota(cst_i[:, 1, :], pattern=[[0, P]], base=0, channel_multiplier=1).then_inc(sem("iota_ready"), 1)
            pool.iota(iota, pattern=[[1, NBLK]], base=0, channel_multiplier=0, allow_small_or_imprecise_dtypes=True)
            pool.iota(tokid, pattern=[[P, NT]], base=0, channel_multiplier=1, allow_small_or_imprecise_dtypes=True)
            pool.memset(U[:, :, 0:14], 0.0)
            pool.memset(nhalf, -0.5)
            pool.memset(view(QE, D), 0.0)
            pool.memset(scT[0], 0.0)
            pool.memset(scT[1], 0.0).then_inc(sem("const_ready"), 1)


            def rsqrt(v, wait, n, done, rows=P):
                pool.wait_ge(sem(wait), n)
                pool.tensor_tensor(v, v, nhalf[0:rows, :].to_broadcast([rows, v.shape[-1]]), ALU.pow).then_inc(sem(done), 1)
            for i in range(NT + 1):
                n = P if i < NT else META
                rsqrt(rs[0:n, i:i + 1], "ms_ready", i + 1, "rs_ready", n)
            for c in range(8):
                v, g = glu_t[c % 2], glu_t[2 + c % 2]
                pool.wait_ge(sem("pair_free"), 2 * c + 2)
                link(pool.tensor_tensor(g, g, v, ALU.mult))
                pool.tensor_tensor(U[:, c, 30:542], g[:, 0:T], v[:, 0:T], ALU.add)
                pool.tensor_tensor(U[:, c, 14:30], g[:, T:L], v[:, T:L], ALU.add).then_inc(sem("u_ready"), 1)
            pool.wait_ge(sem("const_ready"), 5)
            for j in range((NBLK - NE) * CAP // P):
                pool.dma_start(y_d[NE * CAP + P * j:NE * CAP + P * j + P, :], view(QE, D)).then_inc(sem("over_zeroed"), 16)
            for h in range(H):
                pool.wait_ge(sem("decay_logs"), h + 1)
                pool.tensor_tensor(Bf[:, h, :], glu_t[h % 2], glu_t[2 + h % 2], ALU.add).then_inc(sem("decay_taken"), 1)
            pool.wait_ge(sem("dlow_ready"), 1)
            for k in range(8):
                pool.wait_ge(sem("conv_taps"), conv_done(k))
                if k:
                    pool.wait_ge(sem("conv_summed"), k)
                m = pool.tensor_tensor(conv_sum, conv_sum, cv[:, k, :], ALU.add) if k else pool.tensor_copy(conv_sum, cv[:, 0, :])
                m.then_inc(sem("conv_summed"), 1)
            for k in range(8):
                pool.wait_ge(sem("ln_sq"), k + 1)
                if k:
                    pool.wait_ge(sem("ln_sq_used"), k)
                m = pool.tensor_tensor(sq_sum, sq_sum, th[k % 2], ALU.add) if k else pool.tensor_copy(sq_sum, th[0])
                m.then_inc(sem("ln_sq_used"), 1)
            rsqrt(rs[:, 0:NT], "ln_read", 2, "ln_rstd")
            n_e = 0
            for b in range(NSLOT):
                for t in slots[b]:
                    c = t[1]
                    if t[0] in ("kdm", "lv", "kd"):
                        ev = E[n_e % 6]
                        pool.wait_ge(sem("e_exp"), n_e + 1)
                        if t[0] == "kdm":
                            m = pool.tensor_tensor(ev[:, :, 0:META], ev[:, :, 0:META], Kf[:, :, T:L], ALU.mult)
                        elif t[0] == "kd":
                            m = pool.tensor_tensor(ev, ev, Kf[:, :, P * c:P * c + P], ALU.mult)
                        else:
                            w = LEVELS[t[2]]
                            e4 = ev.rearrange("p h (g a w) -> p h g a w", a=2, w=w)
                            k4 = Kf[:, :, P * c:P * c + P].rearrange("p h (g a w) -> p h g a w", a=2, w=w)
                            q4 = Qf[:, :, P * c:P * c + P].rearrange("p h (g a w) -> p h g a w", a=2, w=w)
                            pool.tensor_tensor(e4[:, :, :, 0, :], e4[:, :, :, 0, :], k4[:, :, :, 0, :], ALU.mult)
                            m = pool.tensor_tensor(e4[:, :, :, 1, :], e4[:, :, :, 1, :], q4[:, :, :, 1, :], ALU.mult)
                        m.then_inc(sem("e_mul"), 1)
                        n_e += 1
                    if t[0] == "lv" and t[2] == 0:
                        pool.wait_ge(sem("qe_exp"), c + 1)
                        pool.tensor_tensor(qe[c % 2], qe[c % 2], Qf[:, :, P * c:P * c + P], ALU.mult).then_inc(sem("qe_ready"), 1)
                    if t[0] == "o":
                        pool.wait_ge(sem("acc_taken"), a_tasks.index(t) + 1)
                        if c >= 1:
                            pool.wait_ge(sem("score_done"), s_tasks.index(("ss", c - 1)) + 1)
                        pool.tensor_tensor(o_sq, o_t, o_t, ALU.mult).then_inc(sem("o_sq"), 1)
                    if t[0] == "ss":
                        rsqrt(rs[:, 0:H], "score_taken", s_tasks.index(t) + 1, "o_rstd")
                if b in GA_BLOCKS:
                    pool.wait_ge(sem("sgl_act"), 14 + b + 1)
                    pool.tensor_scalar(GT[:, b, :], GT[:, b, :], 1.0, None, ALU.add).then_inc(sem("ga_ready"), 1)
            for i in range(NT):
                rsqrt(rs[:, i:i + 1], "ms2_ready", i + 1, "rs2_ready")
                pool.wait_ge(sem("hn2_ready"), i + 1)
                pool.dma_start(hn2_d[P * i:P * i + P, :], hn2[i % 2]).then_inc(sem(f"hn2_stored{i % 2}"), 16)

            def gather(nth, first):
                if not first:
                    pool.wait_ge(sem("rows_turned"), nth - 1)
                pool.tensor_copy(idx_now[:, :], idx_pair[:, bass.ds(nth - 1, 1)]).then_inc(sem("idx_now"), 1)
                pool.wait_ge(sem("tables_ready"), 1)
                pool.wait_ge(sem("idx_now"), nth)
                pool.indirect_dma_start(xg, None, hn2_d, bass.IndirectOffsetOnAxis(ap=idx_now[:, 0:1], axis=0)).then_inc(sem("rows_gathered"), 16)
            pool.wait_ge(sem("hn2_stored0"), 32)
            pool.wait_ge(sem("hn2_stored1"), 32)
            pool.wait_ge(sem("hn2T_done"), NT)
            pool.wait_ge(sem("tables_ready"), 1)
            gather(1, True)
            with pool.Fori(2, NE // 2 + 1) as nth:
                gather(nth, False)
            flag = pool.value_load(over_e[0:1, 16:17], min_val=0, max_val=NX)
            with pool.If(flag > 0):
                pool.wait_ge(sem("rows_turned"), NE // 2)
                pool.wait_ge(sem("gu_used0"), LAST0)
                with pool.Fori(0, NX) as i:
                    nth = i + 1
                    pool.wait_ge(sem("over_free"), nth)
                    pool.tensor_copy(idx_now[0:CAP, :], idx_over[:, bass.ds(i, 1)]).then_inc(sem("idx_now_over"), 1)
                    pool.wait_ge(sem("tables_ready"), 1)
                    pool.wait_ge(sem("idx_now_over"), nth)
                    pool.indirect_dma_start(xg[0:CAP, :], None, hn2_d, bass.IndirectOffsetOnAxis(ap=idx_now[0:CAP, 0:1], axis=0)).then_inc(sem("rows_gathered_over"), 16)
            with pool.Else():
                pool.nop()
            pool.wait_ge(sem("y_all"), 1)
            pool.wait_ge(sem("gu_used0"), LAST0)
            for i in range(NT):
                for k in range(2):
                    pool.indirect_dma_start(yt[2 * i + k], None, y_d, bass.IndirectOffsetOnAxis(ap=pos_i[:, k, i:i + 1], axis=0)).then_inc(sem(f"y_back{2 * i + k}"), 16)
            for i in range(NT):
                rsqrt(rs[:, i:i + 1], "ms3_ready", i + 1, "rs3_ready")

        @block.vector
        def _(dve):
            link = linker(dve, "dve_order")
            dve.wait_ge(sem("iota_ready"), 2)
            xi, xf = cst_i[:, 0, :], view(SB, P)
            link(dve.tensor_tensor(xi, cst_i[:, 0, :], cst_i[:, 1, :], ALU.bitwise_xor))
            link(dve.tensor_copy(xf, xi))
            dve.wait_ge(sem("const_ready"), 5)
            big = view(SB + P, P)
            link(dve.tensor_tensor(big, before, ident, ALU.add))
            link(dve.tensor_scalar(big, big, -1000.0, 1000.0, ALU.mult, ALU.add))
            link(dve.tensor_tensor(xf, xf, big, ALU.add))
            for n, w in enumerate(LEVELS + [0.5]):
                link(dve.tensor_scalar(masks[:, n, :], xf, float(2 * w), None, ALU.is_lt))
            for i in range(NT + 1):
                n = P if i < NT else META
                dve.wait_ge(sem("ss_ready"), i + 1)
                dve.tensor_scalar(rs[0:n, i:i + 1], ss[0:n, i:i + 1], 1.0 / D, EPS, ALU.mult, ALU.add).then_inc(sem("ms_ready"), 1)
            dve.wait_ge(sem("prm_turned"), 1)
            link(dve.tensor_copy(prm[:, 0:PB + R_END], PS[:, 7, 0:PB + R_END]))
            link(dve.tensor_scalar(prm[:, 0:PB], prm[:, 0:PB], 0.5, None, ALU.mult))
            link(dve.tensor_scalar(prm[:, PB + R_GLA:PB + R_GLA + 8], prm[:, PB + R_GLA:PB + R_GLA + 8], 0.25, None, ALU.mult))
            link(dve.tensor_scalar(prm[:, PB + R_LG:PB + R_BG + 16], prm[:, PB + R_LG:PB + R_BG + 16], 0.5, None, ALU.mult))
            link(dve.tensor_scalar(prm[:, PB + R_BD:PB + R_BD + 4], prm[:, PB + R_BD:PB + R_BD + 4], -1.0, None, ALU.mult))
            dve.nop().then_inc(sem("prm_ready"), 1)
            for i in range(NT + 1):
                dve.wait_ge(sem("xT_done"), i + 1)
                if i < NT:
                    for hf in range(2):
                        g = prm[:, PB + 4 * hf:PB + 4 * hf + 4].rearrange("p (k o) -> p k o", o=1)
                        m = dve.tensor_tensor(hnT[:, 4 * hf:4 * hf + 4, P * i:P * i + P],
                                              PS[:, 2 * i + hf, :].rearrange("p (k t) -> p k t", k=4),
                                              g.to_broadcast([P, 4, P]), ALU.mult)
                else:
                    g = prm[:, PB:PB + 8].rearrange("p (k o) -> p k o", o=1)
                    m = dve.tensor_tensor(hnT[:, :, T:L], PS[:, 0, 0:KT * META].rearrange("p (k t) -> p k t", k=KT),
                                          g.to_broadcast([P, KT, META]), ALU.mult)
                m.then_inc(sem("xT_taken"), 1)
            n = 0
            for c in range(0, 8, 2):
                dve.wait_ge(sem("u_ready"), c + 2)
                for t in range(TAPS):
                    for d in (c, c + 1):
                        if t:
                            dve.wait_ge(sem("conv_taps"), n - 1)
                            m = dve.scalar_tensor_tensor(out=cv[:, d, :], in0=U[:, d, t:t + T], scalar=cw(t, d), in1=cv[:, d, :],
                                                         op0=ALU.mult, op1=ALU.add)
                        else:
                            m = dve.tensor_scalar(cv[:, d, :], U[:, d, 0:T], cw(0, d), par(R_CB, d), ALU.mult, ALU.add)
                        m.then_inc(sem("conv_taps"), 1)
                        n += 1
            dve.wait_ge(sem("decay_taken"), H)
            for h in range(H):
                for c in range(NT + 1):
                    a, n = P * c, P if c < NT else META
                    m = dve.tensor_tensor_scan(Bf[:, h, a:a + n], ones[:, 0:n], Bf[:, h, a:a + n], 0.0, ALU.mult, ALU.add)
            link(m)
            dve.wait_ge(sem("ln_mean"), 1)
            for k in range(8):
                m = dve.tensor_tensor(cv[:, k, :], cv[:, k, :], PS[:, 6, :], ALU.subtract)
                m.then_inc(sem("ln_centred"), 1)
            dve.nop().then_inc(sem("ln_read"), 1)
            dve.wait_ge(sem("ln_var"), 1)
            dve.tensor_scalar(rs[:, 0:NT], PS[:, 7, 0:NT], EPS, None, ALU.add).then_inc(sem("ln_read"), 1)

            def diagonals(wait, n, done):
                dve.wait_ge(sem(wait), n)
                i4 = ident.rearrange("p (o t) -> p o t", o=1).broadcast_to([P, 4, P])
                r4 = rs[:, 0:4].rearrange("p (h o) -> p h o", o=1).to_broadcast([P, 4, P])
                dve.tensor_tensor(diag4, i4, r4, ALU.mult).then_inc(sem(done), 1)
            diagonals("ln_rstd", 1, "ln_diag")
            dve.wait_ge(sem("ln_spread"), 1)
            for k in range(8):
                dve.tensor_tensor(cv[:, k, :], cv[:, k, :], PS[:, 7, :], ALU.mult).then_inc(sem("ln_scaled"), 1)
            for k in range(8):
                dve.wait_ge(sem("ln_tanh"), k + 1)
                link(dve.tensor_scalar(cv[:, k, :], cv[:, k, :], par(R_LG, k), par(R_LB, k), ALU.mult, ALU.add))
                dve.scalar_tensor_tensor(out=cv[:, k, :], in0=th[k % 2], scalar=1.0, in1=cv[:, k, :],
                                         op0=ALU.add, op1=ALU.mult).then_inc(sem("u_final"), 1)

            n_e, n_s, n_a = [0], [0], [0]

            def differences(t):
                c = t[1]
                ei = n_e[0]
                n_e[0] += 1
                if ei >= 6:
                    dve.wait_ge(sem("score_done"), s_tasks.index(e_tasks[ei - 6]) + 1)
                ev = E[ei % 6]
                if t[0] in ("kdm", "kd"):
                    a, n = (T, META) if t[0] == "kdm" else (P * c, P)
                    m = dve.tensor_tensor(ev[:, :, 0:n], Bf[:, :, a + n - 1:a + n].to_broadcast([P, H, n]), Bf[:, :, a:a + n], ALU.subtract)
                else:
                    w = LEVELS[t[2]]
                    e4 = ev.rearrange("p h (g a w) -> p h g a w", a=2, w=w)
                    b4 = Bf[:, :, P * c:P * c + P].rearrange("p h (g a w) -> p h g a w", a=2, w=w)
                    ref = b4[:, :, :, 0, w - 1:w].to_broadcast([P, H, 64 // w, w])
                    dve.tensor_tensor(e4[:, :, :, 0, :], ref, b4[:, :, :, 0, :], ALU.subtract)
                    m = dve.tensor_tensor(e4[:, :, :, 1, :], b4[:, :, :, 1, :], ref, ALU.subtract)
                m.then_inc(sem("e_sub"), 1)

            def take(t):
                kind, c = t[0], t[1]
                if kind in ("kdm", "lv", "diag", "kd", "ss", "bc"):
                    s = n_s[0]
                    n_s[0] += 1
                    bank = PS[:, 4 + s % 2, :].rearrange("p (h t) -> p h t", h=H)
                    dve.wait_ge(sem("score_done"), s + 1)
                    if kind in ("lv", "diag"):
                        lv = t[2] if kind == "lv" else 7
                        mk = masks[:, lv, :].rearrange("p (o t) -> p o t", o=1).broadcast_to([P, H, P])
                        if lv == 0 and c >= 2:
                            dve.wait_ge(sem("acc_done"), a_tasks.index(("o", c - 2)) + 1)
                        dve.copy_predicated(scT[c % 2], mk, bank).then_inc(sem("score_taken"), 1)
                        dve.wait_ge(sem("score_taken"), s + 1)
                    elif kind == "ss":
                        dve.tensor_scalar(rs[:, 0:H], PS[:, 4 + s % 2, 0:H], 1.0 / DV, EPS, ALU.mult, ALU.add).then_inc(sem("score_taken"), 1)
                        diagonals("o_rstd", c + 1, "o_diag")
                    elif kind == "bc":
                        o4 = o_t.rearrange("p (h b) t -> p h b t", h=H)
                        r4 = PS[:, 4 + s % 2, :].rearrange("p (h o t) -> p h o t", h=H, o=1).broadcast_to([P, H, 2, P])
                        dve.tensor_tensor(o4, o4, r4, ALU.mult).then_inc(sem("score_taken"), 1)
                        dve.wait_ge(sem("score_taken"), s + 1)
                        g = prm[:, PB + R_GLA:PB + R_GLA + 8].rearrange("p (k o) -> p k o", o=1).to_broadcast([P, 8, P])
                        link(dve.tensor_tensor(o_t, o_t, g, ALU.mult))
                        gt = GT[:, :, P * c:P * c + P]
                        dve.wait_ge(sem("ga_ready"), 8)
                        m = dve.tensor_tensor(gt, gt, o_t, ALU.mult)
                        link(m)
                        if c == NT - 1:
                            dve.nop().then_inc(sem("attention_done"), 1)
                    else:
                        rows = META if kind == "kdm" else P
                        if kind == "kd" and c >= 0:
                            dve.wait_ge(sem("acc_done"), a_tasks.index(("S", c - 1) if c else ("Sm", 0)) + 1)
                        dve.tensor_copy(kd[0:rows], bank[0:rows]).then_inc(sem("score_taken"), 1)
                    return
                a = n_a[0]
                n_a[0] += 1
                dve.wait_ge(sem("acc_done"), a + 1)
                pair = PS[:, 6:8, :]
                if kind == "o":
                    m = dve.tensor_copy(o_t.rearrange("p (a b) t -> p a (b t)", a=2), pair)
                elif kind == "Sm":
                    m = dve.tensor_copy(S.rearrange("p (a h) v -> p a (h v)", a=2), pair)
                else:
                    for h in range(H):
                        m = dve.scalar_tensor_tensor(out=S[:, h, :], in0=S[:, h, :], scalar=elast[c][:, h, :],
                                                     in1=PS[:, 6 + h // 2, DV * (h % 2):DV * (h % 2) + DV], op0=ALU.mult, op1=ALU.add)
                m.then_inc(sem("acc_taken"), 1)
                dve.wait_ge(sem("acc_taken"), a + 1)

            s = 14
            og = 0
            for b in range(NSLOT + 1):
                if b < NSLOT:
                    for t in slots[b]:
                        if t[0] in ("kdm", "lv", "kd"):
                            differences(t)
                if b >= 1:
                    for t in slots[b - 1]:
                        take(t)
                    if b - 1 in OG_BLOCKS:
                        k = b - 1 - 8
                        bank = PS[:, (14 + b - 1) % 4, :]
                        dve.wait_ge(sem("og_tanh"), k + 1)
                        dve.wait_ge(sem("ga_ready"), 8)
                        link(dve.scalar_tensor_tensor(out=th[k % 2], in0=th[k % 2], scalar=1.0, in1=bank, op0=ALU.add, op1=ALU.mult))
                        link(dve.tensor_tensor(GT[:, k, :], GT[:, k, :], th[k % 2], ALU.mult))
                        dve.nop().then_inc(sem("sgl_dve"), 1)
            u = 38
            for k in range(8):
                dve.wait_ge(sem("single_done"), u + 1)
                bank = PS[:, u % 4, :]
                u += 1
                dve.wait_ge(sem("sgl_act"), 14 + 8 + k + 1)
                link(dve.scalar_tensor_tensor(out=th[k % 2], in0=U[:, k, 0:T], scalar=1.0, in1=bank, op0=ALU.add, op1=ALU.mult))
                dve.nop().then_inc(sem("sgl_dve"), 1)
                link(dve.scalar_tensor_tensor(out=GT[:, k, :], in0=th[k % 2], scalar=0.5, in1=GT[:, k, :], op0=ALU.mult, op1=ALU.add))
                dve.nop().then_inc(sem("mix_ready"), 1)
            dve.nop().then_inc(sem("pw_used"), 1)
            dve.wait_ge(sem("xr_loaded"), 16)
            def rms(i, a, b):
                dve.wait_ge(sem(a), i + 1)
                dve.tensor_scalar(rs[:, i:i + 1], ss[:, i:i + 1], 1.0 / D, EPS, ALU.mult, ALU.add).then_inc(sem(b), 1)

            def add_half(i, j):
                nonlocal u
                dve.wait_ge(sem("single_done"), u + 1)
                hv = xr[:, i, 512 * j:512 * j + 512]
                dve.tensor_tensor(hv, hv, PS[:, u % 4, :], ALU.add).then_inc(sem("sgl_dve"), 1)
                u += 1

            def norm2(i):
                rms(i, "ss2_ready", "ms2_ready")
                dve.wait_ge(sem("g2_loaded"), 16)
                if i >= 2:
                    dve.wait_ge(sem(f"hn2_stored{i % 2}"), 16)
                    dve.wait_ge(sem("hn2T_done"), i - 1)
                dve.wait_ge(sem("rs2_ready"), i + 1)
                dve.scalar_tensor_tensor(out=hn2[i % 2], in0=xr[:, i, :], scalar=rs[:, i:i + 1], in1=g2b,
                                         op0=ALU.mult, op1=ALU.mult).then_inc(sem("hn2_ready"), 1)

            def take_hn2T(i):
                dve.wait_ge(sem("hn2T_done"), i + 1)
                if i >= 2:
                    dve.wait_ge(sem("logits_done"), i - 1)
                dve.tensor_copy(hn2T[i % 2].rearrange("p (a k) t -> p a (k t)", a=2), PS[:, 4:6, :]).then_inc(sem("hn2T_ready"), 1)

            def take_logits(i):
                dve.wait_ge(sem("logits_done"), i + 1)
                dve.tensor_tensor(lg[:, i, :], PS[:, 6 + i % 2, 0:72], brb, ALU.add).then_inc(sem("logits_taken"), 1)
            dve.wait_ge(sem("wr_loaded"), 64)
            for i in range(NT):
                add_half(i, 0)
                if i >= 2:
                    take_logits(i - 2)
                add_half(i, 1)
                dve.wait_ge(sem("sgl_dve"), 16 + 2 * i + 2)
                dve.nop().then_inc(sem("h_ready"), 1)
                norm2(i)
                if i >= 1:
                    take_hn2T(i - 1)
            take_logits(NT - 2)
            take_hn2T(NT - 1)
            take_logits(NT - 1)
            dve.wait_ge(sem("logits_taken"), NT)
            used(dve, len(chunks) - 1)

            def tt(o, a, b, op):
                link(dve.tensor_tensor(o, a, b, op))

            def red(o, a, op=ALU.add):
                link(dve.tensor_reduce(o, a, AX.X, op))

            def b3(v, n):
                return v.rearrange("p (i o) -> p i o", o=1).to_broadcast([P, NT, n])

            def over_i(v, n):
                return v.rearrange("p (o n) -> p o n", o=1).broadcast_to([P, NT, n])
            io8 = over_i(iota[:, 0:8], 8)
            link(dve.tensor_scalar(desc8, iota[:, 0:8], -1.0, 8.0, ALU.mult, ALU.add))
            link(dve.memset(ones64, 1.0))

            def first_max(one, vals, mx):
                red(mx, vals, ALU.max)
                tt(one, vals, b3(mx, 8), ALU.is_equal)
                tt(tb, one, over_i(desc8, 8), ALU.mult)
                red(m4[7], tb, ALU.max)
                tt(one, tb, b3(m4[7], 8), ALU.is_equal)
            lgg = lg[:, :, 0:8]
            first_max(oh, lgg, m4[0])
            dve.tensor_tensor(eg, lgg, b3(m4[0], 8), ALU.subtract).then_inc(sem("group_diff"), 1)
            lge = lg[:, :, 8:72].rearrange("p i (g e) -> p i g e", g=NG)
            tt(prod, lge, oh.rearrange("p i (g o) -> p i g o", o=1).to_broadcast([P, NT, NG, EPG]), ALU.mult)
            red(sel, prod.rearrange("p i g e -> p i e g"))
            first_max(o12[0], sel, m4[1])
            link(dve.scalar_tensor_tensor(out=sel2, in0=o12[0], scalar=-3e38, in1=sel, op0=ALU.mult, op1=ALU.add))
            first_max(o12[1], sel2, m4[2])
            dve.tensor_tensor(m4[3], m4[2], m4[1], ALU.subtract).then_inc(sem("choice_diff"), 1)
            tt(tb, oh, io8, ALU.mult)
            red(gid, tb)
            for k in range(2):
                tt(tb, o12[k], io8, ALU.mult)
                red(e_id[:, k, :], tb)
                link(dve.scalar_tensor_tensor(out=e_id[:, k, :], in0=gid, scalar=float(EPG), in1=e_id[:, k, :], op0=ALU.mult, op1=ALU.add))
                tt(A[k], over_i(iota[:, 0:NE], NE), b3(e_id[:, k, :], NE), ALU.is_equal)
            tt(Asum, A[0], A[1], ALU.add)
            dve.nop().then_inc(sem("choice_ready"), 1)
            dve.wait_ge(sem("group_exp"), 1)
            red(m4[4], eg)
            dve.wait_ge(sem("choice_exp"), 1)
            link(dve.tensor_scalar(m4[5], m4[3], 1.0, None, ALU.add))
            tt(m4[4], m4[4], m4[5], ALU.mult)
            link(dve.reciprocal(wgt[0], m4[4]))
            tt(wgt[1], wgt[0], m4[3], ALU.mult)
            dve.wait_ge(sem("ranks_done"), 1)
            link(dve.tensor_copy(Ccnt, PS[:, 0, 0:320].rearrange("p (i e) -> p i e", i=NT + 1)))
            link(dve.memset(nx, 0.0))
            for m in range(1, T // CAP):
                link(dve.scalar_tensor_tensor(out=nx, in0=Ccnt[:, NT, :], scalar=float(CAP * m), in1=nx, op0=ALU.is_gt, op1=ALU.add))
            link(dve.tensor_tensor_scan(end, ones64, nx, 0.0, ALU.mult, ALU.add))
            tt(start, end, nx, ALU.subtract)
            big3 = prod.rearrange("p i g e -> p i (g e)")
            for k in range(2):
                tt(big3, A[k], Ccnt[:, 0:NT, :], ALU.mult)
                red(rank[:, k, :], big3)
                tt(big3, A[k], over_i(start, NE), ALU.mult)
                red(stt_[:, k, :], big3)
            link(dve.memset(rnd, 0.0))
            for m in range(1, T // CAP):
                link(dve.scalar_tensor_tensor(out=rnd, in0=rank, scalar=float(CAP * m), in1=rnd, op0=ALU.is_ge, op1=ALU.add))
            link(dve.scalar_tensor_tensor(out=row, in0=rnd, scalar=-float(CAP), in1=rank, op0=ALU.mult, op1=ALU.add))
            link(dve.tensor_scalar(isj, rnd, 1.0, None, ALU.is_ge))
            tt(blk, stt_, rnd, ALU.add)
            link(dve.tensor_scalar(blk, blk, float(NE - 1), None, ALU.add))
            tt(blk, blk, e_id, ALU.subtract)
            tt(blk, blk, isj, ALU.mult)
            tt(blk, blk, e_id, ALU.add)
            link(dve.scalar_tensor_tensor(out=stt_, in0=blk, scalar=float(CAP), in1=row, op0=ALU.mult, op1=ALU.add))
            link(dve.tensor_copy(pos_i[:, :, :], stt_))
            e3 = end.rearrange("p (o e) -> p o e", o=1).broadcast_to([P, 16, NE])
            i3 = iota[:, 0:16].rearrange("p (b o) -> p b o", o=1).to_broadcast([P, 16, NE])
            tt(ends, e3, i3, ALU.is_le)
            red(be_f, ends)
            link(dve.tensor_scalar(be_f, be_f, float(NE - 1), None, ALU.min))
            link(dve.tensor_copy(over_e[:, 0:16], be_f))
            link(dve.tensor_copy(over_e[:, 16:17], end[:, NE - 1:NE]))
            for k in range(2):
                tt(OR[k], over_i(iota[:, 0:CAP], CAP), b3(row[:, k, :], CAP), ALU.is_equal)
                tt(AB[k], over_i(iota, NBLK), b3(blk[:, k, :], NBLK), ALU.is_equal)
                tt(AB[k], AB[k], b3(tokid, NBLK), ALU.mult)
            dve.nop().then_inc(sem("onehot_ready"), 1)
            dve.wait_ge(sem("idx_done"), 1)
            link(dve.tensor_copy(idx_pair[:, :], PS[:, 1, 0:NBLK // 2]))
            link(dve.tensor_copy(idx_over[:, :], PS[0:CAP, 2, 0:16]))
            dve.nop().then_inc(sem("tables_ready"), 1)

            def half_swiglu(i, e, s, freed):
                dve.wait_ge(sem("g_tanh" + s), i + 1)
                if freed:
                    dve.wait_ge(sem("h_turned" + s), i)
                ps = PS[:, 2 + e, :]
                dve.scalar_tensor_tensor(out=gth[e], in0=gth[e], scalar=1.0, in1=ps[:, 0:256], op0=ALU.add,
                                         op1=ALU.mult).then_inc(sem("silu" + s), 1)
                dve.wait_ge(sem("silu" + s), i + 1)
                dve.scalar_tensor_tensor(out=hS[e], in0=gth[e], scalar=0.5, in1=ps[:, 256:512], op0=ALU.mult,
                                         op1=ALU.mult).then_inc(sem("h_ready" + s), 1)
                dve.wait_ge(sem("h_turned" + s), i + 1)
                if freed:
                    dve.wait_ge(sem(freed[0]), freed[1])
                dve.tensor_copy(hT[e].rearrange("p b g s -> p (b g s)"), PS[:, 4 + e, 0:256]).then_inc(sem("hT_ready" + s), 1)

            def pair(i0, j):
                i = i0 + 3 * j
                dve.wait_ge(sem("rows_turned"), i + 1)
                if i0:
                    b, nth = turn(2 * i0 - 1, j)
                    dve.wait_ge(sem(f"gu_used{b}"), nth)
                dve.tensor_copy(xT.rearrange("p (a k) t -> p a (k t)", a=2), PS[:, 0:2, :]).then_inc(sem("xT_ready"), 1)
                for e in range(2):
                    freed = None
                    if i0:
                        b, nth = turn(2 * i0 + e - 2, j)
                        freed = (f"dn_used{b}", nth)
                    half_swiglu(i, e, str(e), freed)
            pair(0, 0)
            pair(1, 0)
            with dve.Fori(0, NLOOP) as j:
                for r in range(3):
                    pair(2 + r, j)
            flag = dve.value_load(over_e[0:1, 16:17], min_val=0, max_val=NX)
            with dve.If(flag > 0):
                dve.wait_ge(sem("gu_used0"), LAST0)
                with dve.Fori(0, NX) as i:
                    dve.wait_ge(sem("rows_turned_over"), i + 1)
                    dve.tensor_copy(xT[:, :, 0:CAP].rearrange("p (a k) t -> p a k t", a=2),
                                    PS[:, 0:2, :].rearrange("p a (k t) -> p a k t", k=4)[:, :, :, 0:CAP]).then_inc(sem("xT_ready_over"), 1)
                    half_swiglu(i, 0, "_over", None)
            with dve.Else():
                dve.nop()
            for i in range(NT):
                for k in range(2):
                    dve.wait_ge(sem(f"y_back{2 * i + k}"), 16)
                    link(dve.scalar_tensor_tensor(out=xr[:, i, :], in0=yt[2 * i + k], scalar=wgt[k][:, i:i + 1], in1=xr[:, i, :],
                                                  op0=ALU.mult, op1=ALU.add))
                dve.nop().then_inc(sem("h_final"), 1)
            dve.wait_ge(sem("fg_loaded"), 16)
            for i in range(NT):
                rms(i, "ss3_ready", "ms3_ready")
                dve.wait_ge(sem("fin_scaled"), i + 1)
                dve.tensor_tensor(fin[i], fin[i], fgb, ALU.mult).then_inc(sem("fin_ready"), 1)


def kernel(**inputs):
    import concourse.bacc as bacc
    from concourse.bass_utils import run_bass_kernel_spmd

    a = {k: np.ascontiguousarray(v) for k, v in inputs.items()}
    row = lambda v: v.reshape(-1)
    rows = lambda v: v.reshape(-1, P)
    data = {
        "x": a["x"].reshape(T, D), "meta": a["meta"], "norm1_g": rows(a["norm1_g"]), "w_in": a["w_in"][0],
        "w_decay_up": a["w_decay_up"][0], "b_decay": rows(a["b_decay"]), "gla_norm_g": rows(a["gla_norm_g"]),
        "conv_w": a["conv_w"][0], "conv_b": rows(a["conv_b"]), "conv_ln_g": rows(a["conv_ln_g"]),
        "conv_ln_b": rows(a["conv_ln_b"]), "w_pw2": a["w_pw2"][0], "b_gate": rows(a["b_gate"]),
        "w_out": a["w_out"][0], "norm2_g": row(a["norm2_g"]), "w_rg": a["w_router_group"][0],
        "b_rg": row(a["b_router_group"]), "w_re": a["w_router_expert"][0], "b_re": row(a["b_router_expert"]),
        "w_eg": a["w_exp_gate"][0], "w_eu": a["w_exp_up"][0], "w_ed": a["w_exp_down"][0],
        "final_g": row(a["final_norm_g"]),
    }
    nc = bacc.Bacc("TRN2", target_bir_lowering=False, num_devices=1)
    aps = {n: nc.dram_tensor(n, v.shape, mybir.dt.from_np(v.dtype), kind="ExternalInput").ap() for n, v in data.items()}
    o = nc.dram_tensor("out", (T, D), FP, kind="ExternalOutput").ap()
    program(nc, out=o, **aps)
    r = run_bass_kernel_spmd(nc, [data], core_ids=[0])
    return r.results[0]["out"].reshape(1, T, D)
```

```python
import numpy as np
import concourse.bass as bass
from concourse import mybir
from contextlib import ExitStack

FP = mybir.dt.float32
I32 = mybir.dt.int32
U8 = mybir.dt.uint8

P = 128
D = 1024
KT = D // P
T = 512
META = 16
L = T + META
HALF = L // 2
NT = T // P
H, DK, DV = 4, 128, 256
TAPS = 31
EPS = 1e-6
TAU = 16.0
NG, EPG = 8, 8
NE = NG * EPG
DE = 512
CAP = 64
NX = T * 2 // CAP - 1
NBLK = NE + NX + 1
LEVELS = [64, 32, 16, 8, 4, 2, 1]

Q0, K0, V0, OG0, DL0, GV0, GG0, GA0, GB0 = 0, 512, 1024, 2048, 3072, 3088, 4112, 5136, 6160

R_N1, R_GLA, R_CB, R_LG, R_LB, R_BG, R_BD, R_END = 0, 8, 16, 24, 32, 40, 56, 60


def program(nc, x, meta, norm1_g, w_in, w_decay_up, b_decay, gla_norm_g, conv_w, conv_b, conv_ln_g,
            conv_ln_b, w_pw2, b_gate, w_out, norm2_g, w_rg, b_rg, w_re, b_re, w_eg, w_eu, w_ed,
            final_g, out):
    ALU = mybir.AluOpType
    ACT = mybir.ActivationFunctionType
    AX = mybir.AxisListType
    ctx = ExitStack()
    with ctx:
        sems = {}

        def sem(name):
            if name not in sems:
                sems[name] = ctx.enter_context(nc.semaphore(name))
            return sems[name]

        cst_i = ctx.enter_context(nc.sbuf_tensor("cst_i", [P, 2, P], I32))
        masks = ctx.enter_context(nc.sbuf_tensor("masks", [P, 8, P], U8))
        idx_pair = ctx.enter_context(nc.sbuf_tensor("idx_pair", [P, NE // 2], I32))
        idx_over = ctx.enter_context(nc.sbuf_tensor("idx_over", [CAP, 16], I32))
        idx_now = ctx.enter_context(nc.sbuf_tensor("idx_now", [P, 2], I32))
        to_rows = ctx.enter_context(nc.sbuf_tensor("to_rows", [P, NE], I32))
        to_rows_over = ctx.enter_context(nc.sbuf_tensor("to_rows_over", [P, 16], I32))
        to_now = ctx.enter_context(nc.sbuf_tensor("to_now", [P, 2], I32))
        over_e = ctx.enter_context(nc.sbuf_tensor("over_e", [P, 17], I32))
        ARENA = 52000
        arena = ctx.enter_context(nc.sbuf_tensor("arena", [P, ARENA], FP))
        PS = ctx.enter_context(nc.psum_tensor("PS", [P, 8, 512], FP))
        y_d = nc.dram_tensor("y_rows", (2 * T * 2, 512), FP).ap()
        hn2_d = nc.dram_tensor("hn2_rows", (T, D), FP).ap()

        top = [0]

        def take(n):
            at = top[0]
            top[0] += n
            assert top[0] <= ARENA, top
            return at

        def view(at, n, pattern=None, parts=P, **kw):
            v = arena[0:parts, at:at + n]
            return v.rearrange(pattern, **kw) if pattern else v

        RING = take(3 * 4096)
        HNT = take(KT * L)
        UB = take(8 * 542)
        CV = take(8 * T)
        QF = take(H * T)
        KF = take(H * L)
        BF = take(H * L)
        VB = take(NT * D)
        VM = take(D)
        EB = take(6 * 512)
        SC = take(2 * 512)
        SB = take(D)
        QE = take(2 * 512)
        KD = take(512)
        OT = take(D)
        OSQ = take(D)
        RST = take(512)
        TH = take(2 * 512)
        GTB = take(8 * T)
        PRM = take(320)
        IDN = take(P)
        ONE = take(P)
        MEAN = take(P)
        LTM = take(P)
        SMALL = take(64)
        NHALF = take(1)
        ELAST = take(4 * 4)
        WDL = take(KT * 16)
        SLOT = take(8)
        HALFNO = take(2)
        IOTA = take(NBLK)

        ring = [view(RING + 4096 * s, 4096, "p (k c) -> p k c", k=KT) for s in range(3)]
        hnT = view(HNT, KT * L, "p (k t) -> p k t", k=KT)
        U = view(UB, 8 * 542, "p (k t) -> p k t", k=8)
        cv = view(CV, 8 * T, "p (k t) -> p k t", k=8)
        Qf = view(QF, H * T, "p (h t) -> p h t", h=H)
        Kf = view(KF, H * L, "p (h t) -> p h t", h=H)
        Bf = view(BF, H * L, "p (h t) -> p h t", h=H)
        V = view(VB, NT * D, "p (c v) -> p c v", c=NT)
        Vm = view(VM, D, parts=META)
        GT = view(GTB, 8 * T, "p (k t) -> p k t", k=8)
        E = [view(EB + 512 * i, 512, "p (h t) -> p h t", h=H) for i in range(6)]
        scT = [view(SC + 512 * i, 512, "p (h t) -> p h t", h=H) for i in range(2)]
        S = view(SB, D, "p (h v) -> p h v", h=H)
        qe = [view(QE + 512 * i, 512, "p (h t) -> p h t", h=H) for i in range(2)]
        kd = view(KD, 512, "p (h t) -> p h t", h=H)
        o_t = view(OT, D, "p (b t) -> p b t", b=8)
        o_sq = view(OSQ, D, "p (b t) -> p b t", b=8)
        conv_sum = view(OT + 512, 512)
        sq_sum = view(KD, 512)
        diag4 = view(RST, 512, "p (h t) -> p h t", h=H)
        th = [view(TH + 512 * i, 512) for i in range(2)]
        prm = view(PRM, 320)
        ident = view(IDN, P)
        ones = view(ONE, P)
        mean_w = view(MEAN, P)
        before = view(LTM, P)
        ss = view(SMALL, 8)
        rs = view(SMALL + 8, 8)
        nhalf = view(NHALF, 1)
        elast = [view(ELAST + 4 * i, 4, "p (h o) -> p h o", o=1) for i in range(4)]
        wdl = view(WDL, KT * 16, "p (k c) -> p k c", k=KT)
        slot = view(SLOT, 8)
        half2 = view(HALFNO, 1)
        beyond = view(HALFNO + 1, 1)
        iota = view(IOTA, NBLK)

        x0 = view(VB, NT * D, "p (i d) -> p i d", i=NT)
        xs = [view(GTB + D * i, D) for i in range(2)]
        xm = view(GTB + 2 * D, D, parts=META)
        prow = view(GTB + 3 * D, 3 * P, "p (a c) -> p a c", a=3)
        junk = view(KF, D)

        def rows_of_x(i):
            return (x0[:, i, :], P) if i < NT else (xm, META)
        glu_t = [view(EB + 528 * i, 528) for i in range(4)]
        wup = view(OT, 512, parts=16)
        dlow = view(OSQ, L, parts=16)

        def cw(t, c):
            return prm[:, 8 * t + c:8 * t + c + 1]

        PB = TAPS * 8

        def par(row, c):
            return prm[:, PB + row + c:PB + row + c + 1]

        xr = view(QF, NT * D, "p (i d) -> p i d", i=NT)
        MID = BF + 8192
        hn2T = [view(MID + D * i, D, "p (k t) -> p k t", k=KT) for i in range(2)]
        assert MID + 2 * D <= SC
        hn2 = [view(SC + D * i, D) for i in range(2)]
        g2b = view(SC + 2 * D, D)
        wr = view(SC + 3 * D, KT * 72, "p (k c) -> p k c", k=KT)
        brb = view(SC + 3 * D + 576, 72)
        lg = view(SC + 3 * D + 648, NT * 72, "p (i c) -> p i c", i=NT)
        rt = [SC + 3 * D + 936]

        def arr(n, pattern=None, **kw):
            at = rt[0]
            rt[0] += n
            assert rt[0] <= GTB
            return view(at, n, pattern, **kw)

        squares = view(TH, D)

        oh = arr(32, "p (i g) -> p i g", i=NT)
        tb = arr(32, "p (i g) -> p i g", i=NT)
        eg = arr(32, "p (i g) -> p i g", i=NT)
        prod = arr(256, "p (i g e) -> p i g e", i=NT, g=NG)
        sel = arr(32, "p (i g) -> p i g", i=NT)
        sel2 = arr(32, "p (i g) -> p i g", i=NT)
        o12 = [arr(32, "p (i g) -> p i g", i=NT) for _ in range(2)]
        m4 = [arr(4) for _ in range(8)]
        wgt = [arr(4) for _ in range(2)]
        rank = arr(8)
        rnd = arr(8)
        row = arr(8)
        first_over = arr(8)
        isj = arr(8)
        blk = arr(8)
        A2 = arr(512, "p (k c) -> p k c", k=2)
        A = [A2[:, k, :] for k in range(2)]
        Asum = arr(256)
        Ccnt = arr(NE)
        Apre = arr((NT + 1) * NE)
        nx = arr(64)
        end = arr(64)
        start = arr(64)
        rows_of = [view(MID + 512 * k, 512) for k in range(3)]
        OR, AB, big2 = rows_of
        OR_over, AB_over = view(MID + 1536, 512), Asum[:, 0:128]
        ends = view(SC + 3 * D, 16 * NE, "p (b e) -> p b e", b=16)
        assert 16 * NE <= 936 + 96
        slots_of = prod.rearrange("p i g e -> p (i g e)")
        desc8 = arr(8)
        be_f = arr(16)
        ones64 = arr(64)
        assert rt[0] <= TH

        wgu = [view(b, 8192, "p (a k f) -> p a k f", k=KT, a=2) for b in (HNT, RING, BF)]
        wdn = [view(b, 4096, "p (j d) -> p j d", j=4) for b in (HNT + 8192, RING + 8192, GTB)]
        xg = [hn2[0], view(TH, D)]
        xT = view(SC + D, D, "p (k t) -> p k t", k=KT)
        gth = [view(MID + 256 * i, 256) for i in range(2)]
        hS = [view(MID + 512 + 256 * i, 256) for i in range(2)]
        hT = [view(MID + 1024 + 256 * i, 256, "p (b g s) -> p b g s", b=2, g=2) for i in range(2)]
        ysb = [view(SC + 2 * D + 512 * i, 512) for i in range(2)]
        fgb = view(RING + 4096, D)
        yt = [view(HNT + D * i, D) for i in range(8)]
        fin = [view(RING + D * i, D) for i in range(NT)]

        win_c = w_in.rearrange("(k p) c -> p k c", p=P)
        chunks = []
        for j in range(4):
            chunks.append([(win_c[:, :, GV0 + 256 * j:GV0 + 256 * j + 256], 0, 256),
                           (win_c[:, :, GG0 + 256 * j:GG0 + 256 * j + 256], 256, 512)])
        for c0 in (K0, Q0, V0, V0 + 512, GA0, GA0 + 512, OG0, OG0 + 512, GB0, GB0 + 512):
            chunks.append([(win_c[:, :, c0:c0 + 512], 0, 512)])
        for w in (w_pw2, w_out):
            wv = w.rearrange("(k p) c -> p k c", p=P)
            for j in range(2):
                chunks.append([(wv[:, :, 512 * j:512 * j + 512], 0, 512)])
        C_K, C_Q, C_V, C_GATES, C_PW, C_OUT = 4, 5, 6, 8, 14, 16
        loaded = [0, 0, 0]
        chunk_at = []
        for n, parts in enumerate(chunks):
            loaded[n % 3] += 16 * len(parts)
            chunk_at.append(loaded[n % 3])

        chunk_end = [("pair_done", 4 * n + 4) for n in range(4)] + [("pair_done", 16 + 4 + 5)] + [("single_done", n) for n in (4, 9, 14)]
        chunk_end += [("single_done", 14 + 4 * n + 4) for n in range(10)]

        def conv_done(c):
            return 2 * TAPS * (c // 2 + 1) - 1 + c % 2

        def used(eng, n):
            eng.wait_ge(sem(chunk_end[n][0]), chunk_end[n][1])

        ROUND = 6
        NLOOP = (NE // 2 - 2) // ROUND
        assert 2 + NLOOP * ROUND == NE // 2
        LAST0 = (NE - 1) // 3 + 1

        def turn(n0, j):
            return n0 % 3, 2 * ROUND // 3 * j + n0 // 3 + 1

        tasks = [("kdm", 0), ("Sm", 0)]
        for c in range(NT):
            body = [("lv", c, i) for i in range(7)] + [("diag", c)]
            if c:
                body.insert(2, ("ss", c - 1))
                body.insert(5, ("bc", c - 1))
            if c < NT - 1:
                body.append(("kd", c))
            body.append(("o", c))
            if c < NT - 1:
                body.append(("S", c))
            tasks += body
        tasks += [("ss", NT - 1), ("bc", NT - 1)]
        e_tasks = [t for t in tasks if t[0] in ("kdm", "lv", "kd")]
        s_tasks = [t for t in tasks if t[0] in ("kdm", "lv", "diag", "kd", "ss", "bc")]
        a_tasks = [t for t in tasks if t[0] in ("Sm", "o", "S")]
        NSLOT = 24
        slots = [[] for _ in range(NSLOT)]
        left = list(tasks)
        for b in range(3, NSLOT):
            n = 2 if b < 13 else -(-len(left) // (NSLOT - b))
            for _ in range(min(n, len(left))):
                slots[b].append(left.pop(0))
        assert not left
        GA_BLOCKS, OG_BLOCKS = range(0, 8), range(8, 16)

        freed = []
        counts = {"sgl_act": 0, "sgl_dve": 0}

        def use(by):
            counts[by] += 1
            freed.append((by, counts[by]))
        for _ in range(4 + 10 + 8):
            use("sgl_act")
        for _ in range(8):
            use("sgl_dve")
        for _ in range(8):
            use("sgl_act")
        for _ in range(8 + 8):
            use("sgl_dve")

        def linker(eng, name):
            count = [0]
            s = sem(name)

            def link(ins):
                count[0] += 1
                ins.then_inc(s, 1)
                eng.wait_ge(s, count[0])
            return link

        block = ctx.enter_context(nc.Block())

        @block.sync
        def _(sp):
            for i in range(NT):
                sp.dma_start(x0[:, i, :], x[P * i:P * i + P, :]).then_inc(sem(f"x_loaded{i}"), 16)
            sp.dma_start(xm, meta).then_inc(sem("meta_loaded"), 16)
            cwr = conv_w.rearrange("t (c p) -> (t c) p", p=P)
            for dst, src in ((prow[:, 0, :], cwr[0:P]), (prow[0:120, 1, :], cwr[P:248]),
                             (prow[R_N1:R_N1 + 8, 2, :], norm1_g), (prow[R_GLA:R_GLA + 8, 2, :], gla_norm_g),
                             (prow[R_CB:R_CB + 8, 2, :], conv_b), (prow[R_LG:R_LG + 8, 2, :], conv_ln_g),
                             (prow[R_LB:R_LB + 8, 2, :], conv_ln_b), (prow[R_BG:R_BG + 16, 2, :], b_gate),
                             (prow[R_BD:R_BD + 4, 2, :], b_decay)):
                sp.dma_start(dst, src).then_inc(sem("prow_loaded"), 16)

            def chunk(n):
                for src, a, b in chunks[n]:
                    sp.dma_start(ring[n % 3][:, :, a:b], src).then_inc(sem(f"chunk_loaded{n % 3}"), 16)
            chunk(0)
            chunk(1)
            chunk(2)
            sp.dma_start(wdl, win_c[:, :, DL0:DL0 + 16]).then_inc(sem("decay_w_loaded"), 16)
            sp.dma_start(wup, w_decay_up).then_inc(sem("decay_w_loaded"), 16)

            def half_load(buf, e, s, a, w):
                sp.dma_start(wgu[buf][:, a, :, :], w[bass.ds(e, 1)].rearrange("o (p k) f -> p (o k) f", k=KT)).then_inc(sem("gu"[a] + "_loaded" + s), 16)

            def gate_up_load(buf, e, s):
                half_load(buf, e, s, 0, w_eg)
                half_load(buf, e, s, 1, w_eu)

            def down_load(buf, e, s):
                sp.dma_start(wdn[buf], w_ed[bass.ds(e, 1)].rearrange("o (j p) d -> p (o j) d", p=P)).then_inc(sem("dn_loaded" + s), 16)
            for n in range(3, len(chunks)):
                used(sp, n - 3)
                chunk(n)
                if n == C_PW + 1:
                    sp.wait_ge(sem("attention_done"), 1)
                    sp.dma_start(xr, x.rearrange("(i p) d -> p i d", p=P)).then_inc(sem("router_loaded"), 16)
                    sp.dma_start(g2b, norm2_g.partition_broadcast(P)).then_inc(sem("router_loaded"), 16)
                    sp.dma_start(wr[:, :, 0:8], w_rg.rearrange("(k p) c -> p k c", p=P)).then_inc(sem("router_loaded"), 16)
                    sp.dma_start(wr[:, :, 8:72], w_re.rearrange("(k p) c -> p k c", p=P)).then_inc(sem("router_loaded"), 16)
                    sp.dma_start(brb[:, 0:8], b_rg.partition_broadcast(P)).then_inc(sem("router_loaded"), 16)
                    sp.dma_start(brb[:, 8:72], b_re.partition_broadcast(P)).then_inc(sem("router_loaded"), 16)
                    gate_up_load(2, 2, "2")

            used(sp, C_PW + 1)
            sp.wait_ge(sem("pw_used"), 1)
            gate_up_load(0, 0, "0")
            down_load(0, 0, "0")
            used(sp, len(chunks) - 1)
            gate_up_load(1, 1, "1")
            down_load(1, 1, "1")
            down_load(2, 2, "2")

            def expert(n0, j):
                b, _ = turn(n0, j)
                n = n0 + 2 * ROUND * j
                sp.wait_ge(sem(f"g_used{b}"), turn(n0 - 3, j)[1])
                half_load(b, n, str(b), 0, w_eg)
                sp.wait_ge(sem(f"gu_used{b}"), turn(n0 - 3, j)[1])
                half_load(b, n, str(b), 1, w_eu)
                sp.wait_ge(sem(f"dn_used{b}"), turn(n0 - 3, j)[1])
                down_load(b, n, str(b))
            expert(3, 0)
            with sp.Fori(0, NLOOP) as j:
                for r in range(2 * ROUND):
                    expert(4 + r, j)
            sp.wait_ge(sem("over_ready"), 1)
            flag = sp.value_load(over_e[0:1, 16:17], min_val=0, max_val=NX)
            with sp.If(flag > 0):
                sp.wait_ge(sem("gu_used0"), LAST0)
                sp.wait_ge(sem("dn_used0"), LAST0)
                with sp.Fori(0, NX) as i:
                    sp.wait_ge(sem("over_free"), i + 1)
                    e = sp.value_load(over_e[0:1, bass.ds(i, 1)], min_val=0, max_val=NE - 1)
                    gate_up_load(0, e, "_over")
                    down_load(0, e, "_over")
                sp.wait_ge(sem("y_stored_over"), 16 * NX)
            with sp.Else():
                sp.nop()
            sp.wait_ge(sem("gu_used1"), (NE - 2) // 3 + 1)
            sp.dma_start(fgb, final_g.partition_broadcast(P)).then_inc(sem("fg_loaded"), 16)
            sp.wait_ge(sem("gu_used0"), LAST0)
            sp.wait_ge(sem("y_stored0"), 16 * NE // 2)
            sp.wait_ge(sem("y_stored1"), 16 * NE // 2)
            y_of = y_d.rearrange("(k i p g) c -> k i p (g c)", k=2, i=NT, g=2)
            for i in range(NT):
                for k in range(2):
                    sp.dma_start(yt[2 * i + k], y_of[k, i]).then_inc(sem(f"y_back{i}"), 16)
            for i in range(NT):
                sp.wait_ge(sem("fin_ready"), i + 1)
                sp.dma_start(out[P * i:P * i + P, :], fin[i]).then_inc(sem("out_stored"), 16)
            sp.wait_ge(sem("out_stored"), 16 * NT)

        @block.tensor
        def _(pe):
            pe.wait_ge(sem("const_ready"), 5)
            pe.wait_ge(sem("prow_loaded"), 16 * 9)
            for a, (r0, n) in enumerate(((0, P), (P, 120), (PB, R_END))):
                t = pe.transpose(PS[:, 7, r0:r0 + n], prow[0:n, a, :], ident[0:n, 0:n])
            t.then_inc(sem("prm_turned"), 1)
            for i in range(NT):
                if i == NT - 1:
                    pe.wait_ge(sem("prm_ready"), 1)
                pe.wait_ge(sem("xs_ready"), i + 1)
                for k in range(KT):
                    t = pe.transpose(PS[:, 2 * i + k // 4, P * (k % 4):P * (k % 4) + P], xs[i % 2][:, P * k:P * k + P], ident)
                t.then_inc(sem("xT_done"), 1)
            pe.wait_ge(sem("xs_ready"), NT + 1)
            pe.wait_ge(sem("xT_taken"), 1)
            for k in range(KT):
                t = pe.transpose(PS[:, 0, META * k:META * k + META], xs[0][0:META, P * k:P * k + P], ident[0:META, 0:META])
            t.then_inc(sem("xT_done"), 1)
            pe.wait_ge(sem("xT_taken"), NT + 1)
            pair = [0]

            def next_pair():
                u = pair[0]
                pair[0] += 1
                if u >= 4:
                    pe.wait_ge(sem("pair_free"), u - 3)
                return 2 * (u % 4)

            def proj528(w, cols, rows=P):
                b = next_pair()
                for k in range(KT):
                    for hf in range(2):
                        t = pe.matmul(PS[0:rows, b + hf, 0:HALF], w[:, k, cols], hnT[:, k, HALF * hf:HALF * hf + HALF],
                                      start=(k == 0), stop=(k == KT - 1))
                t.then_inc(sem("pair_done"), 1)
                return t

            def chunk_ready(n):
                pe.wait_ge(sem(f"chunk_loaded{n % 3}"), chunk_at[n])
                return ring[n % 3]

            for n in range(4):
                w = chunk_ready(n)
                for c in range(2):
                    proj528(w, slice(P * c, P * c + P))
                    proj528(w, slice(256 + P * c, 256 + P * c + P))
            pe.wait_ge(sem("decay_w_loaded"), 32)
            proj528(wdl, slice(0, 16), rows=16)
            w = chunk_ready(C_K)
            proj528(w, slice(0, P))
            pe.wait_ge(sem("dlow_ready"), 1)
            for h in range(H):
                b = next_pair()
                for hf in range(2):
                    t = pe.matmul(PS[:, b + hf, 0:HALF], wup[:, P * h:P * h + P], dlow[:, HALF * hf:HALF * hf + HALF],
                                  start=True, stop=True)
                t.then_inc(sem("pair_done"), 1)
            for h in range(1, H):
                proj528(w, slice(P * h, P * h + P))
            pe.wait_ge(sem("pair_free"), pair[0])

            single = [0]

            def next_single():
                u = single[0]
                single[0] += 1
                if u >= 4:
                    s, n = freed[u - 4]
                    pe.wait_ge(sem(s), n)
                return u % 4

            def proj512(w, c, moving):
                b = next_single()
                for k in range(KT):
                    t = pe.matmul(PS[:, b, :], w[:, k, P * c:P * c + P], moving[:, k, 0:T], start=(k == 0), stop=(k == KT - 1))
                t.then_inc(sem("single_done"), 1)
                return t

            w = chunk_ready(C_Q)
            for h in range(H):
                proj512(w, h, hnT)
            for j in range(2):
                w = chunk_ready(C_V + j)
                for i in range(NT + 1):
                    rows = P if i < NT else META
                    b = next_single()
                    for k in range(KT):
                        t = pe.matmul(PS[0:rows, b, :], hnT[:, k, P * i:P * i + rows], w[:, k, :], start=(k == 0), stop=(k == KT - 1))
                    t.then_inc(sem("single_done"), 1)
                if j == 0:
                    pe.wait_ge(sem("conv_summed"), 8)
                    pe.matmul(PS[:, 6, :], mean_w, conv_sum, start=True, stop=True).then_inc(sem("ln_mean"), 1)
            pe.wait_ge(sem("ln_sq_used"), 8)
            for i in range(NT):
                t = pe.matmul(PS[:, 7, i:i + 1], sq_sum[:, P * i:P * i + P], mean_w[:, 0:1], start=True, stop=True)
            t.then_inc(sem("ln_var"), 1)

            n_e, n_s, n_a = [0], [0], [0]

            def attend(t):
                kind, c = t[0], t[1]
                if kind in ("kdm", "lv", "diag", "kd", "ss", "bc"):
                    s = n_s[0]
                    n_s[0] += 1
                    bank = 4 + s % 2
                    if s >= 2:
                        pe.wait_ge(sem("score_taken"), s - 1)
                if kind in ("kdm", "lv", "kd"):
                    ei = n_e[0]
                    n_e[0] += 1
                    pe.wait_ge(sem("e_mul"), ei + 1)
                    ev = E[ei % 6]
                if kind == "kdm":
                    for h in range(H):
                        m = pe.transpose(PS[0:META, bank, P * h:P * h + P], ev[:, h, 0:META], ident)
                elif kind == "kd":
                    for h in range(H):
                        m = pe.transpose(PS[:, bank, P * h:P * h + P], ev[:, h, :], ident)
                elif kind == "lv":
                    for h in range(H):
                        m = pe.matmul(PS[:, bank, P * h:P * h + P], ev[:, h, :], ev[:, h, :], start=True, stop=True)
                elif kind == "diag":
                    for h in range(H):
                        m = pe.matmul(PS[:, bank, P * h:P * h + P], Kf[:, h, P * c:P * c + P], Qf[:, h, P * c:P * c + P],
                                      start=True, stop=True)
                elif kind == "ss":
                    pe.wait_ge(sem("o_sq"), c + 1)
                    for j in range(8):
                        m = pe.matmul(PS[:, bank, j // 2:j // 2 + 1], o_sq[:, j, :], ones[:, 0:1], start=(j % 2 == 0), stop=(j % 2 == 1))
                elif kind == "bc":
                    pe.wait_ge(sem("o_diag"), c + 1)
                    m = pe.matmul(PS[:, bank, :], ones, view(RST, 512), start=True, stop=True)
                if kind in ("kdm", "lv", "diag", "kd", "ss", "bc"):
                    m.then_inc(sem("score_done"), 1)
                    return
                a = n_a[0]
                n_a[0] += 1
                if a >= 1:
                    pe.wait_ge(sem("acc_taken"), a)
                pe.wait_ge(sem("score_taken"), n_s[0])
                if kind == "o":
                    pe.wait_ge(sem("qe_ready"), c + 1)
                    for h in range(H):
                        for vb in range(2):
                            j = 2 * h + vb
                            o = PS[:, 6 + j // 4, P * (j % 4):P * (j % 4) + P]
                            pe.matmul(o, S[:, h, P * vb:P * vb + P], qe[c % 2][:, h, :], start=True, stop=False)
                            m = pe.matmul(o, V[:, c, P * j:P * j + P], scT[c % 2][:, h, :], start=False, stop=True)
                else:
                    rows = META if kind == "Sm" else P
                    vs = Vm if kind == "Sm" else V[:, c, :]
                    for h in range(H):
                        m = pe.matmul(PS[:, 6 + h // 2, DV * (h % 2):DV * (h % 2) + DV], kd[0:rows, h, :], vs[0:rows, DV * h:DV * h + DV],
                                      start=True, stop=True)
                m.then_inc(sem("acc_done"), 1)

            for b in range(NSLOT):
                n = C_GATES + b // 4
                if b % 4 == 0:
                    w = chunk_ready(n)
                if b == 2:
                    pe.wait_ge(sem("ln_diag"), 1)
                    pe.matmul(PS[:, 7, :], ones, view(RST, 512), start=True, stop=True).then_inc(sem("ln_spread"), 1)
                proj512(w, b % 4, hnT)
                if b == 3:
                    pe.wait_ge(sem("ln_scaled"), 8)
                    pe.wait_ge(sem("sgl_act"), 14)
                for t_ in slots[b]:
                    attend(t_)
            pe.wait_ge(sem("u_final"), 8)
            for b in range(8):
                if b % 4 == 0:
                    w = chunk_ready(C_PW + b // 4)
                proj512(w, b % 4, cv)
            pe.wait_ge(sem("mix_ready"), 8)
            def out_half(i, j):
                w = chunk_ready(C_OUT + j)
                b = next_single()
                for k in range(KT):
                    t = pe.matmul(PS[:, b, :], GT[:, k, P * i:P * i + P], w[:, k, :], start=(k == 0), stop=(k == KT - 1))
                t.then_inc(sem("single_done"), 1)

            def turn_hn2(i):
                pe.wait_ge(sem("hn2_ready"), i + 1)
                if i >= 1:
                    pe.wait_ge(sem("hn2T_ready"), i)
                for k in range(KT):
                    t = pe.transpose(PS[:, 4 + k // 4, P * (k % 4):P * (k % 4) + P], hn2[i % 2][:, P * k:P * k + P], ident)
                t.then_inc(sem("hn2T_done"), 1)

            def logits(i):
                pe.wait_ge(sem("router_loaded"), 96)
                pe.wait_ge(sem("hn2T_ready"), i + 1)
                if i >= 2:
                    pe.wait_ge(sem("logits_taken"), i - 1)
                for k in range(KT):
                    t = pe.matmul(PS[:, 6 + i % 2, 0:72], hn2T[i % 2][:, k, :], wr[:, k, :], start=(k == 0), stop=(k == KT - 1))
                t.then_inc(sem("logits_done"), 1)
            for i in range(NT):
                out_half(i, 0)
                if i >= 2:
                    logits(i - 2)
                out_half(i, 1)
                if i >= 1:
                    turn_hn2(i - 1)
            logits(NT - 2)
            turn_hn2(NT - 1)
            logits(NT - 1)
            pe.wait_ge(sem("choice_ready"), 1)
            pe.matmul(PS[:, 0, 0:(NT + 1) * NE], ones, Apre, start=True, stop=False)
            pe.matmul(PS[:, 0, 0:NT * NE], before, Asum, start=False, stop=True).then_inc(sem("ranks_done"), 1)

            def slots_by_row(bank, r, e, n):
                for g in range(2):
                    for i in range(2 * NT):
                        t = pe.matmul(PS[CAP * g:CAP * g + CAP, bank, 0:n], r[:, CAP * i:CAP * i + CAP], e[:, n * i:n * i + n],
                                      start=(i == 0), stop=(i == 2 * NT - 1))
                return t
            pe.wait_ge(sem("onehot_ready"), 1)
            slots_by_row(1, OR, AB, NE).then_inc(sem("idx_done"), 1)

            def turn_rows(rows):
                xv = rows.rearrange("r (p k) -> r k p", k=KT)
                for k in range(KT):
                    t = pe.transpose(PS[:, k // 4, P * (k % 4):P * (k % 4) + P], xv[:, k, :], ident)
                return t

            def gate_or_up(a, buf, col0, bank):
                for k in range(KT):
                    for g in range(2):
                        t = pe.matmul(PS[CAP * g:CAP * g + CAP, bank, 256 * a:256 * a + 256],
                                      xT[:, k, col0:col0 + CAP], wgu[buf][:, a, k, 256 * g:256 * g + 256],
                                      start=(k == 0), stop=(k == KT - 1))
                return t

            def turn_h(e, bank):
                for b in range(2):
                    t = pe.transpose(PS[:, bank, P * b:P * b + P], hS[e][:, P * b:P * b + P], ident)
                return t

            def down(e, buf, bank):
                for j in range(4):
                    for g in range(2):
                        t = pe.matmul(PS[CAP * g:CAP * g + CAP, bank, :], hT[e][:, j % 2, j // 2, :],
                                      wdn[buf][:, j, 512 * g:512 * g + 512], start=(j == 0), stop=(j == 3))
                return t

            def pair_of_experts(i0, j):
                first = i0 == 0
                i = i0 + ROUND * j
                pe.wait_ge(sem(f"rows_gathered{i0 % 2}"), 16 * (ROUND // 2 * j + i0 // 2 + 1))
                if not first:
                    pe.wait_ge(sem("xT_ready"), i)
                turn_rows(xg[i0 % 2]).then_inc(sem("rows_turned"), 1)
                pe.wait_ge(sem("xT_ready"), i + 1)
                for e in range(2):
                    b, nth = turn(2 * i0 + e, j)
                    pe.wait_ge(sem(f"g_loaded{b}"), 16 * nth)
                    if not first:
                        pe.wait_ge(sem(f"h_ready{e}"), i)
                    if (i0, e) == (1, 1):
                        pe.wait_ge(sem("over_ready"), 1)
                    gate_or_up(0, b, CAP * e, 2 + e).then_inc(sem(f"g_used{b}"), 1)
                    pe.wait_ge(sem(f"u_loaded{b}"), 16 * nth)
                    gate_or_up(1, b, CAP * e, 2 + e).then_inc(sem(f"gu_used{b}"), 1)
                    pe.wait_ge(sem(f"h_ready{e}"), i + 1)
                    if not first:
                        pe.wait_ge(sem(f"hT_ready{e}"), i)
                    turn_h(e, 4 + e).then_inc(sem(f"h_turned{e}"), 1)
                    pe.wait_ge(sem(f"hT_ready{e}"), i + 1)
                    pe.wait_ge(sem(f"dn_loaded{b}"), 16 * nth)
                    if not first:
                        pe.wait_ge(sem(f"y_taken{e}"), i)
                    down(e, b, 6 + e).then_inc(sem(f"dn_used{b}"), 1)
            pair_of_experts(0, 0)
            pe.wait_ge(sem("onehot_over_ready"), 1)
            slots_by_row(3, OR_over, AB_over, 16).then_inc(sem("idx_over_done"), 1)
            pair_of_experts(1, 0)
            with pe.Fori(0, NLOOP) as j:
                for r in range(ROUND):
                    pair_of_experts(2 + r, j)

            flag = pe.value_load(over_e[0:1, 16:17], min_val=0, max_val=NX)
            with pe.If(flag > 0):
                with pe.Fori(0, NX) as i:
                    pe.wait_ge(sem("rows_gathered_over"), 16 * (i + 1))
                    turn_rows(xg[0]).then_inc(sem("rows_turned_over"), 1)
                    pe.wait_ge(sem("xT_ready_over"), i + 1)
                    pe.wait_ge(sem("g_loaded_over"), 16 * (i + 1))
                    gate_or_up(0, 0, 0, 2)
                    pe.wait_ge(sem("u_loaded_over"), 16 * (i + 1))
                    gate_or_up(1, 0, 0, 2).then_inc(sem("gu_used_over"), 1)
                    pe.wait_ge(sem("h_ready_over"), i + 1)
                    turn_h(0, 4).then_inc(sem("h_turned_over"), 1)
                    pe.wait_ge(sem("hT_ready_over"), i + 1)
                    pe.wait_ge(sem("dn_loaded_over"), 16 * (i + 1))
                    down(0, 0, 6).then_inc(sem("dn_used_over"), 1)
            with pe.Else():
                pe.nop()

        @block.scalar
        def _(act):
            link = linker(act, "act_order")
            for i in range(NT + 1):
                src, n = rows_of_x(i)
                act.wait_ge(sem(f"x_loaded{i}" if i < NT else "meta_loaded"), 16)
                link(act.activation(junk[0:n, :], src, ACT.Square, accum_out=ss[0:n, i:i + 1]))
                act.nop().then_inc(sem("ss_ready"), 1)
            act.wait_ge(sem("prm_ready"), 1)
            u = 0

            def pair_view(u, rows=P):
                b = 2 * (u % 4)
                return PS[0:rows, b:b + 2, 0:HALF]

            def split(t):
                return t.rearrange("p (a t) -> p a t", a=2)
            for c in range(8):
                if c >= 2:
                    act.wait_ge(sem("u_ready"), c - 1)
                act.wait_ge(sem("pair_done"), u + 1)
                act.activation(split(glu_t[c % 2]), pair_view(u), ACT.Copy).then_inc(sem("pair_free"), 1)
                u += 1
                act.wait_ge(sem("pair_done"), u + 1)
                act.activation(split(glu_t[2 + c % 2]), pair_view(u), ACT.Tanh, scale=0.5).then_inc(sem("pair_free"), 1)
                u += 1

            def keys(h):
                nonlocal u
                act.wait_ge(sem("pair_done"), u + 1)
                act.activation(split(Kf[:, h, :]), pair_view(u), ACT.Copy).then_inc(sem("pair_free"), 1)
                u += 1
            act.wait_ge(sem("pair_done"), u + 1)
            link(act.activation(split(dlow), pair_view(u, 16), ACT.Copy))
            act.nop().then_inc(sem("dlow_ready"), 1)
            act.nop().then_inc(sem("pair_free"), 1)
            u += 1
            keys(0)
            act.wait_ge(sem("u_ready"), 8)
            for h in range(H):
                act.wait_ge(sem("pair_done"), u + 1)
                if h >= 2:
                    act.wait_ge(sem("decay_taken"), h - 1)
                act.activation(split(glu_t[h % 2]), pair_view(u), ACT.Relu, scale=-1.0, bias=par(R_BD, h))
                link(act.activation(split(glu_t[2 + h % 2]), pair_view(u), ACT.Abs, scale=-1.0, bias=par(R_BD, h)))
                act.nop().then_inc(sem("pair_free"), 1)
                u += 1
                link(act.activation(glu_t[2 + h % 2], glu_t[2 + h % 2], ACT.Exp, scale=-1.0))
                act.activation(glu_t[2 + h % 2], glu_t[2 + h % 2], ACT.Ln, bias=1.0).then_inc(sem("decay_logs"), 1)
            for h in range(1, H):
                keys(h)
            s = 0
            for h in range(H):
                act.wait_ge(sem("single_done"), s + 1)
                act.activation(Qf[:, h, :], PS[:, s % 4, :], ACT.Copy, scale=float(DK) ** -0.5).then_inc(sem("sgl_act"), 1)
                s += 1

            def values(j):
                nonlocal s
                for i in range(NT + 1):
                    act.wait_ge(sem("single_done"), s + 1)
                    n = P if i < NT else META
                    dst = V[:, i, 512 * j:512 * j + 512] if i < NT else Vm[:, 512 * j:512 * j + 512]
                    act.activation(dst, PS[0:n, s % 4, :], ACT.Copy).then_inc(sem("sgl_act"), 1)
                    s += 1
            values(0)
            for k in range(8):
                act.wait_ge(sem("ln_centred"), k + 1)
                if k >= 2:
                    act.wait_ge(sem("ln_sq_used"), k - 1)
                act.activation(th[k % 2], cv[:, k, :], ACT.Square).then_inc(sem("ln_sq"), 1)
            values(1)
            n_e = 0
            for b in range(NSLOT):
                if b == 2:
                    for k in range(8):
                        act.wait_ge(sem("ln_scaled"), k + 1)
                        if k >= 2:
                            act.wait_ge(sem("u_final"), k - 1)
                        act.activation(th[k % 2], cv[:, k, :], ACT.Tanh, scale=par(R_LG, k), bias=par(R_LB, k)).then_inc(sem("ln_tanh"), 1)
                for t in slots[b]:
                    if t[0] in ("kdm", "lv", "kd"):
                        act.wait_ge(sem("e_sub"), n_e + 1)
                        ev = E[n_e % 6]
                        if t[0] == "kdm":
                            ev = ev[:, :, 0:META]
                        act.activation(ev, ev, ACT.Exp, scale=-1.0 / TAU).then_inc(sem("e_exp"), 1)
                        n_e += 1
                    if t[0] == "lv" and t[2] == 0:
                        c = t[1]
                        if c >= 2:
                            act.wait_ge(sem("acc_done"), a_tasks.index(("o", c - 2)) + 1)
                        act.activation(elast[c], Bf[:, :, P * c + P - 1:P * c + P], ACT.Exp, scale=-1.0 / TAU)
                        act.activation(qe[c % 2], Bf[:, :, P * c:P * c + P], ACT.Exp, scale=-1.0 / TAU).then_inc(sem("qe_exp"), 1)
                act.wait_ge(sem("single_done"), s + 1)
                bank = PS[:, s % 4, :]
                s += 1
                if b in GA_BLOCKS:
                    act.activation(GT[:, b, :], bank, ACT.Tanh, scale=0.5, bias=par(R_BG, b)).then_inc(sem("sgl_act"), 1)
                elif b in OG_BLOCKS:
                    k = b - 8
                    if k >= 2:
                        act.wait_ge(sem("sgl_dve"), k - 1)
                    else:
                        act.wait_ge(sem("u_final"), 8)
                    act.activation(th[k % 2], bank, ACT.Tanh, scale=0.5).then_inc(sem("og_tanh"), 1)
                else:
                    if b == 16:
                        act.wait_ge(sem("conv_taps"), conv_done(7))
                    act.activation(U[:, b - 16, 0:T], bank, ACT.Tanh, scale=0.5, bias=par(R_BG, 8 + b - 16)).then_inc(sem("sgl_act"), 1)
            for i in range(NT):
                act.wait_ge(sem("h_ready"), i + 1)
                link(act.activation(squares, xr[:, i, :], ACT.Square, accum_out=ss[:, i:i + 1]))
                act.nop().then_inc(sem("ss2_ready"), 1)
            act.wait_ge(sem("group_diff"), 1)
            act.activation(eg, eg, ACT.Exp).then_inc(sem("group_exp"), 1)
            act.wait_ge(sem("choice_diff"), 1)
            act.activation(m4[3], m4[3], ACT.Exp).then_inc(sem("choice_exp"), 1)

            def expert(i0, e, j):
                i = i0 + ROUND * j
                b, nth = turn(2 * i0 + e, j)
                act.wait_ge(sem(f"gu_used{b}"), nth)
                if i0:
                    act.wait_ge(sem(f"h_ready{e}"), i)
                act.activation(gth[e], PS[:, 2 + e, 0:256], ACT.Tanh, scale=0.5).then_inc(sem(f"g_tanh{e}"), 1)
                act.wait_ge(sem(f"dn_used{b}"), nth)
                if i0:
                    act.wait_ge(sem(f"y_stored{e}"), 16 * i)
                act.activation(ysb[e], PS[:, 6 + e, :], ACT.Copy).then_inc(sem(f"y_taken{e}"), 1)
            act.wait_ge(sem("rows_gathered0"), 16)
            for i0 in range(2):
                for e in range(2):
                    expert(i0, e, 0)
            with act.Fori(0, NLOOP) as j:
                for r in range(ROUND):
                    for e in range(2):
                        expert(2 + r, e, j)
            act.wait_ge(sem("over_ready"), 1)
            flag = act.value_load(over_e[0:1, 16:17], min_val=0, max_val=NX)
            with act.If(flag > 0):
                with act.Fori(0, NX) as i:
                    act.wait_ge(sem("gu_used_over"), i + 1)
                    act.activation(gth[0], PS[:, 2, 0:256], ACT.Tanh, scale=0.5).then_inc(sem("g_tanh_over"), 1)
                    act.wait_ge(sem("dn_used_over"), i + 1)
                    act.activation(ysb[0], PS[:, 6, :], ACT.Copy).then_inc(sem("y_taken_over"), 1)
            with act.Else():
                act.nop()
            for i in range(NT):
                act.wait_ge(sem("h_final"), i + 1)
                link(act.activation(fin[i], xr[:, i, :], ACT.Square, accum_out=ss[:, i:i + 1]))
                act.nop().then_inc(sem("ss3_ready"), 1)

        @block.gpsimd
        def _(pool):
            link = linker(pool, "pool_order")
            link(pool.memset(ident, 0.0))
            pool.affine_select(out=ident, in_=ident, compare_op=ALU.not_equal, fill=1.0, base=0,
                               pattern=[[-1, P]], channel_multiplier=1).then_inc(sem("const_ready"), 1)
            pool.memset(ones, 1.0).then_inc(sem("const_ready"), 1)
            pool.memset(mean_w, 1.0 / D).then_inc(sem("const_ready"), 1)
            link(pool.memset(before, 1.0))
            pool.affine_select(out=before, in_=before, compare_op=ALU.is_gt, fill=0.0, base=0,
                               pattern=[[1, P]], channel_multiplier=-1).then_inc(sem("const_ready"), 1)
            pool.iota(cst_i[:, 0, :], pattern=[[1, P]], base=0, channel_multiplier=0).then_inc(sem("iota_ready"), 1)
            pool.iota(cst_i[:, 1, :], pattern=[[0, P]], base=0, channel_multiplier=1).then_inc(sem("iota_ready"), 1)
            pool.iota(iota, pattern=[[1, NBLK]], base=0, channel_multiplier=0, allow_small_or_imprecise_dtypes=True)
            pool.iota(slot, pattern=[[P, 2 * NT]], base=1, channel_multiplier=1, allow_small_or_imprecise_dtypes=True)
            pool.iota(beyond, pattern=[[0, 1]], base=4 * T * 2, channel_multiplier=1, allow_small_or_imprecise_dtypes=True)
            pool.memset(U[:, :, 0:14], 0.0)
            pool.memset(nhalf, -0.5)
            pool.memset(view(QE, D), 0.0)
            pool.memset(scT[0], 0.0)
            pool.memset(scT[1], 0.0).then_inc(sem("const_ready"), 1)


            def rsqrt(v, wait, n, done, rows=P):
                pool.wait_ge(sem(wait), n)
                pool.tensor_tensor(v, v, nhalf[0:rows, :].to_broadcast([rows, v.shape[-1]]), ALU.pow).then_inc(sem(done), 1)
            pool.wait_ge(sem("const_ready"), 5)
            for i in range(NT + 1):
                n = P if i < NT else META
                rsqrt(rs[0:n, i:i + 1], "ms_ready", i + 1, "rs_ready", n)
            for c in range(8):
                v, g = glu_t[c % 2], glu_t[2 + c % 2]
                pool.wait_ge(sem("pair_free"), 2 * c + 2)
                link(pool.tensor_tensor(g, g, v, ALU.mult))
                pool.tensor_tensor(U[:, c, 30:542], g[:, 0:T], v[:, 0:T], ALU.add)
                pool.tensor_tensor(U[:, c, 14:30], g[:, T:L], v[:, T:L], ALU.add).then_inc(sem("u_ready"), 1)
            for h in range(H):
                pool.wait_ge(sem("decay_logs"), h + 1)
                pool.tensor_tensor(Bf[:, h, :], glu_t[h % 2], glu_t[2 + h % 2], ALU.add).then_inc(sem("decay_taken"), 1)
            pool.wait_ge(sem("dlow_ready"), 1)
            for k in range(8):
                pool.wait_ge(sem("conv_taps"), conv_done(k))
                if k:
                    pool.wait_ge(sem("conv_summed"), k)
                m = pool.tensor_tensor(conv_sum, conv_sum, cv[:, k, :], ALU.add) if k else pool.tensor_copy(conv_sum, cv[:, 0, :])
                m.then_inc(sem("conv_summed"), 1)
            for k in range(8):
                pool.wait_ge(sem("ln_sq"), k + 1)
                if k:
                    pool.wait_ge(sem("ln_sq_used"), k)
                m = pool.tensor_tensor(sq_sum, sq_sum, th[k % 2], ALU.add) if k else pool.tensor_copy(sq_sum, th[0])
                m.then_inc(sem("ln_sq_used"), 1)
            rsqrt(rs[:, 0:NT], "ln_read", 2, "ln_rstd")
            n_e = 0
            for b in range(NSLOT):
                for t in slots[b]:
                    c = t[1]
                    if t[0] in ("kdm", "lv", "kd"):
                        ev = E[n_e % 6]
                        pool.wait_ge(sem("e_exp"), n_e + 1)
                        if t[0] == "kdm":
                            m = pool.tensor_tensor(ev[:, :, 0:META], ev[:, :, 0:META], Kf[:, :, T:L], ALU.mult)
                        elif t[0] == "kd":
                            m = pool.tensor_tensor(ev, ev, Kf[:, :, P * c:P * c + P], ALU.mult)
                        else:
                            w = LEVELS[t[2]]
                            e4 = ev.rearrange("p h (g a w) -> p h g a w", a=2, w=w)
                            k4 = Kf[:, :, P * c:P * c + P].rearrange("p h (g a w) -> p h g a w", a=2, w=w)
                            q4 = Qf[:, :, P * c:P * c + P].rearrange("p h (g a w) -> p h g a w", a=2, w=w)
                            pool.tensor_tensor(e4[:, :, :, 0, :], e4[:, :, :, 0, :], k4[:, :, :, 0, :], ALU.mult)
                            m = pool.tensor_tensor(e4[:, :, :, 1, :], e4[:, :, :, 1, :], q4[:, :, :, 1, :], ALU.mult)
                        m.then_inc(sem("e_mul"), 1)
                        n_e += 1
                    if t[0] == "lv" and t[2] == 0:
                        pool.wait_ge(sem("qe_exp"), c + 1)
                        pool.tensor_tensor(qe[c % 2], qe[c % 2], Qf[:, :, P * c:P * c + P], ALU.mult).then_inc(sem("qe_ready"), 1)
                    if t[0] == "o":
                        pool.wait_ge(sem("acc_taken"), a_tasks.index(t) + 1)
                        if c >= 1:
                            pool.wait_ge(sem("score_done"), s_tasks.index(("ss", c - 1)) + 1)
                        pool.tensor_tensor(o_sq, o_t, o_t, ALU.mult).then_inc(sem("o_sq"), 1)
                    if t[0] == "ss":
                        rsqrt(rs[:, 0:H], "score_taken", s_tasks.index(t) + 1, "o_rstd")
                if b in GA_BLOCKS:
                    pool.wait_ge(sem("sgl_act"), 14 + b + 1)
                    pool.tensor_scalar(GT[:, b, :], GT[:, b, :], 1.0, None, ALU.add).then_inc(sem("ga_ready"), 1)
            for i in range(NT):
                rsqrt(rs[:, i:i + 1], "ms2_ready", i + 1, "rs2_ready")
                pool.wait_ge(sem("hn2_ready"), i + 1)
                pool.dma_start(hn2_d[P * i:P * i + P, :], hn2[i % 2]).then_inc(sem(f"hn2_stored{i % 2}"), 16)


            def gather(nth, buf):
                pool.tensor_copy(idx_now[:, buf:buf + 1], idx_pair[:, bass.ds(nth - 1, 1)]).then_inc(sem("idx_now"), 1)
                pool.wait_ge(sem("idx_now"), nth)
                pool.nop().then_inc(sem("dma_index"), 1)
                pool.indirect_dma_start(xg[buf], None, hn2_d, bass.IndirectOffsetOnAxis(ap=idx_now[:, buf:buf + 1], axis=0),
                                        bounds_check=T - 1, oob_is_err=False).then_inc(sem(f"rows_gathered{buf}"), 16)

            def scatter(nth, e):
                pool.wait_ge(sem(f"y_taken{e}"), nth)
                pool.tensor_copy(to_now[:, e:e + 1], to_rows[:, bass.ds(2 * nth - 2 + e, 1)]).then_inc(sem(f"to_now{e}"), 1)
                pool.wait_ge(sem(f"to_now{e}"), nth)
                pool.nop().then_inc(sem("dma_index"), 1)
                pool.indirect_dma_start(y_d, bass.IndirectOffsetOnAxis(ap=to_now[:, e:e + 1], axis=0), ysb[e], None,
                                        bounds_check=4 * T - 1, oob_is_err=False).then_inc(sem(f"y_stored{e}"), 16)
            pool.wait_ge(sem("hn2_stored0"), 32)
            pool.wait_ge(sem("hn2_stored1"), 32)
            pool.wait_ge(sem("hn2T_done"), NT)
            link(pool.memset(xg[0], 0.0))
            link(pool.memset(xg[1], 0.0))
            pool.wait_ge(sem("tables_ready"), 1)
            gather(1, 0)
            gather(2, 1)
            pool.wait_ge(sem("to_rows_ready"), 1)
            with pool.Fori(0, (NE // 2 - 2) // 2) as m:
                for q in range(2):
                    nth = 2 * m + q + 1
                    pool.wait_ge(sem("rows_turned"), nth)
                    gather(nth + 2, q)
                    for e in range(2):
                        scatter(nth, e)
            for nth in (NE // 2 - 1, NE // 2):
                for e in range(2):
                    scatter(nth, e)
            pool.wait_ge(sem("over_ready"), 1)
            flag = pool.value_load(over_e[0:1, 16:17], min_val=0, max_val=NX)
            with pool.If(flag > 0):
                pool.wait_ge(sem("rows_turned"), NE // 2)
                pool.wait_ge(sem("gu_used0"), LAST0)
                pool.wait_ge(sem("y_stored0"), 16 * NE // 2)
                pool.nop().then_inc(sem("over_free"), 1)
                with pool.Fori(0, NX) as i:
                    nth = i + 1
                    pool.tensor_copy(idx_now[0:CAP, 0:1], idx_over[:, bass.ds(i, 1)]).then_inc(sem("idx_now_over"), 1)
                    pool.wait_ge(sem("idx_now_over"), nth)
                    pool.nop().then_inc(sem("dma_index"), 1)
                    pool.indirect_dma_start(xg[0][0:CAP, :], None, hn2_d, bass.IndirectOffsetOnAxis(ap=idx_now[0:CAP, 0:1], axis=0),
                                            bounds_check=T - 1, oob_is_err=False).then_inc(sem("rows_gathered_over"), 16)
                    pool.wait_ge(sem("y_taken_over"), nth)
                    pool.tensor_copy(to_now[:, 0:1], to_rows_over[:, bass.ds(i, 1)]).then_inc(sem("to_now_over"), 1)
                    pool.wait_ge(sem("to_now_over"), nth)
                    pool.nop().then_inc(sem("dma_index"), 1)
                    pool.indirect_dma_start(y_d, bass.IndirectOffsetOnAxis(ap=to_now[:, 0:1], axis=0), ysb[0], None,
                                            bounds_check=4 * T - 1, oob_is_err=False).then_inc(sem("y_stored_over"), 16)
                    pool.wait_ge(sem("y_stored_over"), 16 * nth)
                    pool.nop().then_inc(sem("over_free"), 1)
            with pool.Else():
                pool.nop()
            for i in range(NT):
                rsqrt(rs[:, i:i + 1], "ms3_ready", i + 1, "rs3_ready")

        @block.vector
        def _(dve):
            link = linker(dve, "dve_order")
            def scale_rows(i):
                src, n = rows_of_x(i)
                dve.wait_ge(sem("rs_ready"), i + 1)
                if i >= 2:
                    dve.wait_ge(sem("xT_done"), i - 1)
                dve.tensor_scalar(xs[i % 2][0:n, :], src, rs[0:n, i:i + 1], None, ALU.mult).then_inc(sem("xs_ready"), 1)

            def mean_square(i):
                n = P if i < NT else META
                dve.wait_ge(sem("ss_ready"), i + 1)
                dve.tensor_scalar(rs[0:n, i:i + 1], ss[0:n, i:i + 1], 1.0 / D, EPS, ALU.mult, ALU.add).then_inc(sem("ms_ready"), 1)
            mean_square(0)
            mean_square(1)
            scale_rows(0)
            scale_rows(1)
            dve.wait_ge(sem("prm_turned"), 1)
            link(dve.tensor_copy(prm[:, 0:PB + R_END], PS[:, 7, 0:PB + R_END]))
            link(dve.tensor_scalar(prm[:, 0:PB], prm[:, 0:PB], 0.5, None, ALU.mult))
            link(dve.tensor_scalar(prm[:, PB + R_GLA:PB + R_GLA + 8], prm[:, PB + R_GLA:PB + R_GLA + 8], 0.25, None, ALU.mult))
            link(dve.tensor_scalar(prm[:, PB + R_LG:PB + R_BG + 16], prm[:, PB + R_LG:PB + R_BG + 16], 0.5, None, ALU.mult))
            link(dve.tensor_scalar(prm[:, PB + R_BD:PB + R_BD + 4], prm[:, PB + R_BD:PB + R_BD + 4], -1.0, None, ALU.mult))
            dve.nop().then_inc(sem("prm_ready"), 1)
            for i in range(NT + 1):
                if 2 <= i + 1 <= NT:
                    mean_square(i + 1)
                    scale_rows(i + 1)
                dve.wait_ge(sem("xT_done"), i + 1)
                if i < NT:
                    for hf in range(2):
                        g = prm[:, PB + 4 * hf:PB + 4 * hf + 4].rearrange("p (k o) -> p k o", o=1)
                        m = dve.tensor_tensor(hnT[:, 4 * hf:4 * hf + 4, P * i:P * i + P],
                                              PS[:, 2 * i + hf, :].rearrange("p (k t) -> p k t", k=4),
                                              g.to_broadcast([P, 4, P]), ALU.mult)
                else:
                    g = prm[:, PB:PB + 8].rearrange("p (k o) -> p k o", o=1)
                    m = dve.tensor_tensor(hnT[:, :, T:L], PS[:, 0, 0:KT * META].rearrange("p (k t) -> p k t", k=KT),
                                          g.to_broadcast([P, KT, META]), ALU.mult)
                m.then_inc(sem("xT_taken"), 1)
            dve.wait_ge(sem("iota_ready"), 2)
            xi, xf = cst_i[:, 0, :], view(SB, P)
            link(dve.tensor_tensor(xi, cst_i[:, 0, :], cst_i[:, 1, :], ALU.bitwise_xor))
            link(dve.tensor_copy(xf, xi))
            dve.wait_ge(sem("const_ready"), 5)
            big = view(SB + P, P)
            link(dve.tensor_tensor(big, before, ident, ALU.add))
            link(dve.tensor_scalar(big, big, -1000.0, 1000.0, ALU.mult, ALU.add))
            link(dve.tensor_tensor(xf, xf, big, ALU.add))
            for n, w in enumerate(LEVELS + [0.5]):
                link(dve.tensor_scalar(masks[:, n, :], xf, float(2 * w), None, ALU.is_lt))
            n = 0
            for c in range(0, 8, 2):
                dve.wait_ge(sem("u_ready"), c + 2)
                for t in range(TAPS):
                    for d in (c, c + 1):
                        if t:
                            dve.wait_ge(sem("conv_taps"), n - 1)
                            m = dve.scalar_tensor_tensor(out=cv[:, d, :], in0=U[:, d, t:t + T], scalar=cw(t, d), in1=cv[:, d, :],
                                                         op0=ALU.mult, op1=ALU.add)
                        else:
                            m = dve.tensor_scalar(cv[:, d, :], U[:, d, 0:T], cw(0, d), par(R_CB, d), ALU.mult, ALU.add)
                        m.then_inc(sem("conv_taps"), 1)
                        n += 1
            dve.wait_ge(sem("decay_taken"), H)
            for h in range(H):
                for c in range(NT + 1):
                    a, n = P * c, P if c < NT else META
                    m = dve.tensor_tensor_scan(Bf[:, h, a:a + n], ones[:, 0:n], Bf[:, h, a:a + n], 0.0, ALU.mult, ALU.add)
            link(m)
            dve.wait_ge(sem("ln_mean"), 1)
            for k in range(8):
                m = dve.tensor_tensor(cv[:, k, :], cv[:, k, :], PS[:, 6, :], ALU.subtract)
                m.then_inc(sem("ln_centred"), 1)
            dve.nop().then_inc(sem("ln_read"), 1)
            dve.wait_ge(sem("ln_var"), 1)
            dve.tensor_scalar(rs[:, 0:NT], PS[:, 7, 0:NT], EPS, None, ALU.add).then_inc(sem("ln_read"), 1)

            def diagonals(wait, n, done):
                dve.wait_ge(sem(wait), n)
                i4 = ident.rearrange("p (o t) -> p o t", o=1).broadcast_to([P, 4, P])
                r4 = rs[:, 0:4].rearrange("p (h o) -> p h o", o=1).to_broadcast([P, 4, P])
                dve.tensor_tensor(diag4, i4, r4, ALU.mult).then_inc(sem(done), 1)
            diagonals("ln_rstd", 1, "ln_diag")
            dve.wait_ge(sem("ln_spread"), 1)
            for k in range(8):
                dve.tensor_tensor(cv[:, k, :], cv[:, k, :], PS[:, 7, :], ALU.mult).then_inc(sem("ln_scaled"), 1)
            for k in range(8):
                dve.wait_ge(sem("ln_tanh"), k + 1)
                link(dve.tensor_scalar(cv[:, k, :], cv[:, k, :], par(R_LG, k), par(R_LB, k), ALU.mult, ALU.add))
                dve.scalar_tensor_tensor(out=cv[:, k, :], in0=th[k % 2], scalar=1.0, in1=cv[:, k, :],
                                         op0=ALU.add, op1=ALU.mult).then_inc(sem("u_final"), 1)

            n_e, n_s, n_a = [0], [0], [0]

            def differences(t):
                c = t[1]
                ei = n_e[0]
                n_e[0] += 1
                if ei >= 6:
                    dve.wait_ge(sem("score_done"), s_tasks.index(e_tasks[ei - 6]) + 1)
                ev = E[ei % 6]
                if t[0] in ("kdm", "kd"):
                    a, n = (T, META) if t[0] == "kdm" else (P * c, P)
                    m = dve.tensor_tensor(ev[:, :, 0:n], Bf[:, :, a + n - 1:a + n].to_broadcast([P, H, n]), Bf[:, :, a:a + n], ALU.subtract)
                else:
                    w = LEVELS[t[2]]
                    e4 = ev.rearrange("p h (g a w) -> p h g a w", a=2, w=w)
                    b4 = Bf[:, :, P * c:P * c + P].rearrange("p h (g a w) -> p h g a w", a=2, w=w)
                    ref = b4[:, :, :, 0, w - 1:w].to_broadcast([P, H, 64 // w, w])
                    dve.tensor_tensor(e4[:, :, :, 0, :], ref, b4[:, :, :, 0, :], ALU.subtract)
                    m = dve.tensor_tensor(e4[:, :, :, 1, :], b4[:, :, :, 1, :], ref, ALU.subtract)
                m.then_inc(sem("e_sub"), 1)

            def take(t):
                kind, c = t[0], t[1]
                if kind in ("kdm", "lv", "diag", "kd", "ss", "bc"):
                    s = n_s[0]
                    n_s[0] += 1
                    bank = PS[:, 4 + s % 2, :].rearrange("p (h t) -> p h t", h=H)
                    dve.wait_ge(sem("score_done"), s + 1)
                    if kind in ("lv", "diag"):
                        lv = t[2] if kind == "lv" else 7
                        mk = masks[:, lv, :].rearrange("p (o t) -> p o t", o=1).broadcast_to([P, H, P])
                        if lv == 0 and c >= 2:
                            dve.wait_ge(sem("acc_done"), a_tasks.index(("o", c - 2)) + 1)
                        dve.copy_predicated(scT[c % 2], mk, bank).then_inc(sem("score_taken"), 1)
                        dve.wait_ge(sem("score_taken"), s + 1)
                    elif kind == "ss":
                        dve.tensor_scalar(rs[:, 0:H], PS[:, 4 + s % 2, 0:H], 1.0 / DV, EPS, ALU.mult, ALU.add).then_inc(sem("score_taken"), 1)
                        diagonals("o_rstd", c + 1, "o_diag")
                    elif kind == "bc":
                        o4 = o_t.rearrange("p (h b) t -> p h b t", h=H)
                        r4 = PS[:, 4 + s % 2, :].rearrange("p (h o t) -> p h o t", h=H, o=1).broadcast_to([P, H, 2, P])
                        dve.tensor_tensor(o4, o4, r4, ALU.mult).then_inc(sem("score_taken"), 1)
                        dve.wait_ge(sem("score_taken"), s + 1)
                        g = prm[:, PB + R_GLA:PB + R_GLA + 8].rearrange("p (k o) -> p k o", o=1).to_broadcast([P, 8, P])
                        link(dve.tensor_tensor(o_t, o_t, g, ALU.mult))
                        gt = GT[:, :, P * c:P * c + P]
                        dve.wait_ge(sem("ga_ready"), 8)
                        m = dve.tensor_tensor(gt, gt, o_t, ALU.mult)
                        link(m)
                        if c == NT - 1:
                            dve.nop().then_inc(sem("attention_done"), 1)
                    else:
                        rows = META if kind == "kdm" else P
                        if kind == "kd" and c >= 0:
                            dve.wait_ge(sem("acc_done"), a_tasks.index(("S", c - 1) if c else ("Sm", 0)) + 1)
                        dve.tensor_copy(kd[0:rows], bank[0:rows]).then_inc(sem("score_taken"), 1)
                    return
                a = n_a[0]
                n_a[0] += 1
                dve.wait_ge(sem("acc_done"), a + 1)
                pair = PS[:, 6:8, :]
                if kind == "o":
                    m = dve.tensor_copy(o_t.rearrange("p (a b) t -> p a (b t)", a=2), pair)
                elif kind == "Sm":
                    m = dve.tensor_copy(S.rearrange("p (a h) v -> p a (h v)", a=2), pair)
                else:
                    for h in range(H):
                        m = dve.scalar_tensor_tensor(out=S[:, h, :], in0=S[:, h, :], scalar=elast[c][:, h, :],
                                                     in1=PS[:, 6 + h // 2, DV * (h % 2):DV * (h % 2) + DV], op0=ALU.mult, op1=ALU.add)
                m.then_inc(sem("acc_taken"), 1)
                dve.wait_ge(sem("acc_taken"), a + 1)

            for b in range(NSLOT + 1):
                if b < NSLOT:
                    for t in slots[b]:
                        if t[0] in ("kdm", "lv", "kd"):
                            differences(t)
                if b >= 1:
                    for t in slots[b - 1]:
                        take(t)
                    if b - 1 in OG_BLOCKS:
                        k = b - 1 - 8
                        bank = PS[:, (14 + b - 1) % 4, :]
                        dve.wait_ge(sem("og_tanh"), k + 1)
                        dve.wait_ge(sem("ga_ready"), 8)
                        link(dve.scalar_tensor_tensor(out=th[k % 2], in0=th[k % 2], scalar=1.0, in1=bank, op0=ALU.add, op1=ALU.mult))
                        link(dve.tensor_tensor(GT[:, k, :], GT[:, k, :], th[k % 2], ALU.mult))
                        dve.nop().then_inc(sem("sgl_dve"), 1)
            u = 38
            for k in range(8):
                dve.wait_ge(sem("single_done"), u + 1)
                bank = PS[:, u % 4, :]
                u += 1
                dve.wait_ge(sem("sgl_act"), 14 + 8 + k + 1)
                link(dve.scalar_tensor_tensor(out=th[k % 2], in0=U[:, k, 0:T], scalar=1.0, in1=bank, op0=ALU.add, op1=ALU.mult))
                dve.nop().then_inc(sem("sgl_dve"), 1)
                link(dve.scalar_tensor_tensor(out=GT[:, k, :], in0=th[k % 2], scalar=0.5, in1=GT[:, k, :], op0=ALU.mult, op1=ALU.add))
                dve.nop().then_inc(sem("mix_ready"), 1)
            dve.nop().then_inc(sem("pw_used"), 1)
            dve.wait_ge(sem("router_loaded"), 96)
            def rms(i, a, b):
                dve.wait_ge(sem(a), i + 1)
                dve.tensor_scalar(rs[:, i:i + 1], ss[:, i:i + 1], 1.0 / D, EPS, ALU.mult, ALU.add).then_inc(sem(b), 1)

            def add_half(i, j):
                nonlocal u
                dve.wait_ge(sem("single_done"), u + 1)
                hv = xr[:, i, 512 * j:512 * j + 512]
                dve.tensor_tensor(hv, hv, PS[:, u % 4, :], ALU.add).then_inc(sem("sgl_dve"), 1)
                u += 1

            def norm2(i):
                rms(i, "ss2_ready", "ms2_ready")
                if i >= 2:
                    dve.wait_ge(sem(f"hn2_stored{i % 2}"), 16)
                    dve.wait_ge(sem("hn2T_done"), i - 1)
                dve.wait_ge(sem("rs2_ready"), i + 1)
                dve.scalar_tensor_tensor(out=hn2[i % 2], in0=xr[:, i, :], scalar=rs[:, i:i + 1], in1=g2b,
                                         op0=ALU.mult, op1=ALU.mult).then_inc(sem("hn2_ready"), 1)

            def take_hn2T(i):
                dve.wait_ge(sem("hn2T_done"), i + 1)
                if i >= 2:
                    dve.wait_ge(sem("logits_done"), i - 1)
                dve.tensor_copy(hn2T[i % 2].rearrange("p (a k) t -> p a (k t)", a=2), PS[:, 4:6, :]).then_inc(sem("hn2T_ready"), 1)

            def take_logits(i):
                dve.wait_ge(sem("logits_done"), i + 1)
                dve.tensor_tensor(lg[:, i, :], PS[:, 6 + i % 2, 0:72], brb, ALU.add).then_inc(sem("logits_taken"), 1)
            dve.wait_ge(sem("router_loaded"), 96)
            for i in range(NT):
                add_half(i, 0)
                if i >= 2:
                    take_logits(i - 2)
                add_half(i, 1)
                dve.wait_ge(sem("sgl_dve"), 16 + 2 * i + 2)
                dve.nop().then_inc(sem("h_ready"), 1)
                if i >= 1:
                    take_hn2T(i - 1)
                norm2(i)
            take_logits(NT - 2)
            link(dve.tensor_scalar(desc8, iota[:, 0:8], -1.0, 8.0, ALU.mult, ALU.add))
            link(dve.memset(ones64, 1.0))
            link(dve.memset(Apre[:, 0:NE], 0.0))
            link(dve.memset(half2[0:CAP], -2.0))
            link(dve.memset(half2[CAP:P], -1.0))
            take_hn2T(NT - 1)
            take_logits(NT - 1)
            dve.wait_ge(sem("logits_taken"), NT)
            used(dve, len(chunks) - 1)

            def tt(o, a, b, op):
                link(dve.tensor_tensor(o, a, b, op))

            def red(o, a, op=ALU.add):
                link(dve.tensor_reduce(o, a, AX.X, op))

            def b3(v, n):
                return v.rearrange("p (i o) -> p i o", o=1).to_broadcast([P, NT, n])

            def over_i(v, n):
                return v.rearrange("p (o n) -> p o n", o=1).broadcast_to([P, NT, n])
            def first_max(one, vals, mx):
                red(mx, vals, ALU.max)
                tt(one, vals, b3(mx, 8), ALU.is_equal)
                tt(tb, one, over_i(desc8, 8), ALU.mult)
                red(m4[7], tb, ALU.max)
                tt(one, tb, b3(m4[7], 8), ALU.is_equal)
            lgg = lg[:, :, 0:8]
            first_max(oh, lgg, m4[0])
            dve.tensor_tensor(eg, lgg, b3(m4[0], 8), ALU.subtract).then_inc(sem("group_diff"), 1)
            lge = lg[:, :, 8:72].rearrange("p i (g e) -> p i g e", g=NG)
            tt(prod, lge, oh.rearrange("p i (g o) -> p i g o", o=1).to_broadcast([P, NT, NG, EPG]), ALU.mult)
            red(sel, prod.rearrange("p i g e -> p i e g"))
            first_max(o12[0], sel, m4[1])
            link(dve.scalar_tensor_tensor(out=sel2, in0=o12[0], scalar=-3e38, in1=sel, op0=ALU.mult, op1=ALU.add))
            first_max(o12[1], sel2, m4[2])
            oh4 = oh.rearrange("p i (g o) -> p i g o", o=1).to_broadcast([P, NT, NG, EPG])
            for k in range(2):
                tt(A[k].rearrange("p (i g e) -> p i g e", i=NT, g=NG), oh4,
                   o12[k].rearrange("p i (o e) -> p i o e", o=1).broadcast_to([P, NT, NG, EPG]), ALU.mult)
            tt(Asum, A[0], A[1], ALU.add)
            for i in range(NT):
                tt(Apre[:, NE * i + NE:NE * i + 2 * NE], Apre[:, NE * i:NE * i + NE], Asum[:, NE * i:NE * i + NE], ALU.add)
            dve.nop().then_inc(sem("choice_ready"), 1)
            dve.tensor_tensor(m4[3], m4[2], m4[1], ALU.subtract).then_inc(sem("choice_diff"), 1)

            def each(v, n):
                return v.rearrange("p (c o) -> p c o", o=1).to_broadcast([P, 2 * NT, n])

            def all8(v, n):
                return v.rearrange("p (o n) -> p o n", o=1).broadcast_to([P, 2 * NT, n])

            def by8(v):
                return v.rearrange("p (c n) -> p c n", c=2 * NT)
            A8 = A2.rearrange("p k (i e) -> p (k i) e", i=NT)
            tt(by8(AB), A8, each(slot, NE), ALU.mult)
            dve.wait_ge(sem("ranks_done"), 1)
            tt(big2.rearrange("p (k c) -> p k c", k=2), A2,
               PS[:, 0, 0:NT * NE].rearrange("p (o c) -> p o c", o=1).broadcast_to([P, 2, NT * NE]), ALU.mult)
            red(rank, by8(big2))
            tt(by8(OR), all8(iota[:, 0:CAP], CAP), each(rank, CAP), ALU.is_equal)
            dve.nop().then_inc(sem("onehot_ready"), 1)
            link(dve.tensor_copy(Ccnt, PS[:, 0, NT * NE:NT * NE + NE]))
            dve.wait_ge(sem("group_exp"), 1)
            red(m4[4], eg)
            dve.wait_ge(sem("choice_exp"), 1)
            link(dve.tensor_scalar(m4[5], m4[3], 1.0, None, ALU.add))
            tt(m4[4], m4[4], m4[5], ALU.mult)
            link(dve.reciprocal(wgt[0], m4[4]))
            tt(wgt[1], wgt[0], m4[3], ALU.mult)

            def indices(bank, n):
                s0, inv, tok = (slots_of[:, 80 * m:80 * m + n] for m in range(3))
                link(dve.tensor_copy(s0, PS[:, bank, 0:n]))
                link(dve.tensor_scalar(inv, s0, 0.0, beyond, ALU.is_equal, ALU.mult))
                link(dve.tensor_scalar(tok, s0, float(T), -float(T), ALU.is_gt, ALU.mult))
                link(dve.scalar_tensor_tensor(out=tok, in0=tok, scalar=-1.0, in1=s0, op0=ALU.add, op1=ALU.add))
                tt(tok, tok, inv, ALU.add)
                return s0, inv, tok

            def destinations(s0, inv, dst):
                link(dve.tensor_scalar(s0, s0, 2.0, half2, ALU.mult, ALU.add))
                link(dve.tensor_tensor(dst, s0, inv, ALU.add))
            dve.wait_ge(sem("idx_done"), 1)
            s0, inv, tok = indices(1, NE)
            for g in range(2):
                m = dve.tensor_copy(idx_pair[CAP * g:CAP * g + CAP, :], tok[CAP * g:CAP * g + CAP, g::2])
                link(m)
            dve.nop().then_inc(sem("tables_ready"), 1)
            destinations(s0, inv, to_rows[:, :])
            dve.nop().then_inc(sem("to_rows_ready"), 1)

            def overflow_places():
                link(dve.memset(nx, 0.0))
                for m in range(1, T // CAP):
                    link(dve.scalar_tensor_tensor(out=nx, in0=Ccnt, scalar=float(CAP * m), in1=nx, op0=ALU.is_gt, op1=ALU.add))
                link(dve.tensor_tensor_scan(end, ones64, nx, 0.0, ALU.mult, ALU.add))
                tt(start, end, nx, ALU.subtract)
                for k in range(2):
                    tt(prod.rearrange("p i g e -> p i (g e)"), A[k].rearrange("p (i e) -> p i e", i=NT), over_i(start, NE), ALU.mult)
                    red(first_over[:, NT * k:NT * k + NT], prod.rearrange("p i g e -> p i (g e)"))

            def overflow_rounds():
                link(dve.memset(rnd, 0.0))
                for m in range(1, T // CAP):
                    link(dve.scalar_tensor_tensor(out=rnd, in0=rank, scalar=float(CAP * m), in1=rnd, op0=ALU.is_ge, op1=ALU.add))
                link(dve.scalar_tensor_tensor(out=row, in0=rnd, scalar=-float(CAP), in1=rank, op0=ALU.mult, op1=ALU.add))
                link(dve.tensor_scalar(isj, rnd, 1.0, None, ALU.is_ge))
                tt(blk, first_over, rnd, ALU.add)
                link(dve.scalar_tensor_tensor(out=blk, in0=blk, scalar=float(NE - 1), in1=isj, op0=ALU.add, op1=ALU.mult))

            def overflow_onehots():
                e3 = end.rearrange("p (o e) -> p o e", o=1).broadcast_to([P, 16, NE])
                i3 = iota[:, 0:16].rearrange("p (b o) -> p b o", o=1).to_broadcast([P, 16, NE])
                tt(ends, e3, i3, ALU.is_le)
                red(be_f, ends)
                link(dve.tensor_scalar(be_f, be_f, float(NE - 1), None, ALU.min))
                link(dve.tensor_copy(over_e[:, 0:16], be_f))
                link(dve.tensor_copy(over_e[:, 16:17], end[:, NE - 1:NE]))
                tt(by8(OR_over), all8(iota[:, 0:CAP], CAP), each(row, CAP), ALU.is_equal)
                tt(by8(AB_over), all8(iota[:, NE:NBLK], 16), each(blk, 16), ALU.is_equal)
                tt(by8(AB_over), by8(AB_over), each(slot, 16), ALU.mult)
                dve.nop().then_inc(sem("onehot_over_ready"), 1)

            def overflow_indices():
                dve.wait_ge(sem("idx_over_done"), 1)
                s0, inv, tok = indices(3, 16)
                link(dve.tensor_copy(idx_over[:, :], tok[0:CAP, :]))
                destinations(s0, inv, to_rows_over[:, :])
                dve.nop().then_inc(sem("over_ready"), 1)

            def half_swiglu(i, e, s, freed):
                dve.wait_ge(sem("g_tanh" + s), i + 1)
                if freed:
                    dve.wait_ge(sem("h_turned" + s), i)
                ps = PS[:, 2 + e, :]
                dve.scalar_tensor_tensor(out=gth[e], in0=gth[e], scalar=1.0, in1=ps[:, 0:256], op0=ALU.add,
                                         op1=ALU.mult).then_inc(sem("silu" + s), 1)
                dve.wait_ge(sem("silu" + s), i + 1)
                dve.scalar_tensor_tensor(out=hS[e], in0=gth[e], scalar=0.5, in1=ps[:, 256:512], op0=ALU.mult,
                                         op1=ALU.mult).then_inc(sem("h_ready" + s), 1)
                dve.wait_ge(sem("h_turned" + s), i + 1)
                if freed:
                    dve.wait_ge(sem(freed[0]), freed[1])
                dve.tensor_copy(hT[e].rearrange("p b g s -> p (b g s)"), PS[:, 4 + e, 0:256]).then_inc(sem("hT_ready" + s), 1)

            def take_rows(i0, j):
                i = i0 + ROUND * j
                dve.wait_ge(sem("rows_turned"), i + 1)
                if i0:
                    b, nth = turn(2 * i0 - 1, j)
                    dve.wait_ge(sem(f"gu_used{b}"), nth)
                dve.tensor_copy(xT.rearrange("p (a k) t -> p a (k t)", a=2), PS[:, 0:2, :]).then_inc(sem("xT_ready"), 1)

            def swiglus(i0, j):
                for e in range(2):
                    freed = None
                    if i0:
                        b, nth = turn(2 * i0 + e - 2, j)
                        freed = (f"dn_used{b}", nth)
                    half_swiglu(i0 + ROUND * j, e, str(e), freed)

            def pair(i0, j):
                take_rows(i0, j)
                swiglus(i0, j)
            overflow_places()
            take_rows(0, 0)
            overflow_rounds()
            overflow_onehots()
            swiglus(0, 0)
            overflow_indices()
            pair(1, 0)
            with dve.Fori(0, NLOOP) as j:
                for r in range(ROUND):
                    pair(2 + r, j)
            flag = dve.value_load(over_e[0:1, 16:17], min_val=0, max_val=NX)
            with dve.If(flag > 0):
                dve.wait_ge(sem("gu_used0"), LAST0)
                with dve.Fori(0, NX) as i:
                    dve.wait_ge(sem("rows_turned_over"), i + 1)
                    dve.tensor_copy(xT[:, :, 0:CAP].rearrange("p (a k) t -> p a k t", a=2),
                                    PS[:, 0:2, :].rearrange("p a (k t) -> p a k t", k=4)[:, :, :, 0:CAP]).then_inc(sem("xT_ready_over"), 1)
                    half_swiglu(i, 0, "_over", None)
            with dve.Else():
                dve.nop()
            def final_norm(i):
                rms(i, "ss3_ready", "ms3_ready")
                dve.wait_ge(sem("rs3_ready"), i + 1)
                dve.scalar_tensor_tensor(out=fin[i], in0=xr[:, i, :], scalar=rs[:, i:i + 1], in1=fgb,
                                         op0=ALU.mult, op1=ALU.mult).then_inc(sem("fin_ready"), 1)
            dve.wait_ge(sem("fg_loaded"), 16)
            for i in range(NT):
                dve.wait_ge(sem(f"y_back{i}"), 32)
                for k in range(2):
                    link(dve.scalar_tensor_tensor(out=xr[:, i, :], in0=yt[2 * i + k], scalar=wgt[k][:, i:i + 1], in1=xr[:, i, :],
                                                  op0=ALU.mult, op1=ALU.add))
                dve.nop().then_inc(sem("h_final"), 1)
                if i >= 1:
                    final_norm(i - 1)
            final_norm(NT - 1)


def kernel(**inputs):
    import concourse.bacc as bacc
    from concourse.bass_utils import run_bass_kernel_spmd

    a = {k: np.ascontiguousarray(v) for k, v in inputs.items()}
    row = lambda v: v.reshape(-1)
    rows = lambda v: v.reshape(-1, P)
    data = {
        "x": a["x"].reshape(T, D), "meta": a["meta"], "norm1_g": rows(a["norm1_g"]), "w_in": a["w_in"][0],
        "w_decay_up": a["w_decay_up"][0], "b_decay": rows(a["b_decay"]), "gla_norm_g": rows(a["gla_norm_g"]),
        "conv_w": a["conv_w"][0], "conv_b": rows(a["conv_b"]), "conv_ln_g": rows(a["conv_ln_g"]),
        "conv_ln_b": rows(a["conv_ln_b"]), "w_pw2": a["w_pw2"][0], "b_gate": rows(a["b_gate"]),
        "w_out": a["w_out"][0], "norm2_g": row(a["norm2_g"]), "w_rg": a["w_router_group"][0],
        "b_rg": row(a["b_router_group"]), "w_re": a["w_router_expert"][0], "b_re": row(a["b_router_expert"]),
        "w_eg": a["w_exp_gate"][0], "w_eu": a["w_exp_up"][0], "w_ed": a["w_exp_down"][0],
        "final_g": row(a["final_norm_g"]),
    }
    nc = bacc.Bacc("TRN2", target_bir_lowering=False, num_devices=1)
    aps = {n: nc.dram_tensor(n, v.shape, mybir.dt.from_np(v.dtype), kind="ExternalInput").ap() for n, v in data.items()}
    o = nc.dram_tensor("out", (T, D), FP, kind="ExternalOutput").ap()
    program(nc, out=o, **aps)
    r = run_bass_kernel_spmd(nc, [data], core_ids=[0])
    return r.results[0]["out"].reshape(1, T, D)
```
